# Optimizing a Trainium2 kernel written in Bass

```python
import math
import jax, jax.numpy as jnp
from jax import lax
import numpy as np

D_MODEL = 1024
BATCH = 1
SEQ = 256
DEPTH = 1

GRID_W = 64
CTX_LEN = 256
MIX_W = D_MODEL
F_GROUPS = 4
F_DIM = D_MODEL // 8
FOURIER_W = F_GROUPS * F_DIM
GDN_HEADS = 4
GDN_DK = D_MODEL // 8
GDN_DV = D_MODEL // 8
QK_W = GDN_HEADS * GDN_DK
V_W = GDN_HEADS * GDN_DV
IN_W = FOURIER_W + 2 * QK_W + 2 * V_W + 4 * GDN_HEADS
SHORT_CONV = 3
CHUNK = 64
D_FF = ((8 * D_MODEL // 3 + 127) // 128) * 128
EPS = 1e-6


def rmsnorm(t, g):
    tf = t.astype(jnp.float32)
    y = tf * lax.rsqrt(jnp.mean(tf * tf, axis=-1, keepdims=True) + EPS)
    return y.astype(t.dtype) * g

def l2norm(t):
    tf = t.astype(jnp.float32)
    return (tf * lax.rsqrt(jnp.sum(tf * tf, axis=-1, keepdims=True) + EPS)).astype(t.dtype)

def modulate(h, shift, scale):
    return h * (1 + scale) + shift

def dwconv1d(t, w):
    k_w = w.shape[0]
    pad = k_w // 2
    length = t.shape[1]
    tp = jnp.pad(t, ((0, 0), (pad, pad), (0, 0)))
    out = tp[:, 0:length] * w[0]
    for j in range(1, k_w):
        out = out + tp[:, j:j + length] * w[j]
    return out

def gated_delta_chunked(q, k, v, beta, g, s0):
    f32 = jnp.float32
    bsz, length, heads, dk = q.shape
    dv = v.shape[-1]
    n_chunks = length // CHUNK

    def chunks(t):
        t = t.astype(f32).reshape(bsz, n_chunks, CHUNK, heads, t.shape[-1])
        return jnp.transpose(t, (1, 0, 3, 2, 4))

    def chunks_s(t):
        t = t.astype(f32).reshape(bsz, n_chunks, CHUNK, heads)
        return jnp.transpose(t, (1, 0, 3, 2))

    qc = chunks(q) * (dk ** -0.5)
    kc = chunks(k)
    vc = chunks(v)
    bc = chunks_s(beta)
    gc = jnp.cumsum(chunks_s(g), axis=-1)
    lower = jnp.tril(jnp.ones((CHUNK, CHUNK), dtype=bool))
    strict = jnp.tril(jnp.ones((CHUNK, CHUNK), dtype=bool), -1)
    diff = gc[..., :, None] - gc[..., None, :]
    decay = jnp.where(lower, jnp.exp(jnp.where(lower, diff, 0.0)), 0.0)

    kb = kc * bc[..., None]
    vb = vc * bc[..., None]
    a_mat = jnp.where(strict, jnp.einsum('nbhid,nbhjd->nbhij', kb, kc) * decay, 0.0)
    eye = jnp.eye(CHUNK, dtype=f32)
    t_inv = lax.linalg.triangular_solve(eye + a_mat, jnp.broadcast_to(eye, a_mat.shape),
                                        left_side=True, lower=True, unit_diagonal=True)
    u_val = jnp.einsum('nbhij,nbhjd->nbhid', t_inv, vb)
    w_key = jnp.einsum('nbhij,nbhjd->nbhid', t_inv, kb * jnp.exp(gc)[..., None])
    attn_intra = jnp.where(lower, jnp.einsum('nbhid,nbhjd->nbhij', qc, kc) * decay, 0.0)
    g_last = gc[..., -1]
    k_dec = kc * jnp.exp(g_last[..., None] - gc)[..., None]
    q_dec = qc * jnp.exp(gc)[..., None]

    def step(s, xs):
        u_i, w_i, a_i, qd_i, kd_i, gl_i = xs
        v_new = u_i - jnp.einsum('bhcd,bhde->bhce', w_i, s)
        o_i = jnp.einsum('bhcd,bhde->bhce', qd_i, s) + jnp.einsum('bhij,bhje->bhie', a_i, v_new)
        s = s * jnp.exp(gl_i)[..., None, None] + jnp.einsum('bhcd,bhce->bhde', kd_i, v_new)
        return s, o_i

    s_final, o = lax.scan(step, s0.astype(f32), (u_val, w_key, attn_intra, q_dec, k_dec, g_last))
    o = jnp.transpose(o, (1, 0, 3, 2, 4)).reshape(bsz, length, heads, dv)
    return o.astype(v.dtype), s_final

def bidir_gdn(q, k, v, beta, g, s0_f, s0_b):
    flip = lambda t: jnp.flip(t, axis=1)
    o_f, s_f = gated_delta_chunked(q, k, v, beta[:, :, 0], g[:, :, 0], s0_f)
    o_b, s_b = gated_delta_chunked(flip(q), flip(k), flip(v), flip(beta[:, :, 1]), flip(g[:, :, 1]), s0_b)
    return o_f + flip(o_b), s_f, s_b

def mixer_inputs(h, w_in_l, conv_l, a_log_l, dt_bias_l):
    bsz, length, _ = h.shape
    p = h @ w_in_l
    o1 = FOURIER_W
    o2 = o1 + 2 * QK_W + V_W
    o3 = o2 + V_W
    u = p[..., :o1]
    qkv = jax.nn.silu(dwconv1d(p[..., o1:o2], conv_l))
    z = p[..., o2:o3]
    ab = p[..., o3:].astype(jnp.float32).reshape(bsz, length, 4, GDN_HEADS)
    q = l2norm(qkv[..., :QK_W].reshape(bsz, length, GDN_HEADS, GDN_DK))
    k = l2norm(qkv[..., QK_W:2 * QK_W].reshape(bsz, length, GDN_HEADS, GDN_DK))
    v = qkv[..., 2 * QK_W:].reshape(bsz, length, GDN_HEADS, GDN_DV)
    beta = jax.nn.sigmoid(ab[:, :, 0:2])
    g = -jnp.exp(a_log_l.astype(jnp.float32)) * jax.nn.softplus(ab[:, :, 2:4] + dt_bias_l.astype(jnp.float32))
    return u, z, q, k, v, beta, g

def fourier_mix(u, w_f):
    bsz, length, _ = u.shape
    ug = u.astype(jnp.float32).reshape(bsz, length, F_GROUPS, F_DIM)
    y = jnp.fft.fft2(ug, axes=(1, 3), norm='ortho').real.astype(u.dtype)
    return jnp.einsum('blgc,gcd->blgd', y, w_f).reshape(bsz, length, FOURIER_W)

def mixer_out(u, o, z, w_f, g_gdn_l, w_out_l):
    bsz, length, _ = z.shape
    y_f = fourier_mix(u, w_f)
    y_d = rmsnorm(o, g_gdn_l) * jax.nn.silu(z).reshape(bsz, length, GDN_HEADS, GDN_DV)
    return jnp.concatenate([y_f, y_d.reshape(bsz, length, V_W)], axis=-1) @ w_out_l

def conv_ffn(h, w_up_l, w_dwc_l, w_down_l, on_grid):
    bsz, length, _ = h.shape
    p = h @ w_up_l
    val, gate = p[..., :D_FF], p[..., D_FF:]
    if on_grid:
        rows = length // GRID_W
        gate = lax.conv_general_dilated(
            gate.reshape(bsz, rows, GRID_W, D_FF), w_dwc_l[:, :, None, :],
            window_strides=(1, 1), padding='SAME',
            dimension_numbers=('NHWC', 'HWIO', 'NHWC'),
            feature_group_count=D_FF).reshape(bsz, length, D_FF)
    else:
        gate = dwconv1d(gate, w_dwc_l[1])
    return (jax.nn.silu(gate) * val) @ w_down_l

def first_inputs(seed: int = 0) -> dict:
    key = jax.random.key(seed)
    ks = jax.random.split(key, 20)
    f32 = jnp.float32

    def nrm(k, shape, s):
        return jax.random.normal(k, shape, f32) * s

    L = DEPTH
    x = nrm(ks[0], (BATCH, SEQ, D_MODEL), 1.0)
    c = nrm(ks[1], (BATCH, D_MODEL), 1.0)
    ctx = nrm(ks[2], (BATCH, CTX_LEN, D_MODEL), 1.0)
    c_ctx = nrm(ks[3], (D_MODEL,), 1.0)
    w_ada = nrm(ks[4], (L, D_MODEL, 6 * D_MODEL), 0.5 * D_MODEL ** -0.5)
    b_ada = nrm(ks[5], (L, 6 * D_MODEL), 0.02)
    g_pre_mix = 1.0 + nrm(ks[6], (L, D_MODEL), 0.1)
    g_post_mix = 1.0 + nrm(ks[7], (L, D_MODEL), 0.1)
    g_pre_ffn = 1.0 + nrm(ks[8], (L, D_MODEL), 0.1)
    g_post_ffn = 1.0 + nrm(ks[9], (L, D_MODEL), 0.1)
    w_in = nrm(ks[10], (L, D_MODEL, IN_W), D_MODEL ** -0.5)
    w_qkv_conv = nrm(ks[11], (L, SHORT_CONV, 2 * QK_W + V_W), SHORT_CONV ** -0.5)
    a_log = jnp.log(jax.random.uniform(ks[12], (L, 2, GDN_HEADS), f32, minval=1.0, maxval=16.0))
    dt = jnp.exp(jax.random.uniform(ks[13], (L, 2, GDN_HEADS), f32,
                                    minval=math.log(1e-3), maxval=math.log(1e-1)))
    dt_bias = dt + jnp.log(-jnp.expm1(-dt))
    g_gdn = 1.0 + nrm(ks[14], (L, GDN_DV), 0.1)
    w_fourier = nrm(ks[15], (L, F_GROUPS, F_DIM, F_DIM), F_DIM ** -0.5)
    w_out = nrm(ks[16], (L, MIX_W, D_MODEL), MIX_W ** -0.5)
    w_up = nrm(ks[17], (L, D_MODEL, 2 * D_FF), D_MODEL ** -0.5)
    w_dwc = nrm(ks[18], (L, 3, 3, D_FF), 1.0 / 3.0)
    w_down = nrm(ks[19], (L, D_FF, D_MODEL), D_FF ** -0.5)
    return {"x": x, "c": c, "ctx": ctx, "c_ctx": c_ctx, "w_ada": w_ada, "b_ada": b_ada,
            "g_pre_mix": g_pre_mix, "g_post_mix": g_post_mix, "g_pre_ffn": g_pre_ffn,
            "g_post_ffn": g_post_ffn, "w_in": w_in, "w_qkv_conv": w_qkv_conv, "a_log": a_log,
            "dt_bias": dt_bias, "g_gdn": g_gdn, "w_fourier": w_fourier, "w_out": w_out,
            "w_up": w_up, "w_dwc": w_dwc, "w_down": w_down}

def first_block(x, c, ctx, c_ctx, w_ada, b_ada, g_pre_mix, g_post_mix, g_pre_ffn, g_post_ffn,
              w_in, w_qkv_conv, a_log, dt_bias, g_gdn, w_fourier, w_out, w_up, w_dwc, w_down):
    xl, xc = x, ctx
    bsz = x.shape[0]
    silu_c = jax.nn.silu(c)
    silu_cc = jax.nn.silu(c_ctx)
    for i in range(DEPTH):
        update_ctx = i < DEPTH - 1
        mod_l = (silu_c @ w_ada[i] + b_ada[i])[:, None, :]
        mod_c = silu_cc @ w_ada[i] + b_ada[i]
        sh1l, sc1l, gt1l, sh2l, sc2l, gt2l = jnp.split(mod_l, 6, axis=-1)
        sh1c, sc1c, gt1c, sh2c, sc2c, gt2c = jnp.split(mod_c, 6, axis=-1)

        hl = modulate(rmsnorm(xl, g_pre_mix[i]), sh1l, sc1l)
        hc = modulate(rmsnorm(xc, g_pre_mix[i]), sh1c, sc1c)
        ul, zl, ql, kl, vl, bl, gl = mixer_inputs(hl, w_in[i], w_qkv_conv[i], a_log[i], dt_bias[i])
        uc, zc, qc, kc, vc, bc, gc = mixer_inputs(hc, w_in[i], w_qkv_conv[i], a_log[i], dt_bias[i])
        s_zero = jnp.zeros((bsz, GDN_HEADS, GDN_DK, GDN_DV), jnp.float32)
        oc, s_f, s_b = bidir_gdn(qc, kc, vc, bc, gc, s_zero, s_zero)
        ol, _, _ = bidir_gdn(ql, kl, vl, bl, gl, s_f, s_b)
        yl = mixer_out(ul, ol, zl, w_fourier[i], g_gdn[i], w_out[i])
        xl = xl + gt1l * rmsnorm(yl, g_post_mix[i])
        if update_ctx:
            yc = mixer_out(uc, oc, zc, w_fourier[i], g_gdn[i], w_out[i])
            xc = xc + gt1c * rmsnorm(yc, g_post_mix[i])

        hl = modulate(rmsnorm(xl, g_pre_ffn[i]), sh2l, sc2l)
        xl = xl + gt2l * rmsnorm(conv_ffn(hl, w_up[i], w_dwc[i], w_down[i], True), g_post_ffn[i])
        if update_ctx:
            hc = modulate(rmsnorm(xc, g_pre_ffn[i]), sh2c, sc2c)
            xc = xc + gt2c * rmsnorm(conv_ffn(hc, w_up[i], w_dwc[i], w_down[i], False), g_post_ffn[i])
    return xl


DEPTH_2 = 2

N_MIXERS = 2
N_LAYERS_A = (DEPTH_2 + 1) // 2
N_LAYERS_B = DEPTH_2 // 2
PLE_DIM = 256
CONV_A_WIDTH = 3
D_RNN = D_MODEL
LRU_BLOCK = 256
N_LRU_BLOCKS = D_RNN // LRU_BLOCK
CONV_B_WIDTH = 4
RG_C = 8.0
N_GROUPS = 4
EXPERTS_PER_GROUP = 8
N_EXPERTS = N_GROUPS * EXPERTS_PER_GROUP
TOP_K = 2
D_EXPERT = 512
ROUTE_BLOCK = 128


def rmsnorm_2(x, g):
    x32 = x.astype(jnp.float32)
    y = x32 * lax.rsqrt(jnp.mean(x32 * x32, axis=-1, keepdims=True) + EPS)
    return (y * g.astype(jnp.float32)).astype(x.dtype)

def depthwise_conv(x, w, pad):
    return lax.conv_general_dilated(
        x, w[:, None, :], window_strides=(1,), padding=[pad],
        dimension_numbers=('NWC', 'WIO', 'NWC'), feature_group_count=x.shape[-1])

def short_conv_mixer(xn, w_in, conv_w, w_out):
    bgate, cgate, h = jnp.split(xn @ w_in, 3, axis=-1)
    u = depthwise_conv(cgate * h, conv_w, (1, 1))
    return (bgate * u) @ w_out

def _linear_combine(earlier, later):
    a_e, b_e = earlier
    a_l, b_l = later
    return a_l * a_e, a_l * b_e + b_l

def rglru_direction(uh, w_r, b_r, w_i, b_i, lam, reverse):
    bsz, s, nh, dh = uh.shape
    u = uh.reshape(bsz, s, nh * dh)
    r = jax.nn.sigmoid((jnp.einsum('bshd,hde->bshe', uh, w_r).reshape(bsz, s, -1) + b_r).astype(jnp.float32))
    i = jax.nn.sigmoid((jnp.einsum('bshd,hde->bshe', uh, w_i).reshape(bsz, s, -1) + b_i).astype(jnp.float32))
    log_a = -RG_C * r * jax.nn.softplus(-lam.astype(jnp.float32))
    a = jnp.exp(log_a)
    gated = jnp.sqrt(-jnp.expm1(2.0 * log_a)) * (i * u.astype(jnp.float32))
    _, h = lax.associative_scan(_linear_combine, (a, gated), axis=1, reverse=reverse)
    return h.astype(uh.dtype)

def rglru_mixer(xn, w_in, conv_w, conv_bias, w_rg, b_rg, w_ig, b_ig, lam, w_out):
    y_branch, u = jnp.split(xn @ w_in, 2, axis=-1)
    y_branch = jax.nn.gelu(y_branch)
    u = depthwise_conv(u, conv_w, (2, 1)) + conv_bias
    bsz, s, _ = u.shape
    uh = u.reshape(bsz, s, N_LRU_BLOCKS, LRU_BLOCK)
    h = (rglru_direction(uh, w_rg[0], b_rg[0], w_ig[0], b_ig[0], lam[0], False)
         + rglru_direction(uh, w_rg[1], b_rg[1], w_ig[1], b_ig[1], lam[1], True))
    return (y_branch * h) @ w_out

def hier_moe(x, w_rg, b_rg, w_re, b_re, w_gate, w_up, w_down):
    bsz, s, d = x.shape
    n = bsz * s
    xf = x.reshape(n, d)
    pg = jax.nn.softmax((xf @ w_rg).astype(jnp.float32) + b_rg.astype(jnp.float32), axis=-1)
    pg_top, g_top = lax.top_k(pg, 1)
    le = ((xf @ w_re).astype(jnp.float32) + b_re.astype(jnp.float32)).reshape(n, N_GROUPS, EXPERTS_PER_GROUP)
    le_sel = jnp.take_along_axis(le, g_top[:, :, None], axis=1)[:, 0]
    pe = jax.nn.softmax(le_sel, axis=-1)
    top_p, top_i = lax.top_k(pe, TOP_K)
    top_p = top_p / jnp.sum(top_p, axis=-1, keepdims=True)
    expert = g_top * EXPERTS_PER_GROUP + top_i
    weight = pg_top * top_p

    n_slots = n * TOP_K
    e_flat = expert.reshape(-1)
    tok_flat = jnp.arange(n_slots, dtype=jnp.int32) // TOP_K
    w_flat = weight.reshape(-1)
    order = jnp.argsort(e_flat)
    e_sorted = e_flat[order]
    counts = jnp.bincount(e_flat, length=N_EXPERTS)
    start = jnp.cumsum(counts) - counts
    padded = ((counts + ROUTE_BLOCK - 1) // ROUTE_BLOCK) * ROUTE_BLOCK
    pend = jnp.cumsum(padded)
    pstart = pend - padded
    dest = pstart[e_sorted] + (jnp.arange(n_slots) - start[e_sorted])
    n_blocks = -(-n_slots // ROUTE_BLOCK) + N_EXPERTS
    slot_of_pos = jnp.full((n_blocks * ROUTE_BLOCK,), n_slots, jnp.int32).at[dest].set(order.astype(jnp.int32))
    tok_pad = jnp.concatenate([tok_flat, jnp.array([n], jnp.int32)])[slot_of_pos]
    w_pad = jnp.concatenate([w_flat, jnp.zeros((1,), jnp.float32)])[slot_of_pos]
    block_expert = jnp.clip(jnp.searchsorted(pend, jnp.arange(n_blocks) * ROUTE_BLOCK, side='right'), 0, N_EXPERTS - 1)
    x_pad = jnp.concatenate([xf, jnp.zeros((1, d), xf.dtype)], axis=0)

    def expert_block(args):
        idx, e = args
        xb = x_pad[idx]
        hb = jax.nn.silu(xb @ w_gate[e]) * (xb @ w_up[e])
        return hb @ w_down[e]

    y_blocks = lax.map(expert_block, (tok_pad.reshape(n_blocks, ROUTE_BLOCK), block_expert))
    contrib = y_blocks.reshape(-1, d) * w_pad[:, None].astype(x.dtype)
    y = jnp.zeros((n + 1, d), x.dtype).at[tok_pad].add(contrib)
    return y[:n].reshape(bsz, s, d)

def _normal(key, shape, fan_in):
    return jax.random.normal(key, shape, jnp.float32) * (fan_in ** -0.5)

def second_inputs(seed: int = 0) -> dict:
    key = jax.random.key(seed)
    ks = jax.random.split(key, 28)
    f32 = jnp.float32
    D, R, H, Bk = D_MODEL, D_RNN, N_LRU_BLOCKS, LRU_BLOCK
    x = jax.random.normal(ks[0], (BATCH, SEQ, D), f32)
    p = jax.random.normal(ks[1], (DEPTH_2, BATCH, SEQ, PLE_DIM), f32)
    norm_mix = 1.0 + 0.05 * jax.random.normal(ks[2], (DEPTH_2, D), f32)
    w_in_a = _normal(ks[3], (N_LAYERS_A, D, 3 * D), D)
    conv_a = _normal(ks[4], (N_LAYERS_A, CONV_A_WIDTH, D), CONV_A_WIDTH)
    w_out_a = _normal(ks[5], (N_LAYERS_A, D, D), D)
    w_in_b = _normal(ks[6], (N_LAYERS_B, D, 2 * R), D)
    conv_b = _normal(ks[7], (N_LAYERS_B, CONV_B_WIDTH, R), CONV_B_WIDTH)
    conv_bias_b = 0.01 * jax.random.normal(ks[8], (N_LAYERS_B, R), f32)
    w_rgate_b = _normal(ks[9], (N_LAYERS_B, 2, H, Bk, Bk), Bk)
    b_rgate_b = 0.01 * jax.random.normal(ks[10], (N_LAYERS_B, 2, R), f32)
    w_igate_b = _normal(ks[11], (N_LAYERS_B, 2, H, Bk, Bk), Bk)
    b_igate_b = 0.01 * jax.random.normal(ks[12], (N_LAYERS_B, 2, R), f32)
    a0 = jax.random.uniform(ks[13], (N_LAYERS_B, 2, R), f32, minval=0.9, maxval=0.999)
    sig = a0 ** (1.0 / RG_C)
    lam_b = jnp.log(sig) - jnp.log1p(-sig)
    w_out_b = _normal(ks[14], (N_LAYERS_B, R, D), R)
    norm_ffn = 1.0 + 0.05 * jax.random.normal(ks[15], (DEPTH_2, D), f32)
    w_router_group = _normal(ks[16], (DEPTH_2, D, N_GROUPS), D)
    b_router_group = 0.01 * jax.random.normal(ks[17], (DEPTH_2, N_GROUPS), f32)
    w_router_expert = _normal(ks[18], (DEPTH_2, D, N_EXPERTS), D)
    b_router_expert = 0.01 * jax.random.normal(ks[19], (DEPTH_2, N_EXPERTS), f32)
    w_exp_gate = _normal(ks[20], (DEPTH_2, N_EXPERTS, D, D_EXPERT), D)
    w_exp_up = _normal(ks[21], (DEPTH_2, N_EXPERTS, D, D_EXPERT), D)
    w_exp_down = _normal(ks[22], (DEPTH_2, N_EXPERTS, D_EXPERT, D), D_EXPERT)
    norm_ple = 1.0 + 0.05 * jax.random.normal(ks[23], (DEPTH_2, D), f32)
    w_ple = _normal(ks[24], (DEPTH_2, PLE_DIM, D), PLE_DIM)
    w_ple_gate = _normal(ks[25], (DEPTH_2, D, D), D)
    b_ple_gate = 0.01 * jax.random.normal(ks[26], (DEPTH_2, D), f32)
    norm_final = 1.0 + 0.05 * jax.random.normal(ks[27], (D,), f32)
    return {'x': x, 'p': p, 'norm_mix': norm_mix,
            'w_in_a': w_in_a, 'conv_a': conv_a, 'w_out_a': w_out_a,
            'w_in_b': w_in_b, 'conv_b': conv_b, 'conv_bias_b': conv_bias_b,
            'w_rgate_b': w_rgate_b, 'b_rgate_b': b_rgate_b,
            'w_igate_b': w_igate_b, 'b_igate_b': b_igate_b,
            'lam_b': lam_b, 'w_out_b': w_out_b, 'norm_ffn': norm_ffn,
            'w_router_group': w_router_group, 'b_router_group': b_router_group,
            'w_router_expert': w_router_expert, 'b_router_expert': b_router_expert,
            'w_exp_gate': w_exp_gate, 'w_exp_up': w_exp_up, 'w_exp_down': w_exp_down,
            'norm_ple': norm_ple, 'w_ple': w_ple, 'w_ple_gate': w_ple_gate,
            'b_ple_gate': b_ple_gate, 'norm_final': norm_final}

def second_block(x, p, norm_mix, w_in_a, conv_a, w_out_a, w_in_b, conv_b, conv_bias_b,
              w_rgate_b, b_rgate_b, w_igate_b, b_igate_b, lam_b, w_out_b, norm_ffn,
              w_router_group, b_router_group, w_router_expert, b_router_expert,
              w_exp_gate, w_exp_up, w_exp_down, norm_ple, w_ple, w_ple_gate,
              b_ple_gate, norm_final):
    h = x
    for i in range(DEPTH_2):
        xn = rmsnorm_2(h, norm_mix[i])
        j = i // N_MIXERS
        if i % N_MIXERS == 0:
            mix = short_conv_mixer(xn, w_in_a[j], conv_a[j], w_out_a[j])
        else:
            mix = rglru_mixer(xn, w_in_b[j], conv_b[j], conv_bias_b[j], w_rgate_b[j], b_rgate_b[j],
                              w_igate_b[j], b_igate_b[j], lam_b[j], w_out_b[j])
        h = h + mix
        h = h + hier_moe(rmsnorm_2(h, norm_ffn[i]), w_router_group[i], b_router_group[i],
                         w_router_expert[i], b_router_expert[i],
                         w_exp_gate[i], w_exp_up[i], w_exp_down[i])
        gate = jax.nn.sigmoid(rmsnorm_2(h, norm_ple[i]) @ w_ple_gate[i] + b_ple_gate[i])
        h = h + gate * (p[i] @ w_ple[i])
    return rmsnorm_2(h, norm_final)


def setup_inputs(seed=0):
    out = dict(first_inputs(seed))
    for name, value in second_inputs(seed + 1).items():
        if name != "x":
            out[name + "_2"] = value
    return out


def reference(
    x, c, ctx, c_ctx, w_ada, b_ada, g_pre_mix, g_post_mix, g_pre_ffn, g_post_ffn, w_in,
    w_qkv_conv, a_log, dt_bias, g_gdn, w_fourier, w_out, w_up, w_dwc, w_down, p_2, norm_mix_2,
    w_in_a_2, conv_a_2, w_out_a_2, w_in_b_2, conv_b_2, conv_bias_b_2, w_rgate_b_2, b_rgate_b_2,
    w_igate_b_2, b_igate_b_2, lam_b_2, w_out_b_2, norm_ffn_2, w_router_group_2,
    b_router_group_2, w_router_expert_2, b_router_expert_2, w_exp_gate_2, w_exp_up_2,
    w_exp_down_2, norm_ple_2, w_ple_2, w_ple_gate_2, b_ple_gate_2, norm_final_2,
):
    x = first_block(
        x, c, ctx, c_ctx, w_ada, b_ada, g_pre_mix, g_post_mix, g_pre_ffn, g_post_ffn, w_in,
        w_qkv_conv, a_log, dt_bias, g_gdn, w_fourier, w_out, w_up, w_dwc, w_down,
    )
    return second_block(
        x, p_2, norm_mix_2, w_in_a_2, conv_a_2, w_out_a_2, w_in_b_2, conv_b_2, conv_bias_b_2,
        w_rgate_b_2, b_rgate_b_2, w_igate_b_2, b_igate_b_2, lam_b_2, w_out_b_2, norm_ffn_2,
        w_router_group_2, b_router_group_2, w_router_expert_2, b_router_expert_2, w_exp_gate_2,
        w_exp_up_2, w_exp_down_2, norm_ple_2, w_ple_2, w_ple_gate_2, b_ple_gate_2, norm_final_2,
    )


_drawn_inputs = setup_inputs


def setup_inputs(seed=0):
    import zlib

    import numpy as np

    out = dict(_drawn_inputs(seed))
    spreads = {}
    factors = {'b_rgate_b_2': 59.177,
     'b_igate_b_2': 31.412,
     'b_router_group_2': 5.198,
     'b_router_expert_2': 4.119,
     'norm_ple_2': 3.757,
     'b_ple_gate_2': 31.043}
    for name, (base, spread) in spreads.items():
        noise = np.random.default_rng([zlib.crc32(name.encode()), seed]).standard_normal(out[name].shape)
        drawn = base * np.exp(spread * noise) if base else spread * noise
        out[name] = __import__('jax').numpy.asarray(drawn.astype(out[name].dtype))
    for name, factor in factors.items():
        out[name] = (out[name] * factor).astype(out[name].dtype)
    return out
```

```python
import math

import numpy as np
import concourse.bass as bass
from concourse import mybir

F32 = mybir.dt.float32
I32 = mybir.dt.int32
U32 = mybir.dt.uint32
ALU = mybir.AluOpType
ACT = mybir.ActivationFunctionType
AX = mybir.AxisListType.X

P = 128
D = 1024
KT = D // P
SEQ = 256
NH = SEQ // P
HEADS = 4
DFF = 2816
FT = DFF // P
GRID_W = 64
ROWS = SEQ // GRID_W
EPS = 1e-6
RG_C = 8.0
N_GROUPS = 4
PER_GROUP = 8
E = N_GROUPS * PER_GROUP
DE = 512
SLOTS = 64
PAIRS = E // 2
RING = 6
CHUNK = 4096
LEVELS = 7
NEG = -1e30
BANKS = 4
LOG1P = [1.0 / (2 * i + 1) for i in range(8)]


def layout(items):
    at, out = 0, {}
    for name, n in items:
        out[name] = (at, n)
        at += n
    return out, at


PARAMS, PARAMS_N = layout([
    ("c", 16), ("b_ada", 48), ("g_pre_mix", 8), ("g_post_mix", 8), ("g_pre_ffn", 8), ("g_post_ffn", 8),
    ("w_ab", KT * 16), ("conv", 12 * 3), ("a_log", 8), ("dt_bias", 8), ("g_gdn", 1), ("w_dwc", FT * 9),
    ("norm_mix", 16), ("conv_a", 8 * 3), ("conv_b", 8 * 4), ("conv_bias", 8), ("b_rg", 16), ("b_ig", 16),
    ("lam", 16), ("norm_ffn", 16), ("norm_ple", 16), ("b_ple", 16), ("norm_final", 8),
    ("w_router", 2 * KT * 36), ("b_router", 2 * 36),
])
CONSTS, CONSTS_N = layout([
    ("ident", P), ("upper", P), ("lower", P), ("strict", P), ("ones", P), ("sel", 2), ("iota", SLOTS), ("eps", 1),
])
MASKS, MASKS_N = layout([("neg", 2 * P), ("level", LEVELS * P)])
FOURIER, FOURIER_N = layout([("cos_c", P), ("nsin_c", P), ("w_f", 4 * P), ("cos_l", 2 * SEQ), ("sin_l", 2 * SEQ)])

DENSE = [("ada", 12, CHUNK), ("w_in", 5, CHUNK), ("fourier", 1, FOURIER_N), ("w_out", 2, CHUNK), ("w_up", 11, CHUNK),
         ("w_down", 8, FT * P), ("w_in_a", 6, CHUNK), ("w_out_a", 2, CHUNK), ("moe0", 0, 0), ("ple0", 2, CHUNK),
         ("ple_w0", 1, 2 * D), ("w_in_b", 4, CHUNK), ("gates", 2, CHUNK), ("w_out_b", 2, CHUNK), ("moe1", 0, 0),
         ("ple1", 2, CHUNK), ("ple_w1", 1, 2 * D)]
USES = [("kv", 8), ("q", 2), ("z", 2), ("u", 2), ("vtok", 4), ("ktok", 4), ("dft_w", 2), ("dft_b", 4), ("dft_y", 2),
        ("w_out", 4), ("up", FT), ("down", 4), ("in_a", 12), ("out_a", 4), ("ple0", 8), ("in_b", 8), ("gates", 16),
        ("out_b", 4), ("ple1", 8)]


def plan():
    first, n, use, at = {}, 0, {}, 0
    for name, count, _ in DENSE:
        first[name] = n
        n += 6 * PAIRS if name.startswith("moe") else count
    for name, count in USES:
        use[name] = at
        at += count
    free = {}
    for c in range(12):
        free[first["ada"] + c] = ("ada_mm", c + 1)
    for c, last in enumerate((4, 8, 10, 12, 14)):
        free[first["w_in"] + c] = ("dense_full", last)
    free[first["fourier"]] = ("dense_full", use["dft_y"] + 2)
    for stage, users, per, n_chunks in (("w_out", "w_out", 2, 2), ("w_up", "up", 2, 11), ("w_in_a", "in_a", 2, 6),
                                        ("w_out_a", "out_a", 2, 2), ("w_in_b", "in_b", 2, 4), ("w_out_b", "out_b", 2, 2)):
        for c in range(n_chunks):
            free[first[stage] + c] = ("dense_full", use[users] + per * (c + 1))
    for c in range(8):
        free[first["w_down"] + c] = ("dense_full", use["down"] + c // 2 + 1)
    for c in range(2):
        free[first["gates"] + c] = ("dense_full", use["gates"] + 16)
    for layer in range(2):
        free[first[f"ple{layer}"]] = ("dense_full", use[f"ple{layer}"] + 3)
        free[first[f"ple{layer}"] + 1] = ("dense_full", use[f"ple{layer}"] + 7)
        free[first[f"ple_w{layer}"]] = ("dense_full", use[f"ple{layer}"] + 8)
        for c, (sem, per) in enumerate((("gate_mm", 1), ("gate_mm", 1), ("up_mm", 1), ("up_mm", 1), ("down_mm", 2), ("down_mm", 2))):
            for i in range(PAIRS):
                free[first[f"moe{layer}"] + 6 * i + c] = (sem, per * (layer * PAIRS + i + 1))
    return first, use, free


FIRST, USE, FREE = plan()
WORK, WORK_N = layout([
    ("kc", 2048), ("vc", 2048), ("qc", 1024), ("ktok", 2048), ("vtok", 2048), ("zs", 1024), ("cat", 2048),
    ("S", 1024), ("oT", 1024), ("masks", MASKS_N), ("dtmp", 4096), ("small", 328),
])
SEMAPHORES = [
    "param_load", "const_load", "ctx_load", "x_load", "mask_load", "p_load", "out_store",
    "zeroed", "c_cols", "ada_mm", "ada_row", "mod_ready", "dve_step", "act_step", 
    "sq_ready", "ss_ready", "rstd_ready", "xn_ready", "h_ready", "dense_full",
    "ab_mm", "ab_sb", "ab_cols", "ab_act", "ab_dve", "silu_ready",
    "qk_sq", "qk_ss", "qk_rstd", "qk_norm",
    "g_rows", "g_diff", "g_masked", "decay", "at_ready", "g_pool", "lvl_mask", "lvl_p", "lvl_p_sb", "lvl_tp", "lvl_t",
    "qk_mm", "ks_mm", "x_ready", "vn_mm", "vn_sb", "o_mm", "ds_mm", "s_ready", "o_ready",
    "o_sq", "o_ss", "o_rstd", "cat_ready", "ffn_conv", "ffn_silu", "c_sb",
    "tok_mm", "tok_sb", "tok_sb2", "mask_ready", "gates_ready", "ada_sum", "lg_mm", "lg_sb", "lg_cols", "route_dve", "route_act", "rank_mm", "route_ready", 
    "onehot", "onehot_w", "gather_mm", "xg_act", "xg_dve", "gate_mm", "up_mm", "sg_sb", "hh_sb", "t_mm", "ht_sb",
    "down_mm", "y_act", "y_dve", "pwt_mm", "pwt_sb", "scat_mm", "scat_add", "moe_done",
    "lru_log", "lru_exp", "lru_var", "lru_sqrt", "lru_h", "fin_ready",
] + [f"slot_full{r}" for r in range(RING)] + [f"dense_free{b}" for b in range(BANKS)] \
  + [f"ov_{what}{layer}" for layer in range(2) for what in ("full", "gu", "sg", "hh", "t", "ht", "down", "add")]


def build(nc, t):
    S = {name: nc.alloc_semaphore(name) for name in SEMAPHORES}

    ring = [nc.alloc_sbuf_tensor(f"ring{r}", [P, CHUNK], F32) for r in range(RING)]
    bank = [nc.alloc_psum_tensor(f"bank{b}", [P, 512], F32) for b in range(8)]
    hT = nc.alloc_sbuf_tensor("hT", [P, KT, SEQ], F32)
    xn = nc.alloc_sbuf_tensor("xn", [P, KT, 2, SEQ], F32)
    params = nc.alloc_sbuf_tensor("params", [P, PARAMS_N], F32)
    consts = nc.alloc_sbuf_tensor("consts", [P, CONSTS_N], F32)
    work = nc.alloc_sbuf_tensor("work", [P, WORK_N], F32)
    mod = nc.alloc_sbuf_tensor("mod", [P, 48, 2], F32)
    gains = nc.alloc_sbuf_tensor("gains", [P, 5, KT], F32)
    flag = nc.alloc_sbuf_tensor("flag", [P, 1], I32)

    def par(name, a=0, size=None):
        at, n = PARAMS[name]
        return params[:, at + a:at + (n if size is None else a + size)]

    def con(name):
        at, n = CONSTS[name]
        return consts[:, at:at + n]

    def wk(name, size=None, off=0):
        at, n = WORK[name]
        return work[:, at + off:at + off + (size or n)]

    def flat(at, n):
        assert at + n <= WORK_N
        return work[:, at:at + n]

    ident, ones, strict = con("ident"), con("ones"), con("strict")
    cums = [con("upper"), con("lower")]

    kc = wk("kc").rearrange("p (h s t) -> p h s t", h=HEADS, s=2)
    vc = wk("vc").rearrange("p (h s t) -> p h s t", h=HEADS, s=2)
    qc = wk("qc").rearrange("p (h t) -> p h t", h=HEADS)
    ktok = wk("ktok").rearrange("p (u h d) -> p u h d", u=4, h=HEADS)
    vtok = wk("vtok").rearrange("p (u h d) -> p u h d", u=4, h=HEADS)
    ctxT = wk("ktok").rearrange("p (k t) -> p k t", k=KT)
    zs = wk("zs").rearrange("p (h t) -> p h t", h=HEADS)
    cat = wk("cat").rearrange("p (k t) -> p k t", k=KT)
    uT = wk("oT").rearrange("p (g t) -> p g t", g=4)
    state = wk("S").rearrange("p (d h e) -> p d h e", d=2, h=HEADS)
    oT = wk("oT").rearrange("p (h t) -> p h t", h=HEADS)
    neg = wk("masks", 2 * P).rearrange("p (d t) -> p d t", d=2)
    level = wk("masks", LEVELS * P, 2 * P).rearrange("p (l t) -> p l t", l=LEVELS)
    dtmp = wk("dtmp").rearrange("p (n d h t) -> p n d h t", n=4, d=2, h=HEADS)
    decayT, attnT, qd, kd = (dtmp[:, n] for n in range(4))
    tri = xn[:].rearrange("p k s t -> p (k s t)").rearrange("p (n d h t) -> p n d h t", n=4, d=2, h=HEADS)
    tinv, tinvT, pmat, amatT = (tri[:, n] for n in range(4))
    xv = wk("vc").rearrange("p (n d h t) -> p n d h t", n=2, d=2, h=HEADS)
    lmask, xmat = xv[:, 0], xv[:, 1]
    vnew = lmask
    sq2 = wk("dtmp").rearrange("p (k s t) -> p k s t", k=KT, s=2)
    sqk = wk("dtmp", 1024, 3072).rearrange("p (n t) -> p n t", n=2)
    ada_row = wk("cat", 1024).rearrange("p (m n) -> p m n", m=2)
    c_cols = wk("S", KT * 32).rearrange("p (k m) -> p k m", k=KT)
    ab_rows = wk("dtmp", 512)
    fo_w = wk("dtmp", 1024).rearrange("p (x n) -> p x n", x=2)
    fo_b = wk("dtmp", 2048, 1024).rearrange("p (x u g e) -> p x u g e", x=2, u=2, g=4)
    ab = wk("small", 64, 0).rearrange("p (u c) -> p u c", u=4)
    beta = wk("small", 32, 64).rearrange("p (u c) -> p u c", u=4)
    glog = wk("small", 32, 96).rearrange("p (u c) -> p u c", u=4)
    gtmp = [wk("small", 32, 128 + 32 * i).rearrange("p (u c) -> p u c", u=4) for i in range(5)]
    gcol = wk("small", 8, 288).rearrange("p (d h) -> p d h", d=2)
    egcol = wk("small", 8, 296).rearrange("p (d h) -> p d h", d=2)
    begc = wk("small", 8, 304).rearrange("p (d h) -> p d h", d=2)
    egl = wk("small", 8, 312).rearrange("p (d h) -> p d h", d=2)
    alog_e = wk("small", 8, 320)

    lnt = wk("dtmp", 512, 2048)

    yT = flat(0, 2048).rearrange("p (k t) -> p k t", k=KT)
    xnT, sq1 = xn[:, :, 0], xn[:, :, 1]
    prod = flat(2048, FT * SEQ).rearrange("p (f t) -> p f t", f=FT)
    acc = flat(7680, 1024).rearrange("p (n t) -> p n t", n=4)
    sgate = flat(8704, 512).rearrange("p (n t) -> p n t", n=2)
    tmp = flat(9216, 1024).rearrange("p (n t) -> p n t", n=4)
    c_sb = flat(2048, 512).rearrange("p (n t) -> p n t", n=2)
    ch = flat(2560, 512).rearrange("p (n t) -> p n t", n=2)
    cu = flat(3072, 1024).rearrange("p (n t) -> p n t", n=4)
    xtok = flat(0, 2048).rearrange("p (u f) -> p u f", u=NH)
    xg = flat(2048, 1024).rearrange("p (k s) -> p k s", k=KT)
    sg, hh = flat(3072, 512), flat(3584, 512)
    hidT = flat(4096, 512).rearrange("p (j s) -> p j s", j=4)
    ysb = flat(4608, 1024)
    pwt = flat(5632, 256)
    oneh = flat(5888, 256).rearrange("p (u x s) -> p u x s", u=NH, x=2)
    onehw = flat(6144, 256).rearrange("p (u x s) -> p u x s", u=NH, x=2)
    lgT = flat(6400, 256)
    lg = flat(6656, 72).rearrange("p (u c) -> p u c", u=NH)
    EP = E + 2
    rankm = flat(7928, NH * EP).rearrange("p (u e) -> p u e", u=NH)
    wgt = flat(7996, NH * EP).rearrange("p (u e) -> p u e", u=NH)
    wov = flat(8064, NH * E).rearrange("p (u e) -> p u e", u=NH)

    def rt(at, n):
        return flat(6728 + at, NH * n).rearrange("p (u c) -> p u c", u=NH)

    gsb = flat(2048, 2048).rearrange("p (k t) -> p k t", k=KT)
    yg = flat(0, 2048).rearrange("p (k t) -> p k t", k=KT)
    uu = flat(2048, 2048).rearrange("p (k t) -> p k t", k=KT)
    rr = flat(4096, 2048).rearrange("p (k t) -> p k t", k=KT)
    hs = flat(6144, 2048).rearrange("p (k t) -> p k t", k=KT)
    ii = flat(9216, 2048).rearrange("p (k t) -> p k t", k=KT)
    aa = flat(11264, 2048).rearrange("p (k t) -> p k t", k=KT)
    vv = flat(14336, 2048).rearrange("p (k t) -> p k t", k=KT)
    nls = flat(13312, 16)
    nlt = [flat(13328 + 16 * i, 16) for i in range(5)]
    hb = xn[:, :, 1]
    pT = flat(16384, 1024).rearrange("p (l k t) -> p l k t", l=2, k=2)

    def arrived(eng, n):
        eng.wait_ge(S[f"slot_full{n % RING}"], 16 * (n // RING + 1))
        return ring[n % RING]

    def released(eng, n):
        eng.wait_ge(S[f"dense_free{n % BANKS}"], n // BANKS + 1)

    ctx_block = nc.Block()
    block = ctx_block.__enter__()

    @block.sync
    def _(sp):
        def load(n, src, size):
            if n >= RING:
                sem, value = FREE[n - RING]
                sp.wait_ge(S[sem], value)
            sp.dma_start(ring[n % RING][:, 0:size], src).then_inc(S[f"slot_full{n % RING}"], 16)

        seen = 0
        for name, count, size in DENSE:
            base = FIRST[name]
            if not name.startswith("moe"):
                for c in range(count):
                    load(base + c, t["dense"][seen + c][:, 0:size], size)
                seen += count
                continue
            layer = int(name[3:])
            gate, up = (t[w][layer].rearrange("e (p j) f -> e p (j f)", j=KT) for w in ("w_gate", "w_up"))
            down = t["w_down"][layer].rearrange("e (p j) f -> e p (j f)", j=4)
            chunks = (gate, gate, up, up, down, down)
            for c, w in enumerate(chunks):
                load(base + c, w[c % 2], CHUNK)
            with sp.Fori(1, PAIRS) as i:
                for c, w in enumerate(chunks):
                    r = (base + c) % RING
                    sem, value = FREE[base + c]
                    sp.wait_ge(S[sem], value + (i - 1) * (2 if c >= 4 else 1))
                    sp.dma_start(ring[r][:], w[i * 2 + c % 2]).then_inc(S[f"slot_full{r}"], 16)
            sp.wait_ge(S["route_ready"], layer + 1)
            over = sp.value_load(flag[0:1, 0:1], min_val=0, max_val=1)
            with sp.If(over > 0):
                gate, up = (t[w][layer].rearrange("e (j p) f -> e p j f", p=P) for w in ("w_gate", "w_up"))
                down = t["w_down"][layer].rearrange("e (j p) f -> e p j f", p=P)
                with sp.Fori(0, E) as e:
                    sp.wait_ge(S[f"ov_down{layer}"], e * 2 + 1)
                    for c, (w, k) in enumerate(((gate, KT), (up, KT), (down, 4))):
                        sp.dma_start(ring[c][:].rearrange("p (j f) -> p j f", j=k), w[e]).then_inc(S[f"ov_full{layer}"], 16)
                sp.wait_ge(S[f"ov_down{layer}"], 2 * E + 1)
                sp.nop()
        sp.wait_ge(S["fin_ready"], 1)
        sp.dma_start(t["out"], yT).then_inc(S["out_store"], 16)
        sp.wait_ge(S["out_store"], 16)

    @block.tensor
    def _(pe):
        mm = nc.tensor.matmul
        count = {}

        def signal(ins, name):
            ins.then_inc(S[name], 1)
            count[name] = count.get(name, 0) + 1
            return count[name]

        def dense(n, tiles):
            if n >= BANKS:
                released(pe, n - BANKS)
            for a, b, products in tiles:
                for k, (w, x) in enumerate(products):
                    last = mm(bank[n % BANKS][:, a:b], w, x, start=k == 0, stop=k == len(products) - 1)
            assert signal(last, "dense_full") == n + 1

        def weights(n, tile, n_k=KT, width=512):
            w = arrived(pe, n)
            return [w[:, k * width + tile * P:k * width + tile * P + P] for k in range(n_k)]

        def projection(stage, chunk, uses, x):
            for b in range(uses):
                tiles = [weights(FIRST[chunk] + b // 2, (2 * b + i) % 4) for i in range(2)]
                dense(USE[stage] + b, [(SEQ * i, SEQ * i + SEQ, list(zip(tiles[i], x))) for i in range(2)])

        def sum_squares():
            for k in range(KT):
                if k % 2 == 0:
                    pe.wait_ge(S["sq_ready"], 4 * (count.get("norms", 0) + 1) + k // 2 + 1)
                last = mm(bank[4][:, 0:SEQ], ones, sq1[:, k], start=k == 0, stop=k == KT - 1)
            signal(last, "ss_ready")
            count["norms"] = count.get("norms", 0) + 1

        def normed():
            pe.wait_ge(S["xn_ready"], 8 * normed.n)
        normed.n = 1

        pe.wait_ge(S["const_load"], 16)
        pe.wait_ge(S["c_cols"], 1)

        def ada_sum(m):
            pe.wait_ge(S["ada_row"], m + 1)
            for i in range(4):
                at = 2 * (4 * m + i)
                last = mm(bank[6][:, at:at + 2], ada_row[:, m % 2, P * i:P * i + P], con("sel"), start=True, stop=True)
            signal(last, "ada_sum")

        for m in range(12):
            w = arrived(pe, FIRST["ada"] + m)
            if m >= 2:
                pe.wait_ge(S["ada_row"], m - 1)
            for kk in range(2):
                for j in range(4):
                    k = 2 * j + kk
                    last = mm(bank[4 + m % 2][32 * j:32 * j + 32, :], c_cols[:, k, :], w[:, 512 * k:512 * k + 512],
                              start=kk == 0, stop=kk == 1)
            signal(last, "ada_mm")
            if m:
                ada_sum(m - 1)
        ada_sum(11)

        for k in range(KT):
            pe.wait_ge(S["sq_ready"], k // 2 + 1)
            last = mm(bank[4][:], ones, sq2[:, k].rearrange("p s t -> p (s t)"), start=k == 0, stop=k == KT - 1)
        signal(last, "ss_ready")

        both = [xn[:, k].rearrange("p s t -> p (s t)") for k in range(KT)]
        w_ab = par("w_ab").rearrange("p (k c) -> p k c", k=KT)
        for k in range(KT):
            pe.wait_ge(S["xn_ready"], k + 1)
            last = mm(bank[7][0:16, :], w_ab[:, k], both[k], start=k == 0, stop=k == KT - 1)
        signal(last, "ab_mm")
        for i in range(8):
            w = weights(FIRST["w_in"] + i // 4, i % 4)
            dense(USE["kv"] + i, [(0, 512, list(zip(w, both)))])
        pe.wait_ge(S["ab_sb"], 1)
        for u in range(4):
            last = nc.tensor.transpose(bank[6][:, 16 * u:16 * u + 16], ab_rows[0:16, P * u:P * u + P], ident[0:16, 0:16])
        signal(last, "ab_cols")
        x_lat = [xn[:, k, 1] for k in range(KT)]

        def four(stage, c):
            for b in range(2):
                tiles = [weights(FIRST["w_in"] + c, 2 * b + i) for i in range(2)]
                dense(USE[stage] + b, [(SEQ * i, SEQ * i + SEQ, list(zip(tiles[i], x_lat))) for i in range(2)])

        four("q", 2)
        four("z", 3)
        four("u", 4)
        pe.wait_ge(S["silu_ready"], 8)
        for u in range(4):
            s, half = u // 2, u % 2
            released(pe, USE["vtok"] + u - BANKS)
            for h in range(HEADS):
                last = nc.tensor.transpose(bank[(USE["vtok"] + u) % BANKS][:, P * h:P * h + P],
                                           vc[:, h, s, P * half:P * half + P], ident)
            signal(last, "dense_full")
        for a in range(6):
            pe.wait_ge(S["qk_sq"], a + 1)
            if a >= 2:
                pe.wait_ge(S["qk_rstd"], a - 1)
            signal(mm(bank[4 + a % 2][:], ones, sqk[:, a % 2], start=True, stop=True), "qk_ss")
        pe.wait_ge(S["qk_norm"], 6)
        for u in range(4):
            s, half = u // 2, u % 2
            released(pe, USE["ktok"] + u - BANKS)
            for h in range(HEADS):
                last = nc.tensor.transpose(bank[(USE["ktok"] + u) % BANKS][:, P * h:P * h + P],
                                           kc[:, h, s, P * half:P * half + P], ident)
            signal(last, "dense_full")

        w = arrived(pe, FIRST["fourier"])

        def fo(name, a=0, n=None):
            at, size = FOURIER[name]
            return w[:, at + a:at + a + (n or size)]

        for x, name in enumerate(("cos_c", "nsin_c")):
            dense(USE["dft_w"] + x, [(0, 512, [(fo(name), fo("w_f"))])])
        released(pe, USE["dft_w"])
        released(pe, USE["dft_w"] + 1)
        for x in range(2):
            for u in range(NH):
                dense(USE["dft_b"] + 2 * x + u, [
                    (P * g, P * g + P, [(uT[:, g, P * u:P * u + P], fo_w[:, x, P * g:P * g + P])]) for g in range(4)])
        for b in range(4):
            released(pe, USE["dft_b"] + b)
        for b in range(2):
            dense(USE["dft_y"] + b, [
                (SEQ * i, SEQ * i + SEQ, [(fo_b[:, x, u, 2 * b + i], fo(("cos_l", "sin_l")[x], SEQ * u, SEQ))
                                          for x in range(2) for u in range(NH)]) for i in range(2)])

        banks = [[bank[0], bank[1], bank[4], bank[5]], [bank[2], bank[3], bank[6], bank[7]]]
        for b in range(2):
            released(pe, USE["dft_y"] + b)
        pe.wait_ge(S["gates_ready"], 1)

        def heads(out, left, right, start=True, stop=True):
            for h in range(HEADS):
                last = mm(out[:, P * h:P * h + P], left(h), right(h), start=start, stop=stop)
            return last

        for n in range(4):
            s, c = n // 2, n % 2
            for d in range(2):
                half, e = (c if d == 0 else 1 - c), 2 * n + d
                a0, a1, a2, a3 = banks[d]
                token = slice(P * half, P * half + P)
                u = 2 * s + half
                if n:
                    pe.wait_ge(S["s_ready"], e - 1)
                heads(a0, lambda h: glog[:, u, 4 * d + h:4 * d + h + 1].to_broadcast([P, P]), lambda h: cums[d])
                heads(a1, lambda h: beta[:, u, 4 * d + h:4 * d + h + 1].to_broadcast([P, P]), lambda h: ident)
                heads(a2, lambda h: kc[:, h, s, token], lambda h: kc[:, h, s, token])
                signal(mm(a3[:, 0:HEADS], cums[d], glog[:, u, 4 * d:4 * d + 4], start=True, stop=True), "g_rows")
            for d in range(2):
                half, e = (c if d == 0 else 1 - c), 2 * n + d
                a0, a1, a2, a3 = banks[d]
                token = slice(P * half, P * half + P)
                if s:
                    pe.wait_ge(S["g_diff"], e + 1)
                    signal(heads(a3, lambda h: kc[:, h, s, token], lambda h: qc[:, h, token]), "qk_mm")
            for l in range(LEVELS):
                for d in range(2):
                    half, e = (c if d == 0 else 1 - c), 2 * n + d
                    a0, a1, a2, a3 = banks[d]
                    i = 2 * (LEVELS * n + l) + d
                    pe.wait_ge(S["lvl_mask"], i + 1)
                    if l:
                        pe.wait_ge(S["lvl_t"], i - 1)
                        signal(heads(a0, lambda h: lmask[:, d, h], lambda h: tinv[:, d, h]), "lvl_p")
                    else:
                        pe.wait_ge(S["decay"], e + 1)
                        signal(heads(a0, lambda h: lmask[:, d, h], lambda h: ident), "lvl_p")
                for d in range(2):
                    a0, a1, a2, a3 = banks[d]
                    i = 2 * (LEVELS * n + l) + d
                    if l:
                        pe.wait_ge(S["lvl_p_sb"], 2 * ((LEVELS - 1) * n + l - 1) + d + 1)
                        if l < LEVELS - 1:
                            heads(a1, lambda h: tinvT[:, d, h], lambda h: pmat[:, d, h])
                        signal(heads(a2, lambda h: pmat[:, d, h], lambda h: tinvT[:, d, h]), "lvl_tp")
            for d in range(2):
                half, e = (c if d == 0 else 1 - c), 2 * n + d
                a0 = banks[d][0]
                token = slice(P * half, P * half + P)
                if n:
                    signal(heads(a0, lambda h: kc[:, h, s, token], lambda h: state[:, d, h]), "ks_mm")
            for d in range(2):
                a1 = banks[d][1]
                pe.wait_ge(S["lvl_t"], 2 * (LEVELS * n + LEVELS - 1) + d + 1)
                if n:
                    pe.wait_ge(S["x_ready"], 2 * (n - 1) + d + 1)
                else:
                    pe.wait_ge(S["g_pool"], d + 1)
                signal(heads(a1, lambda h: tinvT[:, d, h], lambda h: xmat[:, d, h]), "vn_mm")
            for d in range(2):
                half, e = (c if d == 0 else 1 - c), 2 * n + d
                a2, a3 = banks[d][2:]
                pe.wait_ge(S["vn_sb"], e + 1)
                pe.wait_ge(S["g_pool"], e + 1)
                if s:
                    for h in range(HEADS):
                        mm(a2[:, P * h:P * h + P], state[:, d, h], qd[:, d, h], start=True, stop=False)
                        last = mm(a2[:, P * h:P * h + P], vnew[:, d, h], attnT[:, d, h], start=False, stop=True)
                    signal(last, "o_mm")
                if n < 3:
                    signal(heads(a3, lambda h: kd[:, d, h], lambda h: vnew[:, d, h]), "ds_mm")

        for b in range(2):
            pe.wait_ge(S["o_sq"], b + 1)
            signal(mm(bank[4 + b][:], ones, sqk[:, b], start=True, stop=True), "o_ss")
        pe.wait_ge(S["cat_ready"], 4)
        projection("w_out", "w_out", 4, [cat[:, k] for k in range(KT)])

        xs = [xnT[:, k] for k in range(KT)]

        def norm_input():
            sum_squares()
            normed.n += 1
            normed()

        sum_squares()
        norm_input()
        projection("up", "w_up", FT, xs)
        for b in range(BANKS):
            released(pe, USE["up"] + FT - 1 - b)
        for b in range(4):
            tiles = []
            for i in range(2):
                w = arrived(pe, FIRST["w_down"] + 2 * b + i)
                tiles.append((SEQ * i, SEQ * i + SEQ, [(w[:, P * k:P * k + P], prod[:, k]) for k in range(FT)]))
            dense(USE["down"] + b, tiles)
        sum_squares()
        norm_input()
        projection("in_a", "w_in_a", 12, xs)
        for b in range(2):
            released(pe, USE["in_a"] + 11 - b)
        projection("out_a", "w_out_a", 4, [yT[:, k] for k in range(KT)])

        def moe(layer):
            norm_input()
            for b in range(BANKS):
                released(pe, moe.last_use[layer] - b)
            for m in range(4):
                u = m // 2
                b = bank[m]
                for i in range(4):
                    last = nc.tensor.transpose(b[:, P * i:P * i + P], xnT[:, 4 * (m % 2) + i, P * u:P * u + P], ident)
                signal(last, "tok_mm")
            w_r = par("w_router").rearrange("p (l k c) -> p l k c", l=2, k=KT)
            for k in range(KT):
                last = mm(bank[7][0:36, 0:SEQ], w_r[:, layer, k], xs[k], start=k == 0, stop=k == KT - 1)
            signal(last, "lg_mm")
            pe.wait_ge(S["lg_sb"], layer + 1)
            for u in range(NH):
                last = nc.tensor.transpose(bank[6][:, 36 * u:36 * u + 36], lgT[0:36, P * u:P * u + P], ident[0:36, 0:36])
            signal(last, "lg_cols")
            pe.wait_ge(S["mask_ready"], layer + 1)
            m0, m1 = rt(240, E)[:, 0], rt(240, E)[:, 1]
            mm(bank[5][:, 0:E], strict, m0, start=True, stop=True)
            mm(bank[5][:, E:2 * E], ones, m0, start=True, stop=False)
            mm(bank[5][:, E:2 * E], strict, m1, start=False, stop=True)
            mm(bank[5][:, 2 * E:3 * E], ones, m0, start=True, stop=False)
            signal(mm(bank[5][:, 2 * E:3 * E], ones, m1, start=False, stop=True), "rank_mm")

            done, extra = layer * PAIRS, layer * (PAIRS + 1)

            def gather(i):
                pe.wait_ge(S["onehot"], i + extra + 1)
                for k in range(KT):
                    out = bank[2 + k // 4][:, P * (k % 4):P * (k % 4) + P]
                    for u in range(NH):
                        last = mm(out, xtok[:, u, k:D:KT], oneh[:, u].rearrange("p x s -> p (x s)"),
                                  start=u == 0, stop=u == NH - 1)
                last.then_inc(S["gather_mm"], 1)

            def scatter(i):
                pe.wait_ge(S["y_act"], i + done + layer)
                pe.wait_ge(S["y_dve"], i + done + layer)
                pe.wait_ge(S["pwt_sb"], i + done + layer)
                for q in range(4):
                    if q in (0, 3):
                        pe.wait_ge(S["scat_add"], (i - 1) * 4 + (1 if q == 3 else 0) + layer * (4 * PAIRS + 5) + 1)
                    b = bank[(5, 2, 3, 5)[q]]
                    for x in range(2):
                        last = mm(b[:, SEQ * x:SEQ * x + SEQ], ysb[:, P * (2 * q + x):P * (2 * q + x) + P], pwt,
                                  start=True, stop=True)
                    last.then_inc(S["scat_mm"], 1)

            def arrived_pair(i, c):
                n = FIRST[f"moe{layer}"] + c
                pe.wait_ge(S[f"slot_full{n % RING}"], i * 16 + 16 * (n // RING + 1))
                return ring[n % RING]

            pe.wait_ge(S["tok_sb"], 2 * (layer + 1))
            pe.wait_ge(S["tok_sb2"], 2 * (layer + 1))
            gather(0)
            with pe.Fori(0, PAIRS) as i:
                pe.wait_ge(S["xg_act"], i + extra + 1)
                pe.wait_ge(S["xg_dve"], i + extra + 1)
                for c, b, sem in ((0, bank[0], "gate_mm"), (2, bank[1], "up_mm")):
                    ws = [arrived_pair(i, c + x) for x in range(2)]
                    for k in range(KT):
                        for x in range(2):
                            last = mm(b[64 * x:64 * x + 64, :], xg[:, k, 64 * x:64 * x + 64],
                                      ws[x][:, 512 * k:512 * k + 512], start=k == 0, stop=k == KT - 1)
                    last.then_inc(S[sem], 1)
                pe.wait_ge(S["scat_add"], i * 4 + layer * (4 * PAIRS + 5) + 1)
                gather(i + 1)
                pe.wait_ge(S["pwt_sb"], i + 1 + done + layer)
                pe.wait_ge(S["hh_sb"], i + 1 + done)
                for j in range(4):
                    last = nc.tensor.transpose(bank[4][:, P * j:P * j + P], hh[:, j:DE:4], ident)
                last.then_inc(S["t_mm"], 1)
                pe.wait_ge(S["xg_act"], i + extra + 2)
                pe.wait_ge(S["xg_dve"], i + extra + 2)
                scatter(i + 1)
                pe.wait_ge(S["ht_sb"], i + 1 + done)
                ws = [arrived_pair(i, 4 + x) for x in range(2)]
                for half in range(2):
                    for j in range(4):
                        for x in range(2):
                            at = D * j + 512 * half
                            last = mm(bank[6 + half][64 * x:64 * x + 64, :], hidT[:, j, 64 * x:64 * x + 64],
                                      ws[x][:, at:at + 512], start=j == 0, stop=j == 3)
                    last.then_inc(S["down_mm"], 1)
                pe.wait_ge(S["onehot_w"], i + 1 + done)
                for u in range(NH):
                    last = nc.tensor.transpose(bank[4][:, P * u:P * u + P], onehw[:, u].rearrange("p x s -> p (x s)"), ident)
                last.then_inc(S["pwt_mm"], 1)
            scatter(PAIRS + 1)

            over = pe.value_load(flag[0:1, 0:1], min_val=0, max_val=1)
            with pe.If(over > 0):
                with pe.Fori(0, E) as e:
                    pe.wait_ge(S[f"ov_full{layer}"], e * 48 + 48)
                    for u in range(NH):
                        pe.wait_ge(S[f"ov_add{layer}"], e * 2 + u + 1)
                        for b in range(2):
                            for k in range(KT):
                                last = mm(bank[b][:], xnT[:, k, P * u:P * u + P], ring[b][:, 512 * k:512 * k + 512],
                                          start=k == 0, stop=k == KT - 1)
                        last.then_inc(S[f"ov_gu{layer}"], 1)
                        pe.wait_ge(S[f"ov_hh{layer}"], e * 2 + u + 1)
                        for j in range(4):
                            last = nc.tensor.transpose(bank[4][:, P * j:P * j + P], hh[:, P * j:P * j + P], ident)
                        last.then_inc(S[f"ov_t{layer}"], 1)
                        pe.wait_ge(S[f"ov_ht{layer}"], e * 2 + u + 1)
                        for f in range(KT):
                            out = bank[6 + f // 4][:, P * (f % 4):P * (f % 4) + P]
                            for j in range(4):
                                last = mm(out, ring[2][:, D * j + P * f:D * j + P * f + P], hidT[:, j],
                                          start=j == 0, stop=j == 3)
                        last.then_inc(S[f"ov_down{layer}"], 1)
                pe.wait_ge(S[f"ov_add{layer}"], 2 * E + 1)
                nc.tensor.nop()
            pe.wait_ge(S["moe_done"], layer + 1)

        def ple(layer):
            norm_input()
            w = None
            for b in range(4):
                chunk = FIRST[f"ple{layer}"] + b // 2
                tiles = [weights(chunk, (2 * b + i) % 4) for i in range(2)]
                dense(USE[f"ple{layer}"] + 2 * b, [(SEQ * i, SEQ * i + SEQ, list(zip(tiles[i], xs))) for i in range(2)])
                w = arrived(pe, FIRST[f"ple_w{layer}"])
                pe.wait_ge(S["p_load"], 16)
                dense(USE[f"ple{layer}"] + 2 * b + 1, [
                    (SEQ * i, SEQ * i + SEQ, [(w[:, D * k + P * (2 * b + i):D * k + P * (2 * b + i) + P], pT[:, layer, k])
                                              for k in range(2)]) for i in range(2)])

        moe.last_use = [USE["out_a"] + 3, USE["out_b"] + 3]
        moe(0)
        ple(0)
        norm_input()
        projection("in_b", "w_in_b", 8, xs)
        for b in range(BANKS):
            released(pe, USE["in_b"] + 7 - b)
        wr, wi = (arrived(pe, FIRST["gates"] + x) for x in range(2))
        for d in range(2):
            for j in range(KT):
                at = [((d * 4 + j // 2) * 2 + k) * 256 + P * (j % 2) for k in range(2)]
                dense(USE["gates"] + KT * d + j, [
                    (SEQ * x, SEQ * x + SEQ, [(w[:, at[k]:at[k] + P], uu[:, 2 * (j // 2) + k]) for k in range(2)])
                    for x, w in enumerate((wr, wi))])
        pe.wait_ge(S["lru_h"], 2)
        projection("out_b", "w_out_b", 4, [hs[:, k] for k in range(KT)])
        moe(1)
        ple(1)
        sum_squares()

    def bc(ap, shape):
        for _ in range(len(shape) - len(ap.shape)):
            ap = ap.unsqueeze(len(ap.shape))
        return ap.to_broadcast(shape)

    @block.scalar
    def _(act):
        count = {}

        def signal(ins, name):
            ins.then_inc(S[name], 1)
            count[name] = count.get(name, 0) + 1
            return count[name]

        def after(ins):
            act.wait_ge(S["act_step"], signal(ins, "act_step"))

        def free(ins, use):
            ins.then_inc(S[f"dense_free{use % BANKS}"], 1)

        def full(use):
            act.wait_ge(S["dense_full"], use + 1)

        def root(source, out, scale, sem, name):
            n = source.shape[-1]
            act.wait_ge(S[sem], count.get(sem + "s", 0) + 1)
            count[sem + "s"] = count.get(sem + "s", 0) + 1
            if count.get(name):
                act.wait_ge(S[name], count[name])
            after(act.activation(lnt[:, 0:n], source, ACT.Ln, bias=con("eps"), scale=scale))
            signal(act.activation(out, lnt[:, 0:n], ACT.Exp, scale=-0.5), name)

        def squares(src, waits):
            for i, (sem, value) in enumerate(waits):
                act.wait_ge(S[sem], value)
                signal(act.activation(sq1[:, 2 * i:2 * i + 2], src[:, 2 * i:2 * i + 2], ACT.Square), "sq_ready")
            root(bank[4][:, 0:SEQ], bank[5][:, 0:SEQ], 1.0 / D, "ss_ready", "rstd_ready")

        def uses_free(first):
            return [(f"dense_free{n % BANKS}", n // BANKS + 1) for n in range(first, first + 4)]

        act.dma_start(params[:], t["params"]).then_inc(S["param_load"], 16)
        act.dma_start(consts[:], t["consts"]).then_inc(S["const_load"], 16)
        act.dma_start(ctxT, t["ctx"]).then_inc(S["ctx_load"], 16)
        act.dma_start(hT[:], t["x"]).then_inc(S["x_load"], 16)
        act.dma_start(wk("masks"), t["masks"]).then_inc(S["mask_load"], 16)
        act.wait_ge(S["param_load"], 16)
        act.wait_ge(S["zeroed"], 1)
        signal(act.activation(c_cols[:, :, 0:2], par("c").rearrange("p (k m) -> p k m", k=KT), ACT.Silu), "c_cols")
        signal(act.activation(alog_e, par("a_log"), ACT.Exp), "ab_act")
        act.wait_ge(S["const_load"], 16)
        act.wait_ge(S["ctx_load"], 16)
        act.wait_ge(S["x_load"], 16)
        for i in range(4):
            pair = slice(2 * i, 2 * i + 2)
            act.activation(sq2[:, pair, 0], ctxT[:, pair], ACT.Square)
            signal(act.activation(sq2[:, pair, 1], hT[:, pair], ACT.Square), "sq_ready")
        for m in range(12):
            act.wait_ge(S["ada_mm"], m + 1)
            if m >= 2:
                act.wait_ge(S["ada_mm"], m)
                act.wait_ge(S["ada_sum"], m - 1)
            signal(act.activation(ada_row[:, m % 2], bank[4 + m % 2][:], ACT.Copy), "ada_row")
        root(bank[4][:], bank[5][:], 1.0 / D, "ss_ready", "rstd_ready")
        act.wait_ge(S["ab_mm"], 1)
        signal(act.activation(ab_rows[0:16, :], bank[7][0:16, :], ACT.Copy), "ab_sb")

        for i in range(8):
            released(act, USE["kv"] + i)
            x = (kc if i < 4 else vc)[:, i % 4]
            signal(act.activation(x, x, ACT.Silu), "silu_ready")
        for b in range(2):
            released(act, USE["q"] + b)
            signal(act.activation(qc[:, 2 * b:2 * b + 2], qc[:, 2 * b:2 * b + 2], ACT.Silu), "silu_ready")
        for b in range(2):
            full(USE["z"] + b)
            free(act.activation(wk("zs", 512, 512 * b), bank[(USE["z"] + b) % BANKS][:], ACT.Silu), USE["z"] + b)
        for b in range(2):
            full(USE["u"] + b)
            free(act.activation(wk("oT", 512, 512 * b), bank[(USE["u"] + b) % BANKS][:], ACT.Copy), USE["u"] + b)
        act.wait_ge(S["ab_dve"], 1)
        signal(act.activation(beta, ab[:, :, 0:8], ACT.Sigmoid), "ab_act")
        act.wait_ge(S["ab_dve"], 2)
        signal(act.activation(gtmp[1], gtmp[1], ACT.Exp, scale=-1.0), "ab_act")
        for u in range(4):
            n = USE["vtok"] + u
            full(n)
            free(act.activation(wk("vtok", 512, 512 * u), bank[n % BANKS][:], ACT.Copy), n)
        heads_of = [wk("kc", 512, 512 * h) for h in range(4)] + [wk("qc", 512, 512 * h) for h in range(2)]
        act.wait_ge(S["silu_ready"], 10)
        for a in range(7):
            if a < 6:
                if a >= 2:
                    act.wait_ge(S["qk_ss"], a - 1)
                signal(act.activation(sqk[:, a % 2], heads_of[a], ACT.Square), "qk_sq")
            if a:
                b = a - 1
                if b >= 2:
                    act.wait_ge(S["qk_norm"], b - 1)
                root(bank[4 + b % 2][:], bank[6 + b % 2][:], 1.0, "qk_ss", "qk_rstd")
        for u in range(4):
            n = USE["ktok"] + u
            full(n)
            free(act.activation(wk("ktok", 512, 512 * u), bank[n % BANKS][:], ACT.Copy), n)
        for x in range(2):
            n = USE["dft_w"] + x
            full(n)
            free(act.activation(fo_w[:, x], bank[n % BANKS][:], ACT.Copy), n)
        for x in range(4):
            n = USE["dft_b"] + x
            full(n)
            free(act.activation(fo_b[:, x // 2, x % 2].rearrange("p g e -> p (g e)"), bank[n % BANKS][:], ACT.Copy), n)
        for b in range(2):
            n = USE["dft_y"] + b
            full(n)
            free(act.activation(wk("cat", 512, 512 * b), bank[n % BANKS][:], ACT.Copy), n)

        banks = [[bank[0], bank[1], bank[4], bank[5]], [bank[2], bank[3], bank[6], bank[7]]]

        def by_head(b):
            return b[:].rearrange("p (h t) -> p h t", h=HEADS)

        for n in range(4):
            s = n // 2
            for d in range(2):
                e, last = 2 * n + d, (P - 1 if d == 0 else 0)
                a0 = by_head(banks[d][0])
                act.wait_ge(S["g_diff"], e + 1)
                if s:
                    act.activation(qd[:, d], a0, ACT.Exp)
                act.activation(egl[:, d], a0[:, :, last], ACT.Exp)
                act.activation(egcol[:, d], gcol[:, d], ACT.Exp)
                act.wait_ge(S["g_masked"], e + 1)
                signal(act.activation(decayT[:, d], decayT[:, d], ACT.Exp), "decay")
            for l in range(1, LEVELS):
                for d in range(2):
                    i = 2 * (LEVELS * n + l) + d
                    act.wait_ge(S["lvl_p"], i + 1)
                    signal(act.activation(pmat[:, d], by_head(banks[d][0]), ACT.Copy), "lvl_p_sb")
            for d in range(2):
                act.wait_ge(S["vn_mm"], 2 * n + d + 1)
                signal(act.activation(vnew[:, d], by_head(banks[d][1]), ACT.Copy), "vn_sb")
        act.wait_ge(S["o_ready"], 4)
        for b in range(2):
            signal(act.activation(sqk[:, b], wk("oT", 512, 512 * b), ACT.Square), "o_sq")
        for b in range(2):
            root(bank[4 + b][:], bank[6 + b][:], 1.0 / P, "o_ss", "o_rstd")
        act.dma_start(pT, t["p"]).then_inc(S["p_load"], 16)

        def rows(stage):
            for b in range(4):
                n = USE[stage] + b
                full(n)
                free(act.activation(yT[:, 2 * b:2 * b + 2], bank[n % BANKS][:], ACT.Copy), n)
            squares(yT, uses_free(USE[stage]))

        rows("w_out")
        squares(hT, [("h_ready", 2 * i + 2) for i in range(4)])
        for f in range(FT):
            act.wait_ge(S["ffn_conv"], f + 1)
            signal(act.activation(sgate[:, f % 2], acc[:, f % 4], ACT.Silu), "ffn_silu")
        rows("down")
        squares(hT, [("h_ready", 8 + 2 * i + 2) for i in range(4)])
        for j in range(KT):
            n = USE["in_a"] + 3 * (j // 2) + j % 2
            full(n)
            if j >= 2:
                m = USE["in_a"] + 3 * ((j - 2) // 2) + j % 2
                released(act, m)
            signal(act.activation(c_sb[:, j % 2], bank[n % BANKS][:, 0:SEQ], ACT.Copy), "c_sb")

        def moe(layer):
            squares(hT, uses_free(USE[("out_a", "out_b")[layer]]))
            for m in (0, 2):
                act.wait_ge(S["tok_mm"], 4 * layer + m + 1)
                signal(act.activation(xtok[:, m // 2, 0:512], bank[m][:], ACT.Copy), "tok_sb")
            act.wait_ge(S["lg_mm"], layer + 1)
            signal(act.activation(lgT[0:36, :], bank[7][0:36, 0:SEQ], ACT.Copy), "lg_sb")
            act.wait_ge(S["route_dve"], 2 * layer + 1)
            for u in range(NH):
                last = act.activation(rt(52, 4)[:, u], lg[:, u, 0:4], ACT.Exp, bias=rt(50, 1)[:, u], accum_out=rt(60, 1)[:, u])
            signal(last, "route_act")
            act.wait_ge(S["route_dve"], 2 * layer + 2)
            signal(act.activation(rt(190, 1), rt(188, 1), ACT.Exp), "route_act")

            done, extra = layer * PAIRS, layer * (PAIRS + 1)
            act.wait_ge(S["gather_mm"], extra + 1)
            act.activation(xg[:, 0:4], bank[2][:], ACT.Copy).then_inc(S["xg_act"], 1)
            with act.Fori(0, PAIRS) as i:
                act.wait_ge(S["gate_mm"], i + done + 1)
                act.activation(sg, bank[0][:], ACT.Silu).then_inc(S["sg_sb"], 1)
                act.wait_ge(S["gather_mm"], i + extra + 2)
                act.activation(xg[:, 0:4], bank[2][:], ACT.Copy).then_inc(S["xg_act"], 1)
                act.wait_ge(S["t_mm"], i + done + 1)
                act.activation(hidT, bank[4][:], ACT.Copy).then_inc(S["ht_sb"], 1)
                act.wait_ge(S["down_mm"], i * 2 + 2 * done + 1)
                act.activation(ysb[:, 0:512], bank[6][:], ACT.Copy).then_inc(S["y_act"], 1)
                act.wait_ge(S["pwt_mm"], i + extra + 2)
                act.activation(pwt, bank[4][:, 0:SEQ], ACT.Copy).then_inc(S["pwt_sb"], 1)

            over = act.value_load(flag[0:1, 0:1], min_val=0, max_val=1)
            with act.If(over > 0):
                with act.Fori(0, E) as e:
                    for u in range(NH):
                        act.wait_ge(S[f"ov_gu{layer}"], e * 2 + u + 1)
                        act.activation(sg, bank[0][:], ACT.Silu).then_inc(S[f"ov_sg{layer}"], 1)
                        act.wait_ge(S[f"ov_t{layer}"], e * 2 + u + 1)
                        act.activation(hidT, bank[4][:], ACT.Copy).then_inc(S[f"ov_ht{layer}"], 1)

        def ple(layer):
            squares(hT, [("moe_done", layer + 1)] * 4)
            for b in range(4):
                n = USE[f"ple{layer}"] + 2 * b
                full(n)
                for x in range(2):
                    j = 2 * b + x
                    last = act.activation(gsb[:, j], bank[n % BANKS][:, SEQ * x:SEQ * x + SEQ], ACT.Sigmoid,
                                          bias=par("b_ple", 8 * layer + j, 1))
                free(last, n)

        squares_before = {0: 16, 1: 20}
        moe(0)
        ple(0)
        squares(hT, [("h_ready", 16 + i + 1) for i in range(4)])
        for b in range(4):
            n = USE["in_b"] + b
            full(n)
            free(act.activation(yg[:, 2 * b:2 * b + 2], bank[n % BANKS][:], ACT.Gelu_apprx_tanh), n)
        for d in range(2):
            if d:
                act.wait_ge(S["lru_h"], 1)
            for j in range(KT):
                n = USE["gates"] + KT * d + j
                full(n)
                act.activation(rr[:, j], bank[n % BANKS][:, 0:SEQ], ACT.Sigmoid, bias=par("b_rg", 8 * d + j, 1))
                free(act.activation(ii[:, j], bank[n % BANKS][:, SEQ:512], ACT.Sigmoid, bias=par("b_ig", 8 * d + j, 1)), n)
            if d == 0:
                act.wait_ge(S["lru_log"], 1)
                signal(act.activation(nlt[1], nlt[1], ACT.Exp, scale=-1.0), "lru_exp")
            act.wait_ge(S["lru_log"], 2 + d)
            act.activation(aa[:], rr[:], ACT.Exp)
            signal(act.activation(rr[:], rr[:], ACT.Tanh), "lru_exp")
            act.wait_ge(S["lru_var"], d + 1)
            signal(act.activation(vv[:], vv[:], ACT.Sqrt, scale=-1.0), "lru_sqrt")
        moe(1)
        ple(1)
        squares(hT, [("h_ready", 20 + i + 1) for i in range(4)])

    @block.gpsimd
    def _(pool):
        pool.memset(wk("S", KT * 32), 0.0).then_inc(S["zeroed"], 1)
        pool.wait_ge(S["mask_load"], 16)
        shape = [P, HEADS, P]

        def heads(m):
            return m.unsqueeze(1).to_broadcast(shape)

        for n in range(4):
            s, c = n // 2, n % 2
            for d in range(2):
                e = 2 * n + d
                pool.wait_ge(S["g_diff"], e + 1)
                pool.tensor_tensor(decayT[:, d], decayT[:, d], heads(neg[:, d]), ALU.add).then_inc(S["g_masked"], 1)
            for l in range(LEVELS):
                for d in range(2):
                    e, half, last = 2 * n + d, (c if d == 0 else 1 - c), (P - 1 if d == 0 else 0)
                    u = 2 * s + half
                    if l == 0:
                        pool.wait_ge(S["at_ready"], e + 1)
                    else:
                        pool.wait_ge(S["lvl_p"], 2 * (LEVELS * n + l - 1) + d + 1)
                        if l == 1:
                            pool.wait_ge(S["lvl_t"], 2 * LEVELS * n + d + 1)
                    pool.tensor_tensor(lmask[:, d], amatT[:, d], heads(level[:, l]), ALU.mult).then_inc(S["lvl_mask"], 1)
                    if l == 1:
                        if n < 3:
                            pool.tensor_tensor(kd[:, d], ktok[:, u], bc(decayT[:, d, :, last], shape), ALU.mult)
                        if s:
                            pool.tensor_tensor(qd[:, d], qd[:, d], qc[:, :, P * half:P * half + P], ALU.mult)
                        pool.tensor_tensor(xmat[:, d], vtok[:, u], bc(beta[:, u, 4 * d:4 * d + 4], shape), ALU.mult)\
                            .then_inc(S["g_pool"], 1)
        for layer in range(2):
            done, extra = layer * PAIRS, layer * (PAIRS + 1)
            with pool.Fori(0, PAIRS) as i:
                pool.wait_ge(S["onehot"], i + extra + 1)
                pool.wait_ge(S["pwt_mm"], i + extra + 1)
                for u in range(NH):
                    last = pool.tensor_tensor(onehw[:, u], oneh[:, u], bc(wgt[:, u, bass.ds(i * 2, 2)], [P, 2, SLOTS]), ALU.mult)
                last.then_inc(S["onehot_w"], 1)

    @block.vector
    def _(dve):
        v = nc.vector
        count = {}

        def signal(ins, name):
            ins.then_inc(S[name], 1)
            count[name] = count.get(name, 0) + 1
            return count[name]

        def after(ins):
            dve.wait_ge(S["dve_step"], signal(ins, "dve_step"))

        def free(ins, use):
            ins.then_inc(S[f"dense_free{use % BANKS}"], 1)

        def full(use):
            dve.wait_ge(S["dense_full"], use + 1)
            return bank[use % BANKS]

        rstd = bank[5][:, 0:SEQ]

        def roots():
            count["roots"] = count.get("roots", 0) + 1
            dve.wait_ge(S["rstd_ready"], count["roots"])

        def scaled(src, gain, shift=None, out=None):
            roots()
            out = xnT if out is None else out
            for k in range(KT):
                ins = v.scalar_tensor_tensor(out[:, k], src[:, k], gain(k), rstd, ALU.mult, ALU.mult)
                if shift is None:
                    signal(ins, "xn_ready")
                else:
                    signal(ins, "dve_step")
                    if k:
                        dve.wait_ge(S["dve_step"], count["dve_step"] - 1)
                        signal(v.tensor_scalar(out[:, k - 1], out[:, k - 1], shift(k - 1), None, ALU.add), "xn_ready")
            if shift is not None:
                dve.wait_ge(S["dve_step"], count["dve_step"])
                signal(v.tensor_scalar(out[:, KT - 1], out[:, KT - 1], shift(KT - 1), None, ALU.add), "xn_ready")

        def residual(gain):
            roots()
            for k in range(KT + 1):
                if k < KT:
                    signal(v.scalar_tensor_tensor(tmp[:, k % 4], yT[:, k], gain(k), rstd, ALU.mult, ALU.mult), "dve_step")
                if k:
                    dve.wait_ge(S["dve_step"], count["dve_step"] - (1 if k < KT else 0))
                    signal(v.tensor_tensor(hT[:, k - 1], hT[:, k - 1], tmp[:, (k - 1) % 4], ALU.add), "h_ready")

        def log1p(z, e, scratch):
            a, b = scratch
            after(v.tensor_scalar(a, e, 2.0, None, ALU.add))
            after(v.reciprocal(b, a))
            after(v.tensor_tensor(z, e, b, ALU.mult))
            after(v.tensor_tensor(a, z, z, ALU.mult))
            after(v.tensor_scalar(b, a, LOG1P[7], None, ALU.mult))
            for coefficient in LOG1P[6:0:-1]:
                after(v.scalar_tensor_tensor(b, b, coefficient, a, ALU.add, ALU.mult))
            after(v.scalar_tensor_tensor(z, b, 1.0, z, ALU.add, ALU.mult))
            after(v.tensor_scalar(z, z, 2.0, None, ALU.mult))

        dve.wait_ge(S["param_load"], 16)
        dve.wait_ge(S["ada_sum"], 12)
        after(v.tensor_tensor(mod[:], bank[6][:, 0:96].rearrange("p (k m) -> p k m", k=48), bc(par("b_ada"), [P, 48, 2]), ALU.add))
        for i, (tile, m, g) in enumerate(((8, 1, "g_pre_mix"), (8, 0, "g_pre_mix"), (32, 0, "g_pre_ffn"))):
            v.scalar_tensor_tensor(gains[:, i], mod[:, tile:tile + 8, m], 1.0, par(g), ALU.add, ALU.mult)
        v.tensor_tensor(gains[:, 3], mod[:, 16:24, 0], par("g_post_mix"), ALU.mult)
        after(v.tensor_tensor(gains[:, 4], mod[:, 40:48, 0], par("g_post_ffn"), ALU.mult))

        roots()
        dve.wait_ge(S["ctx_load"], 16)
        dve.wait_ge(S["x_load"], 16)
        for k in range(KT):
            for s, src in enumerate((ctxT, hT)):
                ins = v.scalar_tensor_tensor(xn[:, k, s], src[:, k], gains[:, s, k:k + 1], bank[5][:, SEQ * s:SEQ * s + SEQ],
                                             ALU.mult, ALU.mult)
            after(ins)
            for s in range(2):
                ins = v.tensor_scalar(xn[:, k, s], xn[:, k, s], mod[:, k, 1 - s:2 - s], None, ALU.add)
            signal(ins, "xn_ready")

        def conv3(n, out, x, w):
            after(v.tensor_scalar(out, x, w(1), None, ALU.mult))
            a, b = slice(0, SEQ - 1), slice(1, SEQ)
            after(v.scalar_tensor_tensor(out[..., b], x[..., a], w(0), out[..., b], ALU.mult, ALU.add))
            ins = v.scalar_tensor_tensor(out[..., a], x[..., b], w(2), out[..., a], ALU.mult, ALU.add)
            return ins

        def conv_w(tile):
            return lambda j: par("conv", 3 * tile + j, 1)

        for i in range(8):
            n = USE["kv"] + i
            b = full(n)
            free(conv3(n, (kc if i < 4 else vc)[:, i % 4], b[:].rearrange("p (s t) -> p s t", s=2), conv_w(4 + i)), n)
            if i == 7:
                dve.wait_ge(S["ab_cols"], 1)
                signal(v.tensor_copy(ab, bank[6][:, 0:64].rearrange("p (u c) -> p u c", u=4)), "ab_dve")
                dve.wait_ge(S["ab_dve"], 1)
                after(v.tensor_tensor(gtmp[0], ab[:, :, 8:16], par("dt_bias").unsqueeze(1).to_broadcast([P, 4, 8]), ALU.add))
                signal(v.scalar_tensor_tensor(gtmp[1], gtmp[0], -1.0, gtmp[0], ALU.mult, ALU.max), "ab_dve")
        for b in range(2):
            n = USE["q"] + b
            x = full(n)
            for i in range(2):
                ins = conv3(n, qc[:, 2 * b + i], x[:, SEQ * i:SEQ * i + SEQ], conv_w(2 * b + i))
            free(ins, n)
        dve.wait_ge(S["ab_act"], 3)
        log1p(gtmp[2], gtmp[1], gtmp[3:5])
        after(v.scalar_tensor_tensor(gtmp[0], gtmp[0], 0.0, gtmp[2], ALU.max, ALU.add))
        signal(v.scalar_tensor_tensor(glog, gtmp[0], -1.0, alog_e.unsqueeze(1).to_broadcast([P, 4, 8]), ALU.mult, ALU.mult),
               "gates_ready")
        for a in range(6):
            dve.wait_ge(S["qk_rstd"], a + 1)
            r = bank[6 + a % 2][:]
            x = wk("kc", 512, 512 * a) if a < 4 else wk("qc", 512, 512 * (a - 4))
            signal(v.scalar_tensor_tensor(x, x, 1.0 if a < 4 else float(P) ** -0.5, r, ALU.mult, ALU.mult), "qk_norm")

        banks = [[bank[0], bank[1], bank[4], bank[5]], [bank[2], bank[3], bank[6], bank[7]]]
        shape = [P, HEADS, P]

        def by_head(b):
            return b[:].rearrange("p (h t) -> p h t", h=HEADS)

        eye = ident.unsqueeze(1).to_broadcast(shape)
        for n in range(4):
            s, c = n // 2, n % 2
            for d in range(2):
                e = 2 * n + d
                a0, a1, a2, a3 = banks[d]
                dve.wait_ge(S["g_rows"], e + 1)
                after(v.tensor_copy(gcol[:, d], a3[:, 0:HEADS]))
                signal(v.tensor_tensor(decayT[:, d], by_head(a0), bc(gcol[:, d], shape), ALU.subtract), "g_diff")
            for d in range(2):
                e, half = 2 * n + d, (c if d == 0 else 1 - c)
                u = 2 * s + half
                a0, a1, a2, a3 = banks[d]
                dve.wait_ge(S["decay"], e + 1)
                after(v.tensor_tensor(amatT[:, d], by_head(a2), decayT[:, d], ALU.mult))
                signal(v.tensor_tensor(amatT[:, d], amatT[:, d], by_head(a1), ALU.mult), "at_ready")
                signal(v.tensor_tensor(begc[:, d], beta[:, u, 4 * d:4 * d + 4], egcol[:, d], ALU.mult), "dve_step")
                if s:
                    dve.wait_ge(S["qk_mm"], e - 3)
                    v.tensor_tensor(attnT[:, d], by_head(a3), decayT[:, d], ALU.mult)
            for l in range(LEVELS):
                for d in range(2):
                    a0, a1, a2, a3 = banks[d]
                    i = 2 * (LEVELS * n + l) + d
                    if l == 0:
                        dve.wait_ge(S["lvl_p"], i + 1)
                        v.tensor_tensor(tinv[:, d], eye, by_head(a0), ALU.subtract)
                        signal(v.tensor_tensor(tinvT[:, d], eye, lmask[:, d], ALU.subtract), "lvl_t")
                    else:
                        dve.wait_ge(S["lvl_tp"], 2 * ((LEVELS - 1) * n + l - 1) + d + 1)
                        dve.wait_ge(S["lvl_t"], i - 1)
                        if l < LEVELS - 1:
                            v.tensor_tensor(tinv[:, d], tinv[:, d], by_head(a1), ALU.subtract)
                        signal(v.tensor_tensor(tinvT[:, d], tinvT[:, d], by_head(a2), ALU.subtract), "lvl_t")
            for d in range(2):
                a0 = banks[d][0]
                if n:
                    dve.wait_ge(S["ks_mm"], 2 * (n - 1) + d + 1)
                    dve.wait_ge(S["g_pool"], 2 * n + d + 1)
                    dve.wait_ge(S["dve_step"], count["dve_step"])
                    after(v.tensor_tensor(pmat[:, d], by_head(a0), bc(begc[:, d], shape), ALU.mult))
                    signal(v.tensor_tensor(xmat[:, d], xmat[:, d], pmat[:, d], ALU.subtract), "x_ready")
            for d in range(2):
                e, half = 2 * n + d, (c if d == 0 else 1 - c)
                a2, a3 = banks[d][2:]
                if s:
                    dve.wait_ge(S["o_mm"], 2 * (n - 2) + d + 1)
                    out = oT[:, :, P * half:P * half + P]
                    if c == 0:
                        signal(v.tensor_copy(out, by_head(a2)), "o_ready")
                    else:
                        dve.wait_ge(S["o_ready"], 2)
                        signal(v.tensor_tensor(out, out, by_head(a2), ALU.add), "o_ready")
                if n < 3:
                    dve.wait_ge(S["ds_mm"], e + 1)
                    if n == 0:
                        signal(v.tensor_copy(state[:, d], by_head(a3)), "s_ready")
                    else:
                        after(v.tensor_tensor(pmat[:, d], state[:, d], bc(egl[:, d], shape), ALU.mult))
                        signal(v.tensor_tensor(state[:, d], pmat[:, d], by_head(a3), ALU.add), "s_ready")

        for b in range(2):
            dve.wait_ge(S["o_rstd"], b + 1)
            o = wk("oT", 512, 512 * b)
            after(v.scalar_tensor_tensor(o, o, par("g_gdn"), bank[6 + b][:], ALU.mult, ALU.mult))
            for i in range(2):
                h = 2 * b + i
                signal(v.tensor_tensor(cat[:, 4 + h], oT[:, h], zs[:, h], ALU.mult), "cat_ready")

        residual(lambda k: gains[:, 3, k:k + 1])
        scaled(hT, lambda k: gains[:, 2, k:k + 1], lambda k: mod[:, 24 + k, 0:1])

        def gated(f):
            n = USE["up"] + f
            dve.wait_ge(S["ffn_silu"], f + 1)
            free(v.tensor_tensor(prod[:, f], bank[n % BANKS][:, 0:SEQ], sgate[:, f % 2], ALU.mult), n)

        for f in range(FT):
            x = full(USE["up"] + f)[:, SEQ:2 * SEQ].rearrange("p (r c) -> p r c", r=ROWS)
            o = acc[:, f % 4].rearrange("p (r c) -> p r c", r=ROWS)
            if f >= 2:
                pass
            after(v.tensor_scalar(o, x, par("w_dwc", 9 * f + 4, 1), None, ALU.mult))
            taps = [(dy, dx) for dy in (-1, 0, 1) for dx in (-1, 0, 1) if (dy, dx) != (0, 0)]
            for dy, dx in taps:
                r0, r1, c0, c1 = max(0, -dy), ROWS - max(0, dy), max(0, -dx), GRID_W - max(0, dx)
                dst = o[:, r0:r1, c0:c1]
                ins = v.scalar_tensor_tensor(dst, x[:, r0 + dy:r1 + dy, c0 + dx:c1 + dx],
                                             par("w_dwc", 9 * f + 3 * (dy + 1) + dx + 1, 1), dst, ALU.mult, ALU.add)
                if (dy, dx) == taps[-1]:
                    signal(ins, "ffn_conv")
                else:
                    after(ins)
            if f:
                gated(f - 1)
        gated(FT - 1)
        residual(lambda k: gains[:, 4, k:k + 1])

        scaled(hT, lambda k: par("norm_mix", k, 1))
        for j in range(KT):
            n = USE["in_a"] + 3 * (j // 2) + j % 2
            x = full(n)
            dve.wait_ge(S["c_sb"], j + 1)
            ins = v.tensor_tensor(ch[:, j % 2], c_sb[:, j % 2], x[:, SEQ:2 * SEQ], ALU.mult)
            free(ins, n)
            released(dve, n)
            after(conv3(None, cu[:, j % 4], ch[:, j % 2], lambda i: par("conv_a", 3 * j + i, 1)))
            if j % 2:
                n = USE["in_a"] + 3 * (j // 2) + 2
                x = full(n)
                for i in range(2):
                    m = j - 1 + i
                    ins = v.tensor_tensor(yT[:, m], x[:, SEQ * i:SEQ * i + SEQ], cu[:, m % 4], ALU.mult)
                free(ins, n)

        def add_output(stage):
            for b in range(4):
                n = USE[stage] + b
                x = full(n)
                pair = slice(2 * b, 2 * b + 2)
                free(v.tensor_tensor(hT[:, pair], hT[:, pair], x[:].rearrange("p (k t) -> p k t", k=2), ALU.add), n)

        add_output("out_a")

        def moe(layer):
            done, extra = layer * PAIRS, layer * (PAIRS + 1)
            scaled(hT, lambda k: par("norm_ffn", 8 * layer + k, 1))
            for m in (1, 3):
                dve.wait_ge(S["tok_mm"], 4 * layer + m + 1)
                signal(v.tensor_copy(xtok[:, m // 2, 512:1024], bank[m][:]), "tok_sb2")
            signal(v.memset(ysb[:, 0:512], 0.0), "y_act")
            signal(v.memset(ysb[:, 512:1024], 0.0), "y_dve")
            signal(v.memset(pwt, 0.0), "pwt_sb")
            v.memset(rt(0, 8), -3e38)
            v.memset(wgt, 0.0)
            after(v.memset(rankm, -1.0))
            iota = con("iota")
            dve.wait_ge(S["lg_cols"], layer + 1)
            bias = par("b_router", 36 * layer, 36).unsqueeze(1).to_broadcast([P, NH, 36])
            after(v.tensor_tensor(lg, bank[6][:, 0:72].rearrange("p (u c) -> p u c", u=NH), bias, ALU.add))
            g8, gm, gi, oneg, let, les, em, ei = (rt(a, n) for a, n in (
                (0, 8), (16, 8), (32, 8), (64, 4), (72, 32), (136, 8), (152, 8), (168, 8)))
            after(v.tensor_copy(g8[:, :, 0:N_GROUPS], lg[:, :, 0:N_GROUPS]))
            for u in range(NH):
                last = v.max(gm[:, u], g8[:, u])
            after(last)
            signal(v.tensor_scalar(rt(50, 1), gm[:, :, 0:1], -1.0, None, ALU.mult), "route_dve")
            for u in range(NH):
                last = v.max_index(gi[:, u].bitcast(U32), gm[:, u], g8[:, u])
            after(last)
            gif = rt(48, 1)
            after(v.tensor_copy(gif, gi.bitcast(U32)[:, :, 0:1]))
            after(v.tensor_tensor(oneg, iota[:, 0:N_GROUPS].unsqueeze(1).to_broadcast([P, NH, N_GROUPS]),
                                  gif.to_broadcast([P, NH, N_GROUPS]), ALU.is_equal))
            for u in range(NH):
                last = v.tensor_tensor(let[:, u].rearrange("p (e g) -> p e g", g=N_GROUPS),
                                       lg[:, u, N_GROUPS:].rearrange("p (g e) -> p e g", g=N_GROUPS),
                                       oneg[:, u].unsqueeze(1).to_broadcast([P, PER_GROUP, N_GROUPS]), ALU.mult)
            after(last)
            after(v.reduce_sum(les, let.rearrange("p u (e g) -> p u e g", g=N_GROUPS), axis=AX))
            for u in range(NH):
                last = v.max(em[:, u], les[:, u])
            after(last)
            signal(v.tensor_tensor(rt(188, 1), em[:, :, 1:2], em[:, :, 0:1], ALU.subtract), "route_dve")
            for u in range(NH):
                last = v.max_index(ei[:, u].bitcast(U32), em[:, u], les[:, u])
            after(last)
            eif = rt(184, 2)
            after(v.tensor_copy(eif, ei.bitcast(U32)[:, :, 0:2]))
            picked = rt(200, 2)
            after(v.scalar_tensor_tensor(picked, gif.to_broadcast([P, NH, 2]), float(PER_GROUP), eif, ALU.mult, ALU.add))
            m1, m2, m12 = rt(304, E), rt(368, E), rt(240, E)
            for i, m in enumerate((m1, m2)):
                last = v.tensor_tensor(m, iota[:, 0:E].unsqueeze(1).to_broadcast([P, NH, E]),
                                       picked[:, :, i:i + 1].to_broadcast([P, NH, E]), ALU.is_equal)
            after(last)
            signal(v.tensor_tensor(m12, m1, m2, ALU.add), "mask_ready")
            dve.wait_ge(S["route_act"], 2 * layer + 2)
            v.reciprocal(rt(62, 1), rt(60, 1))
            after(v.tensor_scalar(rt(192, 1), rt(190, 1), 1.0, None, ALU.add))
            after(v.reciprocal(rt(194, 1), rt(192, 1)))
            after(v.tensor_tensor(rt(196, 1), rt(194, 1), rt(62, 1), ALU.mult))
            after(v.tensor_tensor(rt(198, 1), rt(196, 1), rt(190, 1), ALU.mult))
            v.tensor_tensor(m1, m1, rt(196, 1).to_broadcast([P, NH, E]), ALU.mult)
            after(v.tensor_tensor(m2, m2, rt(198, 1).to_broadcast([P, NH, E]), ALU.mult))
            after(v.tensor_tensor(wgt[:, :, 0:E], m1, m2, ALU.add))
            dve.wait_ge(S["rank_mm"], layer + 1)
            ranks = bank[5][:, 0:2 * E].rearrange("p (u e) -> p u e", u=NH)
            after(v.scalar_tensor_tensor(rankm[:, :, 0:E], ranks, 1.0, m12, ALU.add, ALU.mult))
            after(v.tensor_scalar(rankm[:, :, 0:E], rankm[:, :, 0:E], -1.0, None, ALU.add))
            after(v.reduce_max(rt(496, 1)[:, 0], bank[5][:, 2 * E:3 * E], axis=AX))
            after(v.scalar_tensor_tensor(wov, rankm[:, :, 0:E], float(SLOTS), wgt[:, :, 0:E], ALU.is_ge, ALU.mult))
            signal(v.tensor_scalar(flag[:], rt(496, 1)[:, 0], float(SLOTS), None, ALU.is_gt), "route_ready")
            signal(v.memset(rt(600, 1), 0.0), "scat_add")
            signal(v.memset(rt(602, 1), 0.0), "pwt_mm")

            def select(pair):
                for u in range(NH):
                    last = v.tensor_tensor(oneh[:, u], iota.unsqueeze(1).to_broadcast([P, 2, SLOTS]),
                                           bc(rankm[:, u, bass.ds(pair * 2, 2)], [P, 2, SLOTS]), ALU.is_equal)
                last.then_inc(S["onehot"], 1)

            def take():
                v.tensor_copy(xg[:, 4:8], bank[3][:].rearrange("p (k s) -> p k s", k=4)).then_inc(S["xg_dve"], 1)

            def add(i):
                base = layer * (4 * PAIRS + 5) + 1
                dve.wait_ge(S["scat_add"], i * 4 + base)
                for q in range(4):
                    dve.wait_ge(S["scat_mm"], i * 4 + layer * (4 * PAIRS + 4) + q + 1)
                    pair = slice(2 * q, 2 * q + 2)
                    v.tensor_tensor(hT[:, pair], hT[:, pair], bank[(5, 2, 3, 5)[q]][:].rearrange("p (k t) -> p k t", k=2), ALU.add)\
                        .then_inc(S["scat_add"], 1)

            select(0)
            dve.wait_ge(S["gather_mm"], extra + 1)
            take()
            with dve.Fori(0, PAIRS) as i:
                dve.wait_ge(S["gather_mm"], i + extra + 1)
                dve.wait_ge(S["onehot_w"], i + done + 1)
                select(i + 1)
                dve.wait_ge(S["sg_sb"], i + done + 1)
                dve.wait_ge(S["up_mm"], i + done + 1)
                v.tensor_tensor(hh, sg, bank[1][:], ALU.mult).then_inc(S["hh_sb"], 1)
                dve.wait_ge(S["gather_mm"], i + extra + 2)
                take()
                add(i)
                dve.wait_ge(S["down_mm"], i * 2 + 2 * done + 2)
                v.tensor_copy(ysb[:, 512:1024], bank[7][:]).then_inc(S["y_dve"], 1)
            add(PAIRS)
            dve.wait_ge(S["scat_add"], (layer + 1) * (4 * PAIRS + 5))

            over = dve.value_load(flag[0:1, 0:1], min_val=0, max_val=1)
            with dve.If(over > 0):
                v.memset(rt(604, 1), 0.0).then_inc(S[f"ov_down{layer}"], 1)
                v.memset(rt(606, 1), 0.0).then_inc(S[f"ov_add{layer}"], 1)
                with dve.Fori(0, E) as e:
                    for u in range(NH):
                        dve.wait_ge(S[f"ov_sg{layer}"], e * 2 + u + 1)
                        v.scalar_tensor_tensor(hh, sg, wov[:, u, bass.ds(e, 1)], bank[1][:], ALU.mult, ALU.mult)\
                            .then_inc(S[f"ov_hh{layer}"], 1)
                        dve.wait_ge(S[f"ov_down{layer}"], e * 2 + u + 2)
                        dve.wait_ge(S[f"ov_add{layer}"], e * 2 + u + 1)
                        for b in range(2):
                            x = hT[:, 4 * b:4 * b + 4, P * u:P * u + P]
                            last = v.tensor_tensor(x, x, bank[6 + b][:].rearrange("p (k t) -> p k t", k=4), ALU.add)
                        last.then_inc(S[f"ov_add{layer}"], 1)
                dve.wait_ge(S[f"ov_add{layer}"], 2 * E + 1)
                v.memset(rt(608, 1), 0.0)
            v.memset(rt(610, 1), 0.0).then_inc(S["moe_done"], 1)

        def ple(layer):
            scaled(hT, lambda k: par("norm_ple", 8 * layer + k, 1))
            for b in range(4):
                n = USE[f"ple{layer}"] + 2 * b
                x = full(n + 1)
                released(dve, n)
                pair = slice(2 * b, 2 * b + 2)
                g = gsb[:, pair]
                free(v.tensor_tensor(g, g, x[:].rearrange("p (k t) -> p k t", k=2), ALU.mult), n + 1)
                released(dve, n + 1)
                signal(v.tensor_tensor(hT[:, pair], hT[:, pair], g, ALU.add), "h_ready")

        moe(0)
        ple(0)

        scaled(hT, lambda k: par("norm_mix", 8 + k, 1))
        x = par("lam")
        signal(v.scalar_tensor_tensor(nlt[1], x, -1.0, x, ALU.mult, ALU.max), "lru_log")
        for b in range(4):
            n = USE["in_b"] + 4 + b
            p = full(n)
            for i in range(2):
                j = 2 * b + i
                x, o = p[:, SEQ * i:SEQ * i + SEQ], uu[:, j]
                after(v.tensor_scalar(o, x, par("conv_b", 4 * j + 2, 1), par("conv_bias", j, 1), ALU.mult, ALU.add))
                after(v.scalar_tensor_tensor(o[:, 1:], x[:, :SEQ - 1], par("conv_b", 4 * j + 1, 1), o[:, 1:], ALU.mult, ALU.add))
                after(v.scalar_tensor_tensor(o[:, 2:], x[:, :SEQ - 2], par("conv_b", 4 * j, 1), o[:, 2:], ALU.mult, ALU.add))
                last = v.scalar_tensor_tensor(o[:, :SEQ - 1], x[:, 1:], par("conv_b", 4 * j + 3, 1), o[:, :SEQ - 1], ALU.mult, ALU.add)
            free(last, n)
        dve.wait_ge(S["lru_exp"], 1)
        log1p(nlt[2], nlt[1], nlt[3:5])
        after(v.tensor_scalar(nlt[0], par("lam"), -1.0, 0.0, ALU.mult, ALU.max))
        after(v.tensor_tensor(nlt[0], nlt[0], nlt[2], ALU.add))
        after(v.tensor_scalar(nls, nlt[0], -RG_C, None, ALU.mult))
        for d in range(2):
            for b in range(BANKS):
                released(dve, USE["gates"] + KT * d + KT - 1 - b)
            for j in range(KT):
                last = v.tensor_scalar(rr[:, j], rr[:, j], nls[:, 8 * d + j:8 * d + j + 1], None, ALU.mult)
            signal(last, "lru_log")
            v.tensor_tensor(ii[:], ii[:], uu[:], ALU.mult)
            dve.wait_ge(S["lru_exp"], 2 + d)
            after(v.tensor_tensor(vv[:], aa[:], aa[:], ALU.mult))
            signal(v.scalar_tensor_tensor(vv[:], vv[:], 1.0, rr[:], ALU.add, ALU.mult), "lru_var")
            dve.wait_ge(S["lru_sqrt"], d + 1)
            after(v.tensor_tensor(vv[:], vv[:], ii[:], ALU.mult))
            way = slice(None) if d == 0 else slice(None, None, -1)
            for j in range(KT):
                last = v.tensor_tensor_scan((hs if d == 0 else hb)[:, j, way], aa[:, j, way], vv[:, j, way], 0.0, ALU.mult, ALU.add)
            if d == 0:
                signal(last, "lru_h")
            else:
                after(last)
        after(v.tensor_tensor(hs[:], hs[:], hb, ALU.add))
        signal(v.tensor_tensor(hs[:], hs[:], yg[:], ALU.mult), "lru_h")
        add_output("out_b")
        moe(1)
        ple(1)
        roots()
        for k in range(KT):
            last = v.scalar_tensor_tensor(yT[:, k], hT[:, k], par("norm_final", k, 1), rstd, ALU.mult, ALU.mult)
        signal(last, "fin_ready")

    ctx_block.__exit__(None, None, None)


def tiles(w):
    k, n = w.shape
    return np.ascontiguousarray(w.reshape(k // P, P, n).transpose(1, 0, 2))


def columns(v):
    v = v.reshape(-1, P)
    return np.ascontiguousarray(v.T)


def constants():
    i = np.arange(P)
    sel = np.zeros((P, 2), np.float32)
    for j in range(4):
        sel[32 * j, 0] = sel[32 * j + 1, 1] = 1.0
    parts = {
        "ident": np.eye(P), "upper": np.triu(np.ones((P, P))), "lower": np.tril(np.ones((P, P))),
        "strict": np.triu(np.ones((P, P)), 1), "ones": np.ones((P, P)), "sel": sel,
        "iota": np.broadcast_to(np.arange(SLOTS), (P, SLOTS)), "eps": np.full((P, 1), EPS),
    }
    consts = np.concatenate([parts[n].reshape(P, -1) for n in CONSTS], 1).astype(np.float32)
    neg = np.stack([np.where(i[None, :] >= i[:, None], 0.0, NEG), np.where(i[None, :] <= i[:, None], 0.0, NEG)], 1)
    level = []
    for l in range(LEVELS):
        size = 1 << l
        b = i // size
        level.append((b[:, None] // 2 == b[None, :] // 2) & (b[:, None] != b[None, :]))
    masks = np.concatenate([neg.reshape(P, -1), np.stack(level, 1).reshape(P, -1)], 1).astype(np.float32)
    c = 2 * np.pi * np.outer(i, i) / P
    l = 2 * np.pi * np.outer(np.arange(SEQ), np.arange(SEQ)) / SEQ
    norm = 1.0 / math.sqrt(P * SEQ)
    dft = {"cos_c": np.cos(c), "nsin_c": -np.sin(c), "cos_l": tiles(np.cos(l) * norm), "sin_l": tiles(np.sin(l) * norm)}
    return consts, masks, {k: v.reshape(P, -1).astype(np.float32) for k, v in dft.items()}


_ORDER = ["x", "ctx", "p", "params", "consts", "masks", "dense", "w_gate", "w_up", "w_down"]


def kernel(**inputs):
    import concourse.bacc as bacc
    from concourse.bass_utils import run_bass_kernel_spmd

    a = {k: np.asarray(v) for k, v in inputs.items()}
    consts, masks, dft = constants()
    each = lambda v: np.broadcast_to(v.reshape(1, -1), (P, v.size))
    w_in, conv = a["w_in"][0], a["w_qkv_conv"][0]
    both = np.stack([a["c"][0], a["c_ctx"]], 1)
    parts = {
        "c": tiles(both), "b_ada": columns(a["b_ada"]), "g_pre_mix": columns(a["g_pre_mix"]),
        "g_post_mix": columns(a["g_post_mix"]), "g_pre_ffn": columns(a["g_pre_ffn"]),
        "g_post_ffn": columns(a["g_post_ffn"]), "w_ab": tiles(w_in[:, 2560:]),
        "conv": conv.reshape(3, 12, P).transpose(2, 1, 0), "a_log": each(a["a_log"]), "dt_bias": each(a["dt_bias"]),
        "g_gdn": columns(a["g_gdn"]), "w_dwc": a["w_dwc"].reshape(9, FT, P).transpose(2, 1, 0),
        "norm_mix": columns(a["norm_mix_2"]), "conv_a": a["conv_a_2"].reshape(3, KT, P).transpose(2, 1, 0),
        "conv_b": a["conv_b_2"].reshape(4, KT, P).transpose(2, 1, 0), "conv_bias": columns(a["conv_bias_b_2"]),
        "b_rg": columns(a["b_rgate_b_2"]), "b_ig": columns(a["b_igate_b_2"]), "lam": columns(a["lam_b_2"]),
        "norm_ffn": columns(a["norm_ffn_2"]), "norm_ple": columns(a["norm_ple_2"]), "b_ple": columns(a["b_ple_gate_2"]),
        "norm_final": columns(a["norm_final_2"]),
        "w_router": np.stack([tiles(np.concatenate([a["w_router_group_2"][l], a["w_router_expert_2"][l]], 1))
                              for l in range(2)], 1),
        "b_router": each(np.concatenate([a["b_router_group_2"], a["b_router_expert_2"]], 1)),
    }
    params = np.concatenate([parts[n].reshape(P, -1) for n in PARAMS], 1)
    assert params.shape == (P, PARAMS_N) and consts.shape == (P, CONSTS_N) and masks.shape == (P, MASKS_N)
    dft["w_f"] = a["w_fourier"][0].transpose(1, 0, 2).reshape(P, -1)

    def chunks(w, width=512):
        return [tiles(w[:, n:n + width]).reshape(P, -1) for n in range(0, w.shape[1], width)]

    def tile_order(w, order):
        return np.concatenate([w[:, P * i:P * i + P] for i in order], 1)

    up_order = [i for f in range(FT) for i in (f, FT + f)]
    a_order = [i for j in range(0, KT, 2) for i in (KT + j, 2 * KT + j, KT + j + 1, 2 * KT + j + 1, j, j + 1)]
    gate_w = [a[n][0].reshape(8, 2, P, 256).transpose(2, 0, 1, 3).reshape(P, -1) for n in ("w_rgate_b_2", "w_igate_b_2")]
    dense = chunks(a["w_ada"][0])
    dense += [c for n in (1024, 1536, 512, 2048, 0) for c in chunks(w_in[:, n:n + 512])]
    dense += [np.concatenate([dft[n] for n in FOURIER], 1)]
    dense += chunks(a["w_out"][0]) + chunks(tile_order(a["w_up"][0], up_order)) + chunks(a["w_down"][0], P)
    dense += chunks(tile_order(a["w_in_a_2"][0], a_order)) + chunks(a["w_out_a_2"][0])
    dense += chunks(a["w_ple_gate_2"][0]) + chunks(a["w_ple_2"][0], D)
    dense += chunks(a["w_in_b_2"][0]) + gate_w + chunks(a["w_out_b_2"][0])
    dense += chunks(a["w_ple_gate_2"][1]) + chunks(a["w_ple_2"][1], D)
    stream = np.zeros((len(dense), P, CHUNK), np.float32)
    for i, c in enumerate(dense):
        stream[i, :, :c.shape[1]] = c

    arrays = {
        "x": tiles(a["x"][0].T), "ctx": tiles(a["ctx"][0].T),
        "p": np.ascontiguousarray(np.stack([tiles(a["p_2"][l, 0].T) for l in range(2)], 1)),
        "params": np.ascontiguousarray(params), "consts": consts, "masks": masks, "dense": stream,
        "w_gate": a["w_exp_gate_2"], "w_up": a["w_exp_up_2"], "w_down": a["w_exp_down_2"],
    }
    nc = bacc.Bacc("TRN2", target_bir_lowering=False, num_devices=1)
    t = {n: nc.dram_tensor(f"in_{n}", list(arrays[n].shape), F32, kind="ExternalInput").ap() for n in _ORDER}
    t["out"] = nc.dram_tensor("out", [P, KT, SEQ], F32, kind="ExternalOutput").ap()
    build(nc, t)
    r = run_bass_kernel_spmd(nc, [{f"in_{n}": arrays[n] for n in _ORDER}], core_ids=[0])
    out = np.asarray(r.results[0]["out"])
    return np.ascontiguousarray(out.transpose(1, 0, 2).reshape(D, SEQ).T)[None]
```

```python
import math

import numpy as np
import concourse.bass as bass
from concourse import mybir

F32 = mybir.dt.float32
I32 = mybir.dt.int32
U32 = mybir.dt.uint32
ALU = mybir.AluOpType
ACT = mybir.ActivationFunctionType
AX = mybir.AxisListType.X

P = 128
D = 1024
KT = D // P
SEQ = 256
NH = SEQ // P
HEADS = 4
DFF = 2816
FT = DFF // P
GRID_W = 64
ROWS = SEQ // GRID_W
EPS = 1e-6
RG_C = 8.0
N_GROUPS = 4
PER_GROUP = 8
E = N_GROUPS * PER_GROUP
DE = 512
SLOTS = 64
PAIRS = E // 2
RING = 6
CHUNK = 4096
LEVELS = 7
NEG = -1e30
LN_EXP, SILU, SIGMOID, GELU, EXP, SQRT = (
    f"{n}_and_others" for n in ("natural_log_exp", "silu", "sigmoid", "gelu_apprx_tanh", "exp", "sqrt"))
BANKS = 4
LOG1P = [1.0 / (2 * i + 1) for i in range(8)]


def layout(items):
    at, out = 0, {}
    for name, n in items:
        out[name] = (at, n)
        at += n
    return out, at


PARAMS, PARAMS_N = layout([
    ("c", 16), ("b_ada", 48), ("g_pre_mix", 8), ("g_post_mix", 8), ("g_pre_ffn", 8), ("g_post_ffn", 8),
    ("w_ab", KT * 16), ("conv", 12 * 3), ("a_log", 8), ("dt_bias", 8), ("g_gdn", 1), ("w_dwc", FT * 9),
    ("norm_mix", 16), ("conv_a", 8 * 3), ("conv_b", 8 * 4), ("conv_bias", 8), ("b_rg", 16), ("b_ig", 16),
    ("lam", 16), ("norm_ffn", 16), ("norm_ple", 16), ("b_ple", 16), ("norm_final", 8),
    ("w_router", 2 * KT * 36), ("b_router", 2 * 36),
])
CONSTS, CONSTS_N = layout([
    ("ident", P), ("upper", P), ("lower", P), ("strict", P), ("ones", P), ("sel", P), ("iota", SLOTS), ("eps", 1),
])
MASKS, MASKS_N = layout([("neg", 2 * P), ("level", LEVELS * P)])
FOURIER, FOURIER_N = layout([("cos_c", P), ("nsin_c", P), ("w_f", 4 * P), ("cos_l", 2 * SEQ), ("sin_l", 2 * SEQ)])

DENSE = [("ada0", 4, CHUNK), ("w_in", 5, CHUNK), ("fourier", 1, FOURIER_N), ("ada1", 4, CHUNK), ("ada2", 4, CHUNK), ("w_out", 2, CHUNK), ("w_up", 11, CHUNK),
         ("w_down", 8, FT * P), ("w_in_a", 6, CHUNK), ("w_out_a", 2, CHUNK), ("moe0", 0, 0), ("ple0", 2, CHUNK),
         ("ple_w0", 1, 2 * D), ("w_in_b", 4, CHUNK), ("gates", 2, CHUNK), ("w_out_b", 2, CHUNK), ("moe1", 0, 0),
         ("ple1", 2, CHUNK), ("ple_w1", 1, 2 * D)]
USES = [("ada0", 8), ("kv", 8), ("q", 2), ("z", 2), ("u", 2), ("dft_w", 2), ("vtok", 4), ("dft_b", 4),
        ("ada1", 8), ("dft_y", 2), ("ada2", 8), ("ktok", 4),
        ("w_out", 4), ("up", FT), ("down", 4), ("in_a", 12), ("out_a", 4), ("ple0", 8), ("in_b", 8), ("gates", 16),
        ("out_b", 4), ("ple1", 8)]


def plan():
    first, n, use, at = {}, 0, {}, 0
    for name, count, _ in DENSE:
        first[name] = n
        n += 6 * PAIRS if name.startswith("moe") else count
    for name, count in USES:
        use[name] = at
        at += count
    free = {}
    for stage in ("ada0", "ada1", "ada2"):
        for c in range(4):
            free[first[stage] + c] = ("dense_full", use[stage] + max(1, 2 * c))
    for c, last in enumerate((4, 8, 10, 12, 14)):
        free[first["w_in"] + c] = ("dense_full", use["kv"] + last)
    free[first["fourier"]] = ("dense_full", use["dft_y"] + 2)
    for stage, users, per, n_chunks in (("w_out", "w_out", 2, 2), ("w_up", "up", 2, 11), ("w_in_a", "in_a", 2, 6),
                                        ("w_out_a", "out_a", 2, 2), ("w_in_b", "in_b", 2, 4), ("w_out_b", "out_b", 2, 2)):
        for c in range(n_chunks):
            free[first[stage] + c] = ("dense_full", use[users] + per * (c + 1))
    for c in range(8):
        free[first["w_down"] + c] = ("dense_full", use["down"] + c // 2 + 1)
    for c in range(2):
        free[first["gates"] + c] = ("dense_full", use["gates"] + 16)
    for layer in range(2):
        free[first[f"ple{layer}"]] = ("dense_full", use[f"ple{layer}"] + 3)
        free[first[f"ple{layer}"] + 1] = ("dense_full", use[f"ple{layer}"] + 7)
        free[first[f"ple_w{layer}"]] = ("dense_full", use[f"ple{layer}"] + 8)
        for c, (sem, per) in enumerate((("gate_mm", 1), ("gate_mm", 1), ("up_mm", 1), ("up_mm", 1), ("down_mm", 2), ("down_mm", 2))):
            for i in range(PAIRS):
                free[first[f"moe{layer}"] + 6 * i + c] = (sem, per * (layer * PAIRS + i + 1))
    return first, use, free


FIRST, USE, FREE = plan()
WORK, WORK_N = layout([
    ("kc", 2048), ("vc", 2048), ("qc", 1024), ("ktok", 2048), ("vtok", 2048), ("zs", 1024), ("cat", 2048),
    ("S", 1024), ("oT", 1024), ("masks", MASKS_N), ("dtmp", 4096), ("small", 328),
])
SEMAPHORES = [
    "param_load", "const_load", "ctx_load", "x_load", "mask_load", "p_load", "out_store",
    "zeroed", "c_cols", "dve_step", "act_step", 
    "sq_ready", "ss_ready", "rstd_ready", "xn_scaled", "xn_ready", "h_ready", "dense_full",
    "ab_mm", "ab_sb", "ab_cols", "ab_act", "ab_dve", "silu_ready",
    "qk_sq", "qk_ss", "qk_rstd", "qk_norm",
    "g_rows", "g_diff", "g_masked", "decay", "at_ready", "g_pool", "lvl_mask", "lvl_p", "lvl_p_sb", "lvl_tp", "lvl_t",
    "qk_mm", "ks_mm", "x_ready", "vn_mm", "vn_sb", "o_mm", "ds_mm", "s_ready", "o_ready",
    "o_sq", "o_ss", "o_rstd", "cat_ready", "ffn_conv", "ffn_silu", "c_sb",
    "tok_mm", "tok_sb", "tok_sb2", "mask_ready", "gates_ready", "lg_mm", "lg_sb", "lg_cols", "route_dve", "route_act", "rank_mm", "route_ready", 
    "onehot", "onehot_w", "gather_mm", "xg_act", "xg_dve", "gate_mm", "up_mm", "sg_sb", "hh_sb", "t_mm", "ht_sb",
    "down_mm", "y_act", "y_dve", "pwt_mm", "pwt_sb", "scat_mm", "scat_add", "moe_done",
    "lru_log", "lru_exp", "lru_var", "lru_sqrt", "lru_h", "fin_ready",
] + [f"slot_full{r}" for r in range(RING)] + [f"dense_free{b}" for b in range(BANKS)] \
  + [f"ov_{what}{layer}" for layer in range(2) for what in ("full", "gu", "sg", "hh", "t", "ht", "down", "add")]


def build(nc, t):
    S = {name: nc.alloc_semaphore(name) for name in SEMAPHORES}

    ring = [nc.alloc_sbuf_tensor(f"ring{r}", [P, CHUNK], F32) for r in range(RING)]
    bank = [nc.alloc_psum_tensor(f"bank{b}", [P, 512], F32) for b in range(8)]
    hT = nc.alloc_sbuf_tensor("hT", [P, KT, SEQ], F32)
    xn = nc.alloc_sbuf_tensor("xn", [P, KT, 2, SEQ], F32)
    params = nc.alloc_sbuf_tensor("params", [P, PARAMS_N], F32)
    consts = nc.alloc_sbuf_tensor("consts", [P, CONSTS_N], F32)
    work = nc.alloc_sbuf_tensor("work", [P, WORK_N], F32)
    mod = nc.alloc_sbuf_tensor("mod", [P, 48, 2], F32)
    gains = nc.alloc_sbuf_tensor("gains", [P, 5, KT], F32)
    flag = nc.alloc_sbuf_tensor("flag", [P, 1], I32)

    def par(name, a=0, size=None):
        at, n = PARAMS[name]
        return params[:, at + a:at + (n if size is None else a + size)]

    def con(name):
        at, n = CONSTS[name]
        return consts[:, at:at + n]

    def wk(name, size=None, off=0):
        at, n = WORK[name]
        return work[:, at + off:at + off + (size or n)]

    def flat(at, n):
        assert at + n <= WORK_N
        return work[:, at:at + n]

    ident, ones, strict = con("ident"), con("ones"), con("strict")
    cums = [con("upper"), con("lower")]

    kc = wk("kc").rearrange("p (h s t) -> p h s t", h=HEADS, s=2)
    vc = wk("vc").rearrange("p (h s t) -> p h s t", h=HEADS, s=2)
    qc = wk("qc").rearrange("p (h t) -> p h t", h=HEADS)
    ktok = wk("ktok").rearrange("p (u h d) -> p u h d", u=4, h=HEADS)
    vtok = wk("vtok").rearrange("p (u h d) -> p u h d", u=4, h=HEADS)
    ctxT = wk("ktok").rearrange("p (k t) -> p k t", k=KT)
    zs = wk("zs").rearrange("p (h t) -> p h t", h=HEADS)
    cat = wk("cat").rearrange("p (k t) -> p k t", k=KT)
    uT = wk("oT").rearrange("p (g t) -> p g t", g=4)
    state = wk("S").rearrange("p (d h e) -> p d h e", d=2, h=HEADS)
    oT = wk("oT").rearrange("p (h t) -> p h t", h=HEADS)
    neg = wk("masks", 2 * P).rearrange("p (d t) -> p d t", d=2)
    level = wk("masks", LEVELS * P, 2 * P).rearrange("p (l t) -> p l t", l=LEVELS)
    dtmp = wk("dtmp").rearrange("p (n d h t) -> p n d h t", n=4, d=2, h=HEADS)
    decayT, attnT, qd, kd = (dtmp[:, n] for n in range(4))
    tri = xn[:].rearrange("p k s t -> p (k s t)").rearrange("p (n d h t) -> p n d h t", n=4, d=2, h=HEADS)
    tinv, tinvT, pmat, amatT = (tri[:, n] for n in range(4))
    xv = wk("vc").rearrange("p (n d h t) -> p n d h t", n=2, d=2, h=HEADS)
    lmask, xmat = xv[:, 0], xv[:, 1]
    vnew = lmask
    sq2 = wk("dtmp").rearrange("p (k s t) -> p k s t", k=KT, s=2)
    sqk = wk("dtmp", 1024, 3072).rearrange("p (n t) -> p n t", n=2)
    ada_row = wk("cat", 1024, 1024).rearrange("p (m n) -> p m n", m=2)
    c_cols = wk("S", KT * 32).rearrange("p (k m) -> p k m", k=KT)
    ab_rows = wk("dtmp", 512)
    fo_w = wk("dtmp", 1024).rearrange("p (x n) -> p x n", x=2)
    fo_b = wk("dtmp", 2048, 1024).rearrange("p (x u g e) -> p x u g e", x=2, u=2, g=4)
    ab = wk("small", 64, 0).rearrange("p (u c) -> p u c", u=4)
    beta = wk("small", 32, 64).rearrange("p (u c) -> p u c", u=4)
    glog = wk("small", 32, 96).rearrange("p (u c) -> p u c", u=4)
    gtmp = [wk("small", 32, 128 + 32 * i).rearrange("p (u c) -> p u c", u=4) for i in range(5)]
    gcol = wk("small", 8, 288).rearrange("p (d h) -> p d h", d=2)
    egcol = wk("small", 8, 296).rearrange("p (d h) -> p d h", d=2)
    begc = wk("small", 8, 304).rearrange("p (d h) -> p d h", d=2)
    egl = wk("small", 8, 312).rearrange("p (d h) -> p d h", d=2)
    alog_e = wk("small", 8, 320)

    yT = flat(0, 2048).rearrange("p (k t) -> p k t", k=KT)
    xnT, sq1 = xn[:, :, 0], xn[:, :, 1]
    prod = flat(2048, FT * SEQ).rearrange("p (f t) -> p f t", f=FT)
    acc = flat(7680, 1024).rearrange("p (n t) -> p n t", n=4)
    sgate = flat(8704, 512).rearrange("p (n t) -> p n t", n=2)
    tmp = flat(9216, 1024).rearrange("p (n t) -> p n t", n=4)
    c_sb = flat(2048, 512).rearrange("p (n t) -> p n t", n=2)
    ch = flat(2560, 512).rearrange("p (n t) -> p n t", n=2)
    cu = flat(3072, 1024).rearrange("p (n t) -> p n t", n=4)
    xtok = flat(0, 2048).rearrange("p (u f) -> p u f", u=NH)
    xg = flat(2048, 1024).rearrange("p (k s) -> p k s", k=KT)
    sg, hh = flat(3072, 512), flat(3584, 512)
    hidT = flat(4096, 512).rearrange("p (j s) -> p j s", j=4)
    ysb = flat(4608, 1024)
    pwt = flat(5632, 256)
    oneh = flat(5888, 256).rearrange("p (u x s) -> p u x s", u=NH, x=2)
    onehw = flat(6144, 256).rearrange("p (u x s) -> p u x s", u=NH, x=2)
    lgT = flat(6400, 256)
    lg = flat(6656, 72).rearrange("p (u c) -> p u c", u=NH)
    EP = E + 2
    rankm = flat(7928, NH * EP).rearrange("p (u e) -> p u e", u=NH)
    wgt = flat(7996, NH * EP).rearrange("p (u e) -> p u e", u=NH)
    wov = flat(8064, NH * E).rearrange("p (u e) -> p u e", u=NH)

    def rt(at, n):
        return flat(6728 + at, NH * n).rearrange("p (u c) -> p u c", u=NH)

    gsb = flat(2048, 2048).rearrange("p (k t) -> p k t", k=KT)
    yg = flat(0, 2048).rearrange("p (k t) -> p k t", k=KT)
    uu = flat(2048, 2048).rearrange("p (k t) -> p k t", k=KT)
    rr, th, gi = ([flat(4096 + 2048 * (3 * d + i), 2048).rearrange("p (k t) -> p k t", k=KT) for d in range(2)]
                  for i in range(3))
    a_sq = [xn[:, :, d] for d in range(2)]
    nls = flat(17408, 16)
    nlt = [flat(17424 + 16 * i, 16) for i in range(5)]
    pT = flat(16384, 1024).rearrange("p (l k t) -> p l k t", l=2, k=2)

    def arrived(eng, n):
        eng.wait_ge(S[f"slot_full{n % RING}"], 16 * (n // RING + 1))
        return ring[n % RING]

    def released(eng, n):
        eng.wait_ge(S[f"dense_free{n % BANKS}"], n // BANKS + 1)

    ctx_block = nc.Block()
    block = ctx_block.__enter__()

    @block.sync
    def _(sp):
        def load(n, src, size):
            if n >= RING:
                sem, value = FREE[n - RING]
                sp.wait_ge(S[sem], value)
            sp.dma_start(ring[n % RING][:, 0:size], src).then_inc(S[f"slot_full{n % RING}"], 16)

        sp.dma_start(ctxT, t["ctx"]).then_inc(S["ctx_load"], 16)
        sp.dma_start(hT[:], t["x"]).then_inc(S["x_load"], 16)
        seen = 0
        for name, count, size in DENSE:
            base = FIRST[name]
            if not name.startswith("moe"):
                for c in range(count):
                    load(base + c, t["dense"][seen + c][:, 0:size], size)
                seen += count
                continue
            layer = int(name[3:])
            gate, up = (t[w][layer].rearrange("e (p j) f -> e p (j f)", j=KT) for w in ("w_gate", "w_up"))
            down = t["w_down"][layer].rearrange("e (p j) f -> e p (j f)", j=4)
            chunks = (gate, gate, up, up, down, down)
            for c, w in enumerate(chunks):
                load(base + c, w[c % 2], CHUNK)
            with sp.Fori(1, PAIRS) as i:
                for c, w in enumerate(chunks):
                    r = (base + c) % RING
                    sem, value = FREE[base + c]
                    sp.wait_ge(S[sem], value + (i - 1) * (2 if c >= 4 else 1))
                    sp.dma_start(ring[r][:], w[i * 2 + c % 2]).then_inc(S[f"slot_full{r}"], 16)
            sp.wait_ge(S["route_ready"], layer + 1)
            over = sp.value_load(flag[0:1, 0:1], min_val=0, max_val=1)
            with sp.If(over > 0):
                gate, up = (t[w][layer].rearrange("e (j p) f -> e p j f", p=P) for w in ("w_gate", "w_up"))
                down = t["w_down"][layer].rearrange("e (j p) f -> e p j f", p=P)
                with sp.Fori(0, E) as e:
                    sp.wait_ge(S[f"ov_down{layer}"], e * 2 + 1)
                    for c, (w, k) in enumerate(((gate, KT), (up, KT), (down, 4))):
                        sp.dma_start(ring[c][:].rearrange("p (j f) -> p j f", j=k), w[e]).then_inc(S[f"ov_full{layer}"], 16)
                sp.wait_ge(S[f"ov_down{layer}"], 2 * E + 1)
                sp.nop()
        sp.wait_ge(S["fin_ready"], 1)
        sp.dma_start(t["out"], yT).then_inc(S["out_store"], 16)
        sp.wait_ge(S["out_store"], 16)

    @block.tensor
    def _(pe):
        mm = nc.tensor.matmul
        count = {}

        def signal(ins, name):
            ins.then_inc(S[name], 1)
            count[name] = count.get(name, 0) + 1
            return count[name]

        def dense(n, tiles, ready=None):
            if n >= BANKS:
                released(pe, n - BANKS)
            for a, b, products in tiles:
                for k, (w, x) in enumerate(products):
                    if ready and a == 0:
                        pe.wait_ge(S[ready[0]], ready[1] + k)
                    last = mm(bank[n % BANKS][:, a:b], w, x, start=k == 0, stop=k == len(products) - 1)
            assert signal(last, "dense_full") == n + 1

        def weights(n, tile, n_k=KT, width=512):
            w = arrived(pe, n)
            return [w[:, k * width + tile * P:k * width + tile * P + P] for k in range(n_k)]

        def projection(stage, chunk, uses, x, ready=None):
            for b in range(uses):
                tiles = [weights(FIRST[chunk] + b // 2, (2 * b + i) % 4) for i in range(2)]
                dense(USE[stage] + b, [(SEQ * i, SEQ * i + SEQ, list(zip(tiles[i], x))) for i in range(2)],
                      ready if b == 0 else None)

        def sum_squares():
            for k in range(KT):
                if k % 2 == 0:
                    pe.wait_ge(S["sq_ready"], 4 * (count.get("norms", 0) + 1) + k // 2 + 1)
                last = mm(bank[4][:, 0:SEQ], ones, sq1[:, k], start=k == 0, stop=k == KT - 1)
            signal(last, "ss_ready")
            count["norms"] = count.get("norms", 0) + 1

        n_normed = [1]

        pe.wait_ge(S["const_load"], 16)
        for k in range(KT):
            pe.wait_ge(S["sq_ready"], k // 2 + 1)
            last = mm(bank[4][:], ones, sq2[:, k].rearrange("p s t -> p (s t)"), start=k == 0, stop=k == KT - 1)
        signal(last, "ss_ready")

        pe.wait_ge(S["c_cols"], 1)

        def ada_rows(part, m):
            n = USE[f"ada{part}"] + max(0, 2 * m - 1)
            w = arrived(pe, FIRST[f"ada{part}"] + m)
            if n >= BANKS:
                released(pe, n - BANKS)
            for kk in range(2):
                for j in range(4):
                    k = 2 * j + kk
                    last = mm(bank[n % BANKS][32 * j:32 * j + 32, :], c_cols[:, k, :], w[:, 512 * k:512 * k + 512],
                              start=kk == 0, stop=kk == 1)
            assert signal(last, "dense_full") == n + 1

        def ada_columns(part, m):
            first = USE[f"ada{part}"]
            released(pe, first + max(0, 2 * m - 1))
            dense(first + min(2 * m + 2, 7), [
                (P * i, P * i + P, [(ada_row[:, m % 2, P * i:P * i + P], con("sel"))]) for i in range(4)])

        def ada_step(part, m):
            if m < 4:
                ada_rows(part, m)
            if m:
                ada_columns(part, m - 1)

        for m in range(5):
            ada_step(0, m)

        both = [xn[:, k].rearrange("p s t -> p (s t)") for k in range(KT)]
        w_ab = par("w_ab").rearrange("p (k c) -> p k c", k=KT)
        for k in range(KT):
            pe.wait_ge(S["xn_ready"], k + 1)
            last = mm(bank[7][0:16, :], w_ab[:, k], both[k], start=k == 0, stop=k == KT - 1)
        signal(last, "ab_mm")
        for i in range(8):
            w = weights(FIRST["w_in"] + i // 4, i % 4)
            dense(USE["kv"] + i, [(0, 512, list(zip(w, both)))])
        pe.wait_ge(S["ab_sb"], 1)
        for u in range(4):
            last = nc.tensor.transpose(bank[6][:, 16 * u:16 * u + 16], ab_rows[0:16, P * u:P * u + P], ident[0:16, 0:16])
        signal(last, "ab_cols")
        x_lat = [xn[:, k, 1] for k in range(KT)]

        def four(stage, c):
            for b in range(2):
                tiles = [weights(FIRST["w_in"] + c, 2 * b + i) for i in range(2)]
                dense(USE[stage] + b, [(SEQ * i, SEQ * i + SEQ, list(zip(tiles[i], x_lat))) for i in range(2)])

        four("q", 2)
        four("z", 3)
        four("u", 4)
        w_fourier = arrived(pe, FIRST["fourier"])

        def fo(name, a=0, n=None):
            at, size = FOURIER[name]
            return w_fourier[:, at + a:at + a + (n or size)]

        def token_major(stage, x):
            for u in range(4):
                s, half = u // 2, u % 2
                n = USE[stage] + u
                released(pe, n - BANKS)
                for h in range(HEADS):
                    last = nc.tensor.transpose(bank[n % BANKS][:, P * h:P * h + P], x[:, h, s, P * half:P * half + P], ident)
                assert signal(last, "dense_full") == n + 1

        def sums_qk(a):
            pe.wait_ge(S["qk_sq"], a + 1)
            if a >= 2:
                pe.wait_ge(S["qk_rstd"], a - 1)
            signal(mm(bank[4 + a % 2][:], ones, sqk[:, a % 2], start=True, stop=True), "qk_ss")

        for x, name in enumerate(("cos_c", "nsin_c")):
            dense(USE["dft_w"] + x, [(0, 512, [(fo(name), fo("w_f"))])])
        pe.wait_ge(S["silu_ready"], 8)
        token_major("vtok", vc)
        released(pe, USE["dft_w"])
        released(pe, USE["dft_w"] + 1)
        for x in range(2):
            for u in range(NH):
                dense(USE["dft_b"] + 2 * x + u, [
                    (P * g, P * g + P, [(uT[:, g, P * u:P * u + P], fo_w[:, x, P * g:P * g + P])]) for g in range(4)])
        for m in range(5):
            if m < 4:
                sums_qk(m)
            ada_step(1, m)
        for b in range(4):
            released(pe, USE["dft_b"] + b)
        for b in range(2):
            dense(USE["dft_y"] + b, [
                (SEQ * i, SEQ * i + SEQ, [(fo_b[:, x, u, 2 * b + i], fo(("cos_l", "sin_l")[x], SEQ * u, SEQ))
                                          for x in range(2) for u in range(NH)]) for i in range(2)])
        for m in range(5):
            if m < 2:
                sums_qk(4 + m)
            ada_step(2, m)
        pe.wait_ge(S["qk_norm"], 6)
        token_major("ktok", kc)

        banks = [[bank[0], bank[1], bank[4], bank[5]], [bank[2], bank[3], bank[6], bank[7]]]
        for u in range(4):
            released(pe, USE["ktok"] + u)
        pe.wait_ge(S["gates_ready"], 1)

        def heads(out, left, right, start=True, stop=True):
            for h in range(HEADS):
                last = mm(out[:, P * h:P * h + P], left(h), right(h), start=start, stop=stop)
            return last

        for n in range(4):
            s, c = n // 2, n % 2
            for d in range(2):
                half, e = (c if d == 0 else 1 - c), 2 * n + d
                a0, a1, a2, a3 = banks[d]
                token = slice(P * half, P * half + P)
                u = 2 * s + half
                if n:
                    pe.wait_ge(S["s_ready"], e - 1)
                heads(a0, lambda h: glog[:, u, 4 * d + h:4 * d + h + 1].to_broadcast([P, P]), lambda h: cums[d])
                heads(a1, lambda h: beta[:, u, 4 * d + h:4 * d + h + 1].to_broadcast([P, P]), lambda h: ident)
                heads(a2, lambda h: kc[:, h, s, token], lambda h: kc[:, h, s, token])
                signal(mm(a3[:, 0:HEADS], cums[d], glog[:, u, 4 * d:4 * d + 4], start=True, stop=True), "g_rows")
            for d in range(2):
                half, e = (c if d == 0 else 1 - c), 2 * n + d
                a0, a1, a2, a3 = banks[d]
                token = slice(P * half, P * half + P)
                if s:
                    pe.wait_ge(S["g_diff"], e + 1)
                    signal(heads(a3, lambda h: kc[:, h, s, token], lambda h: qc[:, h, token]), "qk_mm")
            for l in range(LEVELS):
                for d in range(2):
                    half, e = (c if d == 0 else 1 - c), 2 * n + d
                    a0, a1, a2, a3 = banks[d]
                    i = 2 * (LEVELS * n + l) + d
                    pe.wait_ge(S["lvl_mask"], i + 1)
                    if l:
                        pe.wait_ge(S["lvl_t"], i - 1)
                        signal(heads(a0, lambda h: lmask[:, d, h], lambda h: tinv[:, d, h]), "lvl_p")
                    else:
                        pe.wait_ge(S["decay"], e + 1)
                        signal(heads(a0, lambda h: lmask[:, d, h], lambda h: ident), "lvl_p")
                for d in range(2):
                    a0, a1, a2, a3 = banks[d]
                    i = 2 * (LEVELS * n + l) + d
                    if l:
                        pe.wait_ge(S["lvl_p_sb"], 2 * ((LEVELS - 1) * n + l - 1) + d + 1)
                        if l < LEVELS - 1:
                            heads(a1, lambda h: tinvT[:, d, h], lambda h: pmat[:, d, h])
                        signal(heads(a2, lambda h: pmat[:, d, h], lambda h: tinvT[:, d, h]), "lvl_tp")
            for d in range(2):
                half, e = (c if d == 0 else 1 - c), 2 * n + d
                a0 = banks[d][0]
                token = slice(P * half, P * half + P)
                if n:
                    signal(heads(a0, lambda h: kc[:, h, s, token], lambda h: state[:, d, h]), "ks_mm")
            for d in range(2):
                a1 = banks[d][1]
                pe.wait_ge(S["lvl_t"], 2 * (LEVELS * n + LEVELS - 1) + d + 1)
                if n:
                    pe.wait_ge(S["x_ready"], 2 * (n - 1) + d + 1)
                else:
                    pe.wait_ge(S["g_pool"], d + 1)
                signal(heads(a1, lambda h: tinvT[:, d, h], lambda h: xmat[:, d, h]), "vn_mm")
            for d in range(2):
                half, e = (c if d == 0 else 1 - c), 2 * n + d
                a2, a3 = banks[d][2:]
                pe.wait_ge(S["vn_sb"], e + 1)
                pe.wait_ge(S["g_pool"], e + 1)
                if s:
                    for h in range(HEADS):
                        mm(a2[:, P * h:P * h + P], state[:, d, h], qd[:, d, h], start=True, stop=False)
                        last = mm(a2[:, P * h:P * h + P], vnew[:, d, h], attnT[:, d, h], start=False, stop=True)
                    signal(last, "o_mm")
                if n < 3:
                    signal(heads(a3, lambda h: kd[:, d, h], lambda h: vnew[:, d, h]), "ds_mm")

        for b in range(2):
            pe.wait_ge(S["o_sq"], b + 1)
            signal(mm(bank[4 + b][:], ones, sqk[:, b], start=True, stop=True), "o_ss")
        pe.wait_ge(S["cat_ready"], 4)
        projection("w_out", "w_out", 4, [cat[:, k] for k in range(KT)])

        xs = [xnT[:, k] for k in range(KT)]

        def norm_input():
            sum_squares()
            n_normed[0] += 1
            return "xn_ready", KT * (n_normed[0] - 1) + 1

        sum_squares()
        ready = norm_input()
        projection("up", "w_up", FT, xs, ready)
        for b in range(BANKS):
            released(pe, USE["up"] + FT - 1 - b)
        for b in range(4):
            tiles = []
            for i in range(2):
                w = arrived(pe, FIRST["w_down"] + 2 * b + i)
                tiles.append((SEQ * i, SEQ * i + SEQ, [(w[:, P * k:P * k + P], prod[:, k]) for k in range(FT)]))
            dense(USE["down"] + b, tiles)
        sum_squares()
        ready = norm_input()
        projection("in_a", "w_in_a", 12, xs, ready)
        for b in range(2):
            released(pe, USE["in_a"] + 11 - b)
        projection("out_a", "w_out_a", 4, [yT[:, k] for k in range(KT)])

        def moe(layer):
            pe.wait_ge(S["xn_ready"], norm_input()[1] + KT - 1)
            for b in range(BANKS):
                released(pe, moe.last_use[layer] - b)
            for m in range(4):
                u = m // 2
                b = bank[m]
                for i in range(4):
                    last = nc.tensor.transpose(b[:, P * i:P * i + P], xnT[:, 4 * (m % 2) + i, P * u:P * u + P], ident)
                signal(last, "tok_mm")
            w_r = par("w_router").rearrange("p (l k c) -> p l k c", l=2, k=KT)
            for k in range(KT):
                last = mm(bank[7][0:36, 0:SEQ], w_r[:, layer, k], xs[k], start=k == 0, stop=k == KT - 1)
            signal(last, "lg_mm")
            pe.wait_ge(S["lg_sb"], layer + 1)
            for u in range(NH):
                last = nc.tensor.transpose(bank[6][:, 36 * u:36 * u + 36], lgT[0:36, P * u:P * u + P], ident[0:36, 0:36])
            signal(last, "lg_cols")
            pe.wait_ge(S["mask_ready"], layer + 1)
            m0, m1 = rt(240, E)[:, 0], rt(240, E)[:, 1]
            mm(bank[5][:, 0:E], strict, m0, start=True, stop=True)
            mm(bank[5][:, E:2 * E], ones, m0, start=True, stop=False)
            mm(bank[5][:, E:2 * E], strict, m1, start=False, stop=True)
            mm(bank[5][:, 2 * E:3 * E], ones, m0, start=True, stop=False)
            signal(mm(bank[5][:, 2 * E:3 * E], ones, m1, start=False, stop=True), "rank_mm")

            done, extra = layer * PAIRS, layer * (PAIRS + 1)

            def gather(i):
                pe.wait_ge(S["onehot"], i + extra + 1)
                for k in range(KT):
                    out = bank[2 + k // 4][:, P * (k % 4):P * (k % 4) + P]
                    for u in range(NH):
                        last = mm(out, xtok[:, u, k:D:KT], oneh[:, u].rearrange("p x s -> p (x s)"),
                                  start=u == 0, stop=u == NH - 1)
                last.then_inc(S["gather_mm"], 1)

            def scatter(i):
                pe.wait_ge(S["y_act"], i + done + layer)
                pe.wait_ge(S["y_dve"], i + done + layer)
                pe.wait_ge(S["pwt_sb"], i + done + layer)
                for q in range(4):
                    if q in (0, 3):
                        pe.wait_ge(S["scat_add"], (i - 1) * 4 + (1 if q == 3 else 0) + layer * (4 * PAIRS + 5) + 1)
                    b = bank[(5, 2, 3, 5)[q]]
                    for x in range(2):
                        last = mm(b[:, SEQ * x:SEQ * x + SEQ], ysb[:, P * (2 * q + x):P * (2 * q + x) + P], pwt,
                                  start=True, stop=True)
                    last.then_inc(S["scat_mm"], 1)

            def arrived_pair(i, c):
                n = FIRST[f"moe{layer}"] + c
                pe.wait_ge(S[f"slot_full{n % RING}"], i * 16 + 16 * (n // RING + 1))
                return ring[n % RING]

            pe.wait_ge(S["tok_sb"], 2 * (layer + 1))
            pe.wait_ge(S["tok_sb2"], 2 * (layer + 1))
            gather(0)
            with pe.Fori(0, PAIRS) as i:
                pe.wait_ge(S["xg_act"], i + extra + 1)
                pe.wait_ge(S["xg_dve"], i + extra + 1)
                for c, b, sem in ((0, bank[0], "gate_mm"), (2, bank[1], "up_mm")):
                    ws = [arrived_pair(i, c + x) for x in range(2)]
                    for k in range(KT):
                        for x in range(2):
                            last = mm(b[64 * x:64 * x + 64, :], xg[:, k, 64 * x:64 * x + 64],
                                      ws[x][:, 512 * k:512 * k + 512], start=k == 0, stop=k == KT - 1)
                    last.then_inc(S[sem], 1)
                pe.wait_ge(S["scat_add"], i * 4 + layer * (4 * PAIRS + 5) + 1)
                gather(i + 1)
                pe.wait_ge(S["pwt_sb"], i + 1 + done + layer)
                pe.wait_ge(S["hh_sb"], i + 1 + done)
                for j in range(4):
                    last = nc.tensor.transpose(bank[4][:, P * j:P * j + P], hh[:, j:DE:4], ident)
                last.then_inc(S["t_mm"], 1)
                pe.wait_ge(S["xg_act"], i + extra + 2)
                pe.wait_ge(S["xg_dve"], i + extra + 2)
                scatter(i + 1)
                pe.wait_ge(S["ht_sb"], i + 1 + done)
                ws = [arrived_pair(i, 4 + x) for x in range(2)]
                for half in range(2):
                    for j in range(4):
                        for x in range(2):
                            at = D * j + 512 * half
                            last = mm(bank[6 + half][64 * x:64 * x + 64, :], hidT[:, j, 64 * x:64 * x + 64],
                                      ws[x][:, at:at + 512], start=j == 0, stop=j == 3)
                    last.then_inc(S["down_mm"], 1)
                pe.wait_ge(S["onehot_w"], i + 1 + done)
                for u in range(NH):
                    last = nc.tensor.transpose(bank[4][:, P * u:P * u + P], onehw[:, u].rearrange("p x s -> p (x s)"), ident)
                last.then_inc(S["pwt_mm"], 1)
            scatter(PAIRS + 1)

            over = pe.value_load(flag[0:1, 0:1], min_val=0, max_val=1)
            with pe.If(over > 0):
                with pe.Fori(0, E) as e:
                    pe.wait_ge(S[f"ov_full{layer}"], e * 48 + 48)
                    for u in range(NH):
                        pe.wait_ge(S[f"ov_add{layer}"], e * 2 + u + 1)
                        for b in range(2):
                            for k in range(KT):
                                last = mm(bank[b][:], xnT[:, k, P * u:P * u + P], ring[b][:, 512 * k:512 * k + 512],
                                          start=k == 0, stop=k == KT - 1)
                        last.then_inc(S[f"ov_gu{layer}"], 1)
                        pe.wait_ge(S[f"ov_hh{layer}"], e * 2 + u + 1)
                        for j in range(4):
                            last = nc.tensor.transpose(bank[4][:, P * j:P * j + P], hh[:, P * j:P * j + P], ident)
                        last.then_inc(S[f"ov_t{layer}"], 1)
                        pe.wait_ge(S[f"ov_ht{layer}"], e * 2 + u + 1)
                        for f in range(KT):
                            out = bank[6 + f // 4][:, P * (f % 4):P * (f % 4) + P]
                            for j in range(4):
                                last = mm(out, ring[2][:, D * j + P * f:D * j + P * f + P], hidT[:, j],
                                          start=j == 0, stop=j == 3)
                        last.then_inc(S[f"ov_down{layer}"], 1)
                pe.wait_ge(S[f"ov_add{layer}"], 2 * E + 1)
                nc.tensor.nop()
            pe.wait_ge(S["moe_done"], layer + 1)

        def ple(layer):
            ready = norm_input()
            for b in range(4):
                chunk = FIRST[f"ple{layer}"] + b // 2
                tiles = [weights(chunk, (2 * b + i) % 4) for i in range(2)]
                dense(USE[f"ple{layer}"] + 2 * b, [(SEQ * i, SEQ * i + SEQ, list(zip(tiles[i], xs))) for i in range(2)],
                      None if b else ready)
                w = arrived(pe, FIRST[f"ple_w{layer}"])
                pe.wait_ge(S["p_load"], 16)
                dense(USE[f"ple{layer}"] + 2 * b + 1, [
                    (SEQ * i, SEQ * i + SEQ, [(w[:, D * k + P * (2 * b + i):D * k + P * (2 * b + i) + P], pT[:, layer, k])
                                              for k in range(2)]) for i in range(2)])

        moe.last_use = [USE["out_a"] + 3, USE["out_b"] + 3]
        moe(0)
        ple(0)
        ready = norm_input()
        projection("in_b", "w_in_b", 8, xs, ready)
        for b in range(4):
            released(pe, USE["in_b"] + b)
        wr, wi = (arrived(pe, FIRST["gates"] + x) for x in range(2))
        for d in range(2):
            for j in range(KT):
                at = [((d * 4 + j // 2) * 2 + k) * 256 + P * (j % 2) for k in range(2)]
                dense(USE["gates"] + KT * d + j, [
                    (SEQ * x, SEQ * x + SEQ, [(w[:, at[k]:at[k] + P], uu[:, 2 * (j // 2) + k]) for k in range(2)])
                    for x, w in enumerate((wr, wi))])
        projection("out_b", "w_out_b", 4, [rr[0][:, k] for k in range(KT)], ("lru_h", 1))
        moe(1)
        ple(1)
        sum_squares()

    def bc(ap, shape):
        for _ in range(len(shape) - len(ap.shape)):
            ap = ap.unsqueeze(len(ap.shape))
        return ap.to_broadcast(shape)

    @block.scalar
    def _(act):
        count = {}

        def signal(ins, name):
            ins.then_inc(S[name], 1)
            count[name] = count.get(name, 0) + 1
            return count[name]

        def after(ins):
            act.wait_ge(S["act_step"], signal(ins, "act_step"))

        def free(ins, use):
            ins.then_inc(S[f"dense_free{use % BANKS}"], 1)

        def full(use):
            act.wait_ge(S["dense_full"], use + 1)

        def root(source, out, scale, sem, name):
            act.wait_ge(S[sem], count.get(sem + "s", 0) + 1)
            count[sem + "s"] = count.get(sem + "s", 0) + 1
            after(act.activation(out, source, ACT.Ln, bias=con("eps"), scale=scale))
            signal(act.activation(out, out, ACT.Exp, scale=-0.5), name)

        def squares(src, waits):
            functions(LN_EXP)
            for i, (sem, value) in enumerate(waits):
                act.wait_ge(S[sem], value)
                signal(act.activation(sq1[:, 2 * i:2 * i + 2], src[:, 2 * i:2 * i + 2], ACT.Square), "sq_ready")
            root(bank[4][:, 0:SEQ], bank[5][:, 0:SEQ], 1.0 / D, "ss_ready", "rstd_ready")

        def uses_free(first):
            return [(f"dense_free{n % BANKS}", n // BANKS + 1) for n in range(first, first + 4)]

        held = {}

        def functions(name):
            if held.get("set") != name:
                act.preload_act_table_set(name)
            held["set"] = name

        act.dma_start(params[:], t["params"]).then_inc(S["param_load"], 16)
        act.dma_start(consts[:], t["consts"]).then_inc(S["const_load"], 16)
        act.wait_ge(S["param_load"], 16)
        act.wait_ge(S["zeroed"], 1)
        signal(act.activation(c_cols[:, :, 0:2], par("c").rearrange("p (k m) -> p k m", k=KT), ACT.Silu), "c_cols")
        functions(LN_EXP)
        signal(act.activation(alog_e, par("a_log"), ACT.Exp), "ab_act")
        act.wait_ge(S["const_load"], 16)
        act.wait_ge(S["ctx_load"], 16)
        act.wait_ge(S["x_load"], 16)
        for i in range(4):
            pair = slice(2 * i, 2 * i + 2)
            act.activation(sq2[:, pair, 0], ctxT[:, pair], ACT.Square)
            signal(act.activation(sq2[:, pair, 1], hT[:, pair], ACT.Square), "sq_ready")
        root(bank[4][:], bank[5][:], 1.0 / D, "ss_ready", "rstd_ready")

        def shifts(at, count_before, sequences):
            for k in range(KT):
                act.wait_ge(S["xn_scaled"], count_before + k + 1)
                for s in sequences:
                    column = mod[:, at + k, (1 - s if len(sequences) == 2 else 0):][:, 0:1]
                    last = act.activation(xn[:, k, s], xn[:, k, s], ACT.Identity, bias=column)
                signal(last, "xn_ready")

        shifts(0, 0, (0, 1))
        act.dma_start(wk("masks"), t["masks"]).then_inc(S["mask_load"], 16)
        act.wait_ge(S["ab_mm"], 1)
        signal(act.activation(ab_rows[0:16, :], bank[7][0:16, :], ACT.Copy), "ab_sb")

        functions(SILU)
        for i in range(8):
            released(act, USE["kv"] + i)
            x = (kc if i < 4 else vc)[:, i % 4]
            signal(act.activation(x, x, ACT.Silu), "silu_ready")
        for b in range(2):
            released(act, USE["q"] + b)
            signal(act.activation(qc[:, 2 * b:2 * b + 2], qc[:, 2 * b:2 * b + 2], ACT.Silu), "silu_ready")
        for b in range(2):
            full(USE["z"] + b)
            free(act.activation(wk("zs", 512, 512 * b), bank[(USE["z"] + b) % BANKS][:], ACT.Silu), USE["z"] + b)
        for b in range(2):
            full(USE["u"] + b)
            free(act.activation(wk("oT", 512, 512 * b), bank[(USE["u"] + b) % BANKS][:], ACT.Copy), USE["u"] + b)
        for x in range(2):
            n = USE["dft_w"] + x
            full(n)
            free(act.activation(fo_w[:, x], bank[n % BANKS][:], ACT.Copy), n)
        act.wait_ge(S["ab_dve"], 1)
        functions(SIGMOID)
        signal(act.activation(beta, ab[:, :, 0:8], ACT.Sigmoid), "ab_act")
        functions(LN_EXP)
        act.wait_ge(S["ab_dve"], 2)
        signal(act.activation(gtmp[1], gtmp[1], ACT.Exp, scale=-1.0), "ab_act")
        for u in range(4):
            n = USE["vtok"] + u
            full(n)
            free(act.activation(wk("vtok", 512, 512 * u), bank[n % BANKS][:], ACT.Copy), n)

        heads_of = [wk("kc", 512, 512 * h) for h in range(4)] + [wk("qc", 512, 512 * h) for h in range(2)]

        def square_qk(a):
            if a >= 2:
                act.wait_ge(S["qk_ss"], a - 1)
            signal(act.activation(sqk[:, a % 2], heads_of[a], ACT.Square), "qk_sq")

        act.wait_ge(S["silu_ready"], 10)
        square_qk(0)
        square_qk(1)
        for x in range(4):
            n = USE["dft_b"] + x
            full(n)
            free(act.activation(fo_b[:, x // 2, x % 2].rearrange("p g e -> p (g e)"), bank[n % BANKS][:], ACT.Copy), n)
        for a in range(6):
            if a >= 2:
                act.wait_ge(S["qk_norm"], a - 1)
            root(bank[4 + a % 2][:], bank[6 + a % 2][:], 1.0, "qk_ss", "qk_rstd")
            if a + 2 < 6:
                square_qk(a + 2)
        for b in range(2):
            n = USE["dft_y"] + b
            full(n)
            free(act.activation(wk("cat", 512, 512 * b), bank[n % BANKS][:], ACT.Copy), n)
        for u in range(4):
            n = USE["ktok"] + u
            full(n)
            free(act.activation(wk("ktok", 512, 512 * u), bank[n % BANKS][:], ACT.Copy), n)

        banks = [[bank[0], bank[1], bank[4], bank[5]], [bank[2], bank[3], bank[6], bank[7]]]

        def by_head(b):
            return b[:].rearrange("p (h t) -> p h t", h=HEADS)

        for n in range(4):
            s = n // 2
            for d in range(2):
                e, last = 2 * n + d, (P - 1 if d == 0 else 0)
                a0 = by_head(banks[d][0])
                act.wait_ge(S["g_diff"], e + 1)
                if s:
                    act.activation(qd[:, d], a0, ACT.Exp)
                act.activation(egl[:, d], a0[:, :, last], ACT.Exp)
                act.activation(egcol[:, d], gcol[:, d], ACT.Exp)
                act.wait_ge(S["g_masked"], e + 1)
                signal(act.activation(decayT[:, d], decayT[:, d], ACT.Exp), "decay")
            for l in range(1, LEVELS):
                for d in range(2):
                    i = 2 * (LEVELS * n + l) + d
                    act.wait_ge(S["lvl_p"], i + 1)
                    signal(act.activation(pmat[:, d], by_head(banks[d][0]), ACT.Copy), "lvl_p_sb")
            for d in range(2):
                act.wait_ge(S["vn_mm"], 2 * n + d + 1)
                signal(act.activation(vnew[:, d], by_head(banks[d][1]), ACT.Copy), "vn_sb")
        act.wait_ge(S["o_ready"], 4)
        for b in range(2):
            signal(act.activation(sqk[:, b], wk("oT", 512, 512 * b), ACT.Square), "o_sq")
        for b in range(2):
            root(bank[4 + b][:], bank[6 + b][:], 1.0 / P, "o_ss", "o_rstd")
        act.dma_start(pT, t["p"]).then_inc(S["p_load"], 16)

        def rows(stage):
            for b in range(4):
                n = USE[stage] + b
                full(n)
                free(act.activation(yT[:, 2 * b:2 * b + 2], bank[n % BANKS][:], ACT.Copy), n)
            squares(yT, uses_free(USE[stage]))

        rows("w_out")
        squares(hT, [("h_ready", 2 * i + 2) for i in range(4)])
        shifts(24, KT, (0,))
        functions(SILU)
        for f in range(FT):
            act.wait_ge(S["ffn_conv"], f + 1)
            signal(act.activation(sgate[:, f % 2], acc[:, f % 4], ACT.Silu), "ffn_silu")
        rows("down")
        squares(hT, [("h_ready", 8 + 2 * i + 2) for i in range(4)])
        for j in range(KT):
            n = USE["in_a"] + 3 * (j // 2) + j % 2
            full(n)
            if j >= 2:
                m = USE["in_a"] + 3 * ((j - 2) // 2) + j % 2
                released(act, m)
            signal(act.activation(c_sb[:, j % 2], bank[n % BANKS][:, 0:SEQ], ACT.Copy), "c_sb")

        def moe(layer):
            squares(hT, uses_free(USE[("out_a", "out_b")[layer]]))
            for m in (0, 2):
                act.wait_ge(S["tok_mm"], 4 * layer + m + 1)
                signal(act.activation(xtok[:, m // 2, 0:512], bank[m][:], ACT.Copy), "tok_sb")
            act.wait_ge(S["lg_mm"], layer + 1)
            signal(act.activation(lgT[0:36, :], bank[7][0:36, 0:SEQ], ACT.Copy), "lg_sb")
            act.wait_ge(S["route_dve"], 2 * layer + 1)
            for u in range(NH):
                last = act.activation(rt(52, 4)[:, u], lg[:, u, 0:4], ACT.Exp, bias=rt(50, 1)[:, u], accum_out=rt(60, 1)[:, u])
            signal(last, "route_act")
            act.wait_ge(S["route_dve"], 2 * layer + 2)
            signal(act.activation(rt(190, 1), rt(188, 1), ACT.Exp), "route_act")

            done, extra = layer * PAIRS, layer * (PAIRS + 1)
            functions(SILU)
            act.wait_ge(S["gather_mm"], extra + 1)
            act.activation(xg[:, 0:4], bank[2][:], ACT.Copy).then_inc(S["xg_act"], 1)
            with act.Fori(0, PAIRS) as i:
                act.wait_ge(S["gate_mm"], i + done + 1)
                act.activation(sg, bank[0][:], ACT.Silu).then_inc(S["sg_sb"], 1)
                act.wait_ge(S["gather_mm"], i + extra + 2)
                act.activation(xg[:, 0:4], bank[2][:], ACT.Copy).then_inc(S["xg_act"], 1)
                act.wait_ge(S["t_mm"], i + done + 1)
                act.activation(hidT, bank[4][:], ACT.Copy).then_inc(S["ht_sb"], 1)
                act.wait_ge(S["down_mm"], i * 2 + 2 * done + 1)
                act.activation(ysb[:, 0:512], bank[6][:], ACT.Copy).then_inc(S["y_act"], 1)
                act.wait_ge(S["pwt_mm"], i + extra + 2)
                act.activation(pwt, bank[4][:, 0:SEQ], ACT.Copy).then_inc(S["pwt_sb"], 1)

            over = act.value_load(flag[0:1, 0:1], min_val=0, max_val=1)
            with act.If(over > 0):
                with act.Fori(0, E) as e:
                    for u in range(NH):
                        act.wait_ge(S[f"ov_gu{layer}"], e * 2 + u + 1)
                        act.activation(sg, bank[0][:], ACT.Silu).then_inc(S[f"ov_sg{layer}"], 1)
                        act.wait_ge(S[f"ov_t{layer}"], e * 2 + u + 1)
                        act.activation(hidT, bank[4][:], ACT.Copy).then_inc(S[f"ov_ht{layer}"], 1)

        def ple(layer):
            held.clear()
            squares(hT, [("moe_done", layer + 1)] * 4)
            functions(SIGMOID)
            for b in range(4):
                n = USE[f"ple{layer}"] + 2 * b
                full(n)
                for x in range(2):
                    j = 2 * b + x
                    last = act.activation(gsb[:, j], bank[n % BANKS][:, SEQ * x:SEQ * x + SEQ], ACT.Sigmoid,
                                          bias=par("b_ple", 8 * layer + j, 1))
                free(last, n)

        moe(0)
        ple(0)
        squares(hT, [("h_ready", 16 + i + 1) for i in range(4)])
        act.wait_ge(S["lru_log"], 1)
        signal(act.activation(nlt[1], nlt[1], ACT.Exp, scale=-1.0), "lru_exp")
        functions(GELU)
        for b in range(4):
            n = USE["in_b"] + 4 + b
            full(n)
            free(act.activation(yg[:, 2 * b:2 * b + 2], bank[n % BANKS][:], ACT.Gelu_apprx_tanh), n)
        functions(SIGMOID)
        for i in range(2 * KT + 1):
            if i < 2 * KT:
                d, j = i // KT, i % KT
                n = USE["gates"] + i
                full(n)
                act.activation(rr[d][:, j], bank[n % BANKS][:, 0:SEQ], ACT.Sigmoid, bias=par("b_rg", 8 * d + j, 1))
                free(act.activation(gi[d][:, j], bank[n % BANKS][:, SEQ:512], ACT.Sigmoid, bias=par("b_ig", 8 * d + j, 1)), n)
            if i:
                d, j = (i - 1) // KT, (i - 1) % KT
                act.wait_ge(S["lru_log"], i + 1)
                last = act.activation(th[d][:, j], rr[d][:, j], ACT.Tanh)
        after(last)
        functions(EXP)
        for d in range(2):
            signal(act.activation(a_sq[d], rr[d], ACT.Exp, scale=2.0), "lru_exp")
            signal(act.activation(rr[d], rr[d], ACT.Exp), "lru_exp")
        functions(SQRT)
        for d in range(2):
            act.wait_ge(S["lru_var"], d + 1)
            signal(act.activation(th[d], th[d], ACT.Sqrt, scale=-1.0), "lru_sqrt")
        moe(1)
        ple(1)
        squares(hT, [("h_ready", 20 + i + 1) for i in range(4)])

    @block.gpsimd
    def _(pool):
        pool.memset(wk("S", KT * 32), 0.0).then_inc(S["zeroed"], 1)
        pool.wait_ge(S["mask_load"], 16)
        shape = [P, HEADS, P]

        def heads(m):
            return m.unsqueeze(1).to_broadcast(shape)

        for n in range(4):
            s, c = n // 2, n % 2
            for d in range(2):
                e = 2 * n + d
                pool.wait_ge(S["g_diff"], e + 1)
                pool.tensor_tensor(decayT[:, d], decayT[:, d], heads(neg[:, d]), ALU.add).then_inc(S["g_masked"], 1)
            for l in range(LEVELS):
                for d in range(2):
                    e, half, last = 2 * n + d, (c if d == 0 else 1 - c), (P - 1 if d == 0 else 0)
                    u = 2 * s + half
                    if l == 0:
                        pool.wait_ge(S["at_ready"], e + 1)
                    else:
                        pool.wait_ge(S["lvl_p"], 2 * (LEVELS * n + l - 1) + d + 1)
                        if l == 1:
                            pool.wait_ge(S["lvl_t"], 2 * LEVELS * n + d + 1)
                    pool.tensor_tensor(lmask[:, d], amatT[:, d], heads(level[:, l]), ALU.mult).then_inc(S["lvl_mask"], 1)
                    if l == 1:
                        if n < 3:
                            pool.tensor_tensor(kd[:, d], ktok[:, u], bc(decayT[:, d, :, last], shape), ALU.mult)
                        if s:
                            pool.tensor_tensor(qd[:, d], qd[:, d], qc[:, :, P * half:P * half + P], ALU.mult)
                        pool.tensor_tensor(xmat[:, d], vtok[:, u], bc(beta[:, u, 4 * d:4 * d + 4], shape), ALU.mult)\
                            .then_inc(S["g_pool"], 1)
        for layer in range(2):
            done, extra = layer * PAIRS, layer * (PAIRS + 1)
            with pool.Fori(0, PAIRS) as i:
                pool.wait_ge(S["onehot"], i + extra + 1)
                pool.wait_ge(S["pwt_mm"], i + extra + 1)
                for u in range(NH):
                    last = pool.tensor_tensor(onehw[:, u], oneh[:, u], bc(wgt[:, u, bass.ds(i * 2, 2)], [P, 2, SLOTS]), ALU.mult)
                last.then_inc(S["onehot_w"], 1)

    @block.vector
    def _(dve):
        v = nc.vector
        count = {}

        def signal(ins, name):
            ins.then_inc(S[name], 1)
            count[name] = count.get(name, 0) + 1
            return count[name]

        def after(ins):
            dve.wait_ge(S["dve_step"], signal(ins, "dve_step"))

        def free(ins, use):
            ins.then_inc(S[f"dense_free{use % BANKS}"], 1)

        def full(use):
            dve.wait_ge(S["dense_full"], use + 1)
            return bank[use % BANKS]

        rstd = bank[5][:, 0:SEQ]

        def roots():
            count["roots"] = count.get("roots", 0) + 1
            dve.wait_ge(S["rstd_ready"], count["roots"])

        def scaled(src, gain, ready="xn_ready"):
            roots()
            for k in range(KT):
                ins = v.scalar_tensor_tensor(xnT[:, k], src[:, k], gain(k), rstd, ALU.mult, ALU.mult)
                signal(ins, ready)

        def residual(gain):
            roots()
            for k in range(KT + 1):
                if k < KT:
                    signal(v.scalar_tensor_tensor(tmp[:, k % 4], yT[:, k], gain(k), rstd, ALU.mult, ALU.mult), "dve_step")
                if k:
                    dve.wait_ge(S["dve_step"], count["dve_step"] - (1 if k < KT else 0))
                    signal(v.tensor_tensor(hT[:, k - 1], hT[:, k - 1], tmp[:, (k - 1) % 4], ALU.add), "h_ready")

        def log1p(z, e, scratch):
            a, b = scratch
            after(v.tensor_scalar(a, e, 2.0, None, ALU.add))
            after(v.reciprocal(b, a))
            after(v.tensor_tensor(z, e, b, ALU.mult))
            after(v.tensor_tensor(a, z, z, ALU.mult))
            after(v.tensor_scalar(b, a, LOG1P[7], None, ALU.mult))
            for coefficient in LOG1P[6:0:-1]:
                after(v.scalar_tensor_tensor(b, b, coefficient, a, ALU.add, ALU.mult))
            after(v.scalar_tensor_tensor(z, b, 1.0, z, ALU.add, ALU.mult))
            after(v.tensor_scalar(z, z, 2.0, None, ALU.mult))

        def ada_step(part, m):
            first = USE[f"ada{part}"]
            if m < 4:
                n = first + max(0, 2 * m - 1)
                x = full(n)
                if m >= 2:
                    dve.wait_ge(S["dense_full"], first + 2 * m - 1)
                free(v.tensor_copy(ada_row[:, m % 2], x[:]), n)
            if m:
                n = first + min(2 * m, 7)
                x = full(n)[:].rearrange("p (i c) -> p i c", i=4)[:, :, 0:2]
                at = 4 * (4 * part + m - 1)
                free(v.tensor_tensor(mod[:, at:at + 4], x, bc(par("b_ada", at, 4), [P, 4, 2]), ALU.add), n)

        dve.wait_ge(S["param_load"], 16)
        for m in range(5):
            ada_step(0, m)
        for n in (2, 4, 6, 7):
            released(dve, USE["ada0"] + n)
        for i, (tile, m, g) in enumerate(((8, 1, "g_pre_mix"), (8, 0, "g_pre_mix"))):
            last = v.scalar_tensor_tensor(gains[:, i], mod[:, tile:tile + 8, m], 1.0, par(g), ALU.add, ALU.mult)
        after(last)

        roots()
        dve.wait_ge(S["ctx_load"], 16)
        dve.wait_ge(S["x_load"], 16)
        for k in range(KT):
            for s, src in enumerate((ctxT, hT)):
                ins = v.scalar_tensor_tensor(xn[:, k, s], src[:, k], gains[:, s, k:k + 1], bank[5][:, SEQ * s:SEQ * s + SEQ],
                                             ALU.mult, ALU.mult)
            signal(ins, "xn_scaled")

        def conv3(n, out, x, w):
            after(v.tensor_scalar(out, x, w(1), None, ALU.mult))
            a, b = slice(0, SEQ - 1), slice(1, SEQ)
            after(v.scalar_tensor_tensor(out[..., b], x[..., a], w(0), out[..., b], ALU.mult, ALU.add))
            ins = v.scalar_tensor_tensor(out[..., a], x[..., b], w(2), out[..., a], ALU.mult, ALU.add)
            return ins

        def conv_w(tile):
            return lambda j: par("conv", 3 * tile + j, 1)

        for i in range(8):
            n = USE["kv"] + i
            b = full(n)
            free(conv3(n, (kc if i < 4 else vc)[:, i % 4], b[:].rearrange("p (s t) -> p s t", s=2), conv_w(4 + i)), n)
            if i == 7:
                dve.wait_ge(S["ab_cols"], 1)
                signal(v.tensor_copy(ab, bank[6][:, 0:64].rearrange("p (u c) -> p u c", u=4)), "ab_dve")
                dve.wait_ge(S["ab_dve"], 1)
                after(v.tensor_tensor(gtmp[0], ab[:, :, 8:16], par("dt_bias").unsqueeze(1).to_broadcast([P, 4, 8]), ALU.add))
                signal(v.scalar_tensor_tensor(gtmp[1], gtmp[0], -1.0, gtmp[0], ALU.mult, ALU.max), "ab_dve")
        for b in range(2):
            n = USE["q"] + b
            x = full(n)
            for i in range(2):
                ins = conv3(n, qc[:, 2 * b + i], x[:, SEQ * i:SEQ * i + SEQ], conv_w(2 * b + i))
            free(ins, n)
        dve.wait_ge(S["ab_act"], 3)
        log1p(gtmp[2], gtmp[1], gtmp[3:5])
        after(v.scalar_tensor_tensor(gtmp[0], gtmp[0], 0.0, gtmp[2], ALU.max, ALU.add))
        signal(v.scalar_tensor_tensor(glog, gtmp[0], -1.0, alog_e.unsqueeze(1).to_broadcast([P, 4, 8]), ALU.mult, ALU.mult),
               "gates_ready")
        def norm_qk(a):
            dve.wait_ge(S["qk_rstd"], a + 1)
            r = bank[6 + a % 2][:]
            x = wk("kc", 512, 512 * a) if a < 4 else wk("qc", 512, 512 * (a - 4))
            signal(v.scalar_tensor_tensor(x, x, 1.0 if a < 4 else float(P) ** -0.5, r, ALU.mult, ALU.mult), "qk_norm")

        for m in range(5):
            if m < 4:
                norm_qk(m)
            ada_step(1, m)
        for m in range(5):
            if m < 2:
                norm_qk(4 + m)
            ada_step(2, m)
        for n in (2, 4, 6, 7):
            released(dve, USE["ada2"] + n)
        v.scalar_tensor_tensor(gains[:, 2], mod[:, 32:40, 0], 1.0, par("g_pre_ffn"), ALU.add, ALU.mult)
        v.tensor_tensor(gains[:, 3], mod[:, 16:24, 0], par("g_post_mix"), ALU.mult)
        after(v.tensor_tensor(gains[:, 4], mod[:, 40:48, 0], par("g_post_ffn"), ALU.mult))

        banks = [[bank[0], bank[1], bank[4], bank[5]], [bank[2], bank[3], bank[6], bank[7]]]
        shape = [P, HEADS, P]

        def by_head(b):
            return b[:].rearrange("p (h t) -> p h t", h=HEADS)

        eye = ident.unsqueeze(1).to_broadcast(shape)
        for n in range(4):
            s, c = n // 2, n % 2
            for d in range(2):
                e = 2 * n + d
                a0, a1, a2, a3 = banks[d]
                dve.wait_ge(S["g_rows"], e + 1)
                after(v.tensor_copy(gcol[:, d], a3[:, 0:HEADS]))
                signal(v.tensor_tensor(decayT[:, d], by_head(a0), bc(gcol[:, d], shape), ALU.subtract), "g_diff")
            for d in range(2):
                e, half = 2 * n + d, (c if d == 0 else 1 - c)
                u = 2 * s + half
                a0, a1, a2, a3 = banks[d]
                dve.wait_ge(S["decay"], e + 1)
                after(v.tensor_tensor(amatT[:, d], by_head(a2), decayT[:, d], ALU.mult))
                signal(v.tensor_tensor(amatT[:, d], amatT[:, d], by_head(a1), ALU.mult), "at_ready")
                signal(v.tensor_tensor(begc[:, d], beta[:, u, 4 * d:4 * d + 4], egcol[:, d], ALU.mult), "dve_step")
                if s:
                    dve.wait_ge(S["qk_mm"], e - 3)
                    v.tensor_tensor(attnT[:, d], by_head(a3), decayT[:, d], ALU.mult)
            for l in range(LEVELS):
                for d in range(2):
                    a0, a1, a2, a3 = banks[d]
                    i = 2 * (LEVELS * n + l) + d
                    if l == 0:
                        dve.wait_ge(S["lvl_p"], i + 1)
                        v.tensor_tensor(tinv[:, d], eye, by_head(a0), ALU.subtract)
                        signal(v.tensor_tensor(tinvT[:, d], eye, lmask[:, d], ALU.subtract), "lvl_t")
                    else:
                        dve.wait_ge(S["lvl_tp"], 2 * ((LEVELS - 1) * n + l - 1) + d + 1)
                        dve.wait_ge(S["lvl_t"], i - 1)
                        if l < LEVELS - 1:
                            v.tensor_tensor(tinv[:, d], tinv[:, d], by_head(a1), ALU.subtract)
                        signal(v.tensor_tensor(tinvT[:, d], tinvT[:, d], by_head(a2), ALU.subtract), "lvl_t")
            for d in range(2):
                a0 = banks[d][0]
                if n:
                    dve.wait_ge(S["ks_mm"], 2 * (n - 1) + d + 1)
                    dve.wait_ge(S["g_pool"], 2 * n + d + 1)
                    dve.wait_ge(S["dve_step"], count["dve_step"])
                    after(v.tensor_tensor(pmat[:, d], by_head(a0), bc(begc[:, d], shape), ALU.mult))
                    signal(v.tensor_tensor(xmat[:, d], xmat[:, d], pmat[:, d], ALU.subtract), "x_ready")
            for d in range(2):
                e, half = 2 * n + d, (c if d == 0 else 1 - c)
                a2, a3 = banks[d][2:]
                if s:
                    dve.wait_ge(S["o_mm"], 2 * (n - 2) + d + 1)
                    out = oT[:, :, P * half:P * half + P]
                    if c == 0:
                        signal(v.tensor_copy(out, by_head(a2)), "o_ready")
                    else:
                        dve.wait_ge(S["o_ready"], 2)
                        signal(v.tensor_tensor(out, out, by_head(a2), ALU.add), "o_ready")
                if n < 3:
                    dve.wait_ge(S["ds_mm"], e + 1)
                    if n == 0:
                        signal(v.tensor_copy(state[:, d], by_head(a3)), "s_ready")
                    else:
                        after(v.tensor_tensor(pmat[:, d], state[:, d], bc(egl[:, d], shape), ALU.mult))
                        signal(v.tensor_tensor(state[:, d], pmat[:, d], by_head(a3), ALU.add), "s_ready")

        for b in range(2):
            dve.wait_ge(S["o_rstd"], b + 1)
            o = wk("oT", 512, 512 * b)
            after(v.scalar_tensor_tensor(o, o, par("g_gdn"), bank[6 + b][:], ALU.mult, ALU.mult))
            for i in range(2):
                h = 2 * b + i
                signal(v.tensor_tensor(cat[:, 4 + h], oT[:, h], zs[:, h], ALU.mult), "cat_ready")

        residual(lambda k: gains[:, 3, k:k + 1])
        scaled(hT, lambda k: gains[:, 2, k:k + 1], "xn_scaled")

        def gated(f):
            n = USE["up"] + f
            dve.wait_ge(S["ffn_silu"], f + 1)
            free(v.tensor_tensor(prod[:, f], bank[n % BANKS][:, 0:SEQ], sgate[:, f % 2], ALU.mult), n)

        for f in range(FT):
            x = full(USE["up"] + f)[:, SEQ:2 * SEQ].rearrange("p (r c) -> p r c", r=ROWS)
            o = acc[:, f % 4].rearrange("p (r c) -> p r c", r=ROWS)
            after(v.tensor_scalar(o, x, par("w_dwc", 9 * f + 4, 1), None, ALU.mult))
            taps = [(dy, dx) for dy in (-1, 0, 1) for dx in (-1, 0, 1) if (dy, dx) != (0, 0)]
            for dy, dx in taps:
                r0, r1, c0, c1 = max(0, -dy), ROWS - max(0, dy), max(0, -dx), GRID_W - max(0, dx)
                dst = o[:, r0:r1, c0:c1]
                ins = v.scalar_tensor_tensor(dst, x[:, r0 + dy:r1 + dy, c0 + dx:c1 + dx],
                                             par("w_dwc", 9 * f + 3 * (dy + 1) + dx + 1, 1), dst, ALU.mult, ALU.add)
                if (dy, dx) == taps[-1]:
                    signal(ins, "ffn_conv")
                else:
                    after(ins)
            if f:
                gated(f - 1)
        gated(FT - 1)
        residual(lambda k: gains[:, 4, k:k + 1])

        scaled(hT, lambda k: par("norm_mix", k, 1))
        for j in range(KT):
            n = USE["in_a"] + 3 * (j // 2) + j % 2
            x = full(n)
            dve.wait_ge(S["c_sb"], j + 1)
            ins = v.tensor_tensor(ch[:, j % 2], c_sb[:, j % 2], x[:, SEQ:2 * SEQ], ALU.mult)
            free(ins, n)
            released(dve, n)
            after(conv3(None, cu[:, j % 4], ch[:, j % 2], lambda i: par("conv_a", 3 * j + i, 1)))
            if j % 2:
                n = USE["in_a"] + 3 * (j // 2) + 2
                x = full(n)
                for i in range(2):
                    m = j - 1 + i
                    ins = v.tensor_tensor(yT[:, m], x[:, SEQ * i:SEQ * i + SEQ], cu[:, m % 4], ALU.mult)
                free(ins, n)

        def add_output(stage):
            for b in range(4):
                n = USE[stage] + b
                x = full(n)
                pair = slice(2 * b, 2 * b + 2)
                free(v.tensor_tensor(hT[:, pair], hT[:, pair], x[:].rearrange("p (k t) -> p k t", k=2), ALU.add), n)

        add_output("out_a")

        def moe(layer):
            done, extra = layer * PAIRS, layer * (PAIRS + 1)
            scaled(hT, lambda k: par("norm_ffn", 8 * layer + k, 1))
            for m in (1, 3):
                dve.wait_ge(S["tok_mm"], 4 * layer + m + 1)
                signal(v.tensor_copy(xtok[:, m // 2, 512:1024], bank[m][:]), "tok_sb2")
            signal(v.memset(ysb[:, 0:512], 0.0), "y_act")
            signal(v.memset(ysb[:, 512:1024], 0.0), "y_dve")
            signal(v.memset(pwt, 0.0), "pwt_sb")
            v.memset(rt(0, 8), -3e38)
            v.memset(wgt, 0.0)
            after(v.memset(rankm, -1.0))
            iota = con("iota")
            dve.wait_ge(S["lg_cols"], layer + 1)
            bias = par("b_router", 36 * layer, 36).unsqueeze(1).to_broadcast([P, NH, 36])
            after(v.tensor_tensor(lg, bank[6][:, 0:72].rearrange("p (u c) -> p u c", u=NH), bias, ALU.add))
            g8, gm, gi, oneg, let, les, em, ei = (rt(a, n) for a, n in (
                (0, 8), (16, 8), (32, 8), (64, 4), (72, 32), (136, 8), (152, 8), (168, 8)))
            after(v.tensor_copy(g8[:, :, 0:N_GROUPS], lg[:, :, 0:N_GROUPS]))
            for u in range(NH):
                last = v.max(gm[:, u], g8[:, u])
            after(last)
            signal(v.tensor_scalar(rt(50, 1), gm[:, :, 0:1], -1.0, None, ALU.mult), "route_dve")
            for u in range(NH):
                last = v.max_index(gi[:, u].bitcast(U32), gm[:, u], g8[:, u])
            after(last)
            gif = rt(48, 1)
            after(v.tensor_copy(gif, gi.bitcast(U32)[:, :, 0:1]))
            after(v.tensor_tensor(oneg, iota[:, 0:N_GROUPS].unsqueeze(1).to_broadcast([P, NH, N_GROUPS]),
                                  gif.to_broadcast([P, NH, N_GROUPS]), ALU.is_equal))
            for u in range(NH):
                last = v.tensor_tensor(let[:, u].rearrange("p (e g) -> p e g", g=N_GROUPS),
                                       lg[:, u, N_GROUPS:].rearrange("p (g e) -> p e g", g=N_GROUPS),
                                       oneg[:, u].unsqueeze(1).to_broadcast([P, PER_GROUP, N_GROUPS]), ALU.mult)
            after(last)
            after(v.reduce_sum(les, let.rearrange("p u (e g) -> p u e g", g=N_GROUPS), axis=AX))
            for u in range(NH):
                last = v.max(em[:, u], les[:, u])
            after(last)
            signal(v.tensor_tensor(rt(188, 1), em[:, :, 1:2], em[:, :, 0:1], ALU.subtract), "route_dve")
            for u in range(NH):
                last = v.max_index(ei[:, u].bitcast(U32), em[:, u], les[:, u])
            after(last)
            eif = rt(184, 2)
            after(v.tensor_copy(eif, ei.bitcast(U32)[:, :, 0:2]))
            picked = rt(200, 2)
            after(v.scalar_tensor_tensor(picked, gif.to_broadcast([P, NH, 2]), float(PER_GROUP), eif, ALU.mult, ALU.add))
            m1, m2, m12 = rt(304, E), rt(368, E), rt(240, E)
            for i, m in enumerate((m1, m2)):
                last = v.tensor_tensor(m, iota[:, 0:E].unsqueeze(1).to_broadcast([P, NH, E]),
                                       picked[:, :, i:i + 1].to_broadcast([P, NH, E]), ALU.is_equal)
            after(last)
            signal(v.tensor_tensor(m12, m1, m2, ALU.add), "mask_ready")
            dve.wait_ge(S["route_act"], 2 * layer + 2)
            v.reciprocal(rt(62, 1), rt(60, 1))
            after(v.tensor_scalar(rt(192, 1), rt(190, 1), 1.0, None, ALU.add))
            after(v.reciprocal(rt(194, 1), rt(192, 1)))
            after(v.tensor_tensor(rt(196, 1), rt(194, 1), rt(62, 1), ALU.mult))
            after(v.tensor_tensor(rt(198, 1), rt(196, 1), rt(190, 1), ALU.mult))
            v.tensor_tensor(m1, m1, rt(196, 1).to_broadcast([P, NH, E]), ALU.mult)
            after(v.tensor_tensor(m2, m2, rt(198, 1).to_broadcast([P, NH, E]), ALU.mult))
            after(v.tensor_tensor(wgt[:, :, 0:E], m1, m2, ALU.add))
            dve.wait_ge(S["rank_mm"], layer + 1)
            ranks = bank[5][:, 0:2 * E].rearrange("p (u e) -> p u e", u=NH)
            after(v.scalar_tensor_tensor(rankm[:, :, 0:E], ranks, 1.0, m12, ALU.add, ALU.mult))
            after(v.tensor_scalar(rankm[:, :, 0:E], rankm[:, :, 0:E], -1.0, None, ALU.add))
            after(v.reduce_max(rt(496, 1)[:, 0], bank[5][:, 2 * E:3 * E], axis=AX))
            after(v.scalar_tensor_tensor(wov, rankm[:, :, 0:E], float(SLOTS), wgt[:, :, 0:E], ALU.is_ge, ALU.mult))
            signal(v.tensor_scalar(flag[:], rt(496, 1)[:, 0], float(SLOTS), None, ALU.is_gt), "route_ready")
            signal(v.memset(rt(600, 1), 0.0), "scat_add")
            signal(v.memset(rt(602, 1), 0.0), "pwt_mm")

            def select(pair):
                for u in range(NH):
                    last = v.tensor_tensor(oneh[:, u], iota.unsqueeze(1).to_broadcast([P, 2, SLOTS]),
                                           bc(rankm[:, u, bass.ds(pair * 2, 2)], [P, 2, SLOTS]), ALU.is_equal)
                last.then_inc(S["onehot"], 1)

            def take():
                v.tensor_copy(xg[:, 4:8], bank[3][:].rearrange("p (k s) -> p k s", k=4)).then_inc(S["xg_dve"], 1)

            def add(i):
                base = layer * (4 * PAIRS + 5) + 1
                dve.wait_ge(S["scat_add"], i * 4 + base)
                for q in range(4):
                    dve.wait_ge(S["scat_mm"], i * 4 + layer * (4 * PAIRS + 4) + q + 1)
                    pair = slice(2 * q, 2 * q + 2)
                    v.tensor_tensor(hT[:, pair], hT[:, pair], bank[(5, 2, 3, 5)[q]][:].rearrange("p (k t) -> p k t", k=2), ALU.add)\
                        .then_inc(S["scat_add"], 1)

            select(0)
            dve.wait_ge(S["gather_mm"], extra + 1)
            take()
            with dve.Fori(0, PAIRS) as i:
                dve.wait_ge(S["gather_mm"], i + extra + 1)
                dve.wait_ge(S["onehot_w"], i + done + 1)
                select(i + 1)
                dve.wait_ge(S["sg_sb"], i + done + 1)
                dve.wait_ge(S["up_mm"], i + done + 1)
                v.tensor_tensor(hh, sg, bank[1][:], ALU.mult).then_inc(S["hh_sb"], 1)
                dve.wait_ge(S["gather_mm"], i + extra + 2)
                take()
                add(i)
                dve.wait_ge(S["down_mm"], i * 2 + 2 * done + 2)
                v.tensor_copy(ysb[:, 512:1024], bank[7][:]).then_inc(S["y_dve"], 1)
            add(PAIRS)
            dve.wait_ge(S["scat_add"], (layer + 1) * (4 * PAIRS + 5))

            over = dve.value_load(flag[0:1, 0:1], min_val=0, max_val=1)
            with dve.If(over > 0):
                v.memset(rt(604, 1), 0.0).then_inc(S[f"ov_down{layer}"], 1)
                v.memset(rt(606, 1), 0.0).then_inc(S[f"ov_add{layer}"], 1)
                with dve.Fori(0, E) as e:
                    for u in range(NH):
                        dve.wait_ge(S[f"ov_sg{layer}"], e * 2 + u + 1)
                        v.scalar_tensor_tensor(hh, sg, wov[:, u, bass.ds(e, 1)], bank[1][:], ALU.mult, ALU.mult)\
                            .then_inc(S[f"ov_hh{layer}"], 1)
                        dve.wait_ge(S[f"ov_down{layer}"], e * 2 + u + 2)
                        dve.wait_ge(S[f"ov_add{layer}"], e * 2 + u + 1)
                        for b in range(2):
                            x = hT[:, 4 * b:4 * b + 4, P * u:P * u + P]
                            last = v.tensor_tensor(x, x, bank[6 + b][:].rearrange("p (k t) -> p k t", k=4), ALU.add)
                        last.then_inc(S[f"ov_add{layer}"], 1)
                dve.wait_ge(S[f"ov_add{layer}"], 2 * E + 1)
                v.memset(rt(608, 1), 0.0)
            v.memset(rt(610, 1), 0.0).then_inc(S["moe_done"], 1)

        def ple(layer):
            scaled(hT, lambda k: par("norm_ple", 8 * layer + k, 1))
            for b in range(4):
                n = USE[f"ple{layer}"] + 2 * b
                x = full(n + 1)
                released(dve, n)
                pair = slice(2 * b, 2 * b + 2)
                g = gsb[:, pair]
                free(v.tensor_tensor(g, g, x[:].rearrange("p (k t) -> p k t", k=2), ALU.mult), n + 1)
                released(dve, n + 1)
                signal(v.tensor_tensor(hT[:, pair], hT[:, pair], g, ALU.add), "h_ready")

        moe(0)
        ple(0)

        x = par("lam")
        signal(v.scalar_tensor_tensor(nlt[1], x, -1.0, x, ALU.mult, ALU.max), "lru_log")
        scaled(hT, lambda k: par("norm_mix", 8 + k, 1))
        dve.wait_ge(S["lru_exp"], 1)
        log1p(nlt[2], nlt[1], nlt[3:5])
        after(v.tensor_scalar(nlt[0], par("lam"), -1.0, 0.0, ALU.mult, ALU.max))
        after(v.tensor_tensor(nlt[0], nlt[0], nlt[2], ALU.add))
        after(v.tensor_scalar(nls, nlt[0], -RG_C, None, ALU.mult))
        for b in range(4):
            n = USE["in_b"] + b
            p = full(n)
            for i in range(2):
                j = 2 * b + i
                x, o = p[:, SEQ * i:SEQ * i + SEQ], uu[:, j]
                after(v.tensor_scalar(o, x, par("conv_b", 4 * j + 2, 1), par("conv_bias", j, 1), ALU.mult, ALU.add))
                after(v.scalar_tensor_tensor(o[:, 1:], x[:, :SEQ - 1], par("conv_b", 4 * j + 1, 1), o[:, 1:], ALU.mult, ALU.add))
                after(v.scalar_tensor_tensor(o[:, 2:], x[:, :SEQ - 2], par("conv_b", 4 * j, 1), o[:, 2:], ALU.mult, ALU.add))
                last = v.scalar_tensor_tensor(o[:, :SEQ - 1], x[:, 1:], par("conv_b", 4 * j + 3, 1), o[:, :SEQ - 1], ALU.mult, ALU.add)
            free(last, n)
        for d in range(2):
            for j in range(KT):
                released(dve, USE["gates"] + KT * d + j)
                signal(v.tensor_scalar(rr[d][:, j], rr[d][:, j], nls[:, 8 * d + j:8 * d + j + 1], None, ALU.mult), "lru_log")
                last = v.tensor_tensor(gi[d][:, j], gi[d][:, j], uu[:, j], ALU.mult)
        after(last)
        for d in range(2):
            dve.wait_ge(S["lru_exp"], 2 * d + 2)
            signal(v.scalar_tensor_tensor(th[d], a_sq[d], 1.0, th[d], ALU.add, ALU.mult), "lru_var")
        for d in range(2):
            dve.wait_ge(S["lru_sqrt"], d + 1)
            dve.wait_ge(S["lru_exp"], 2 * d + 3)
            after(v.tensor_tensor(th[d], th[d], gi[d], ALU.mult))
            if d == 0:
                for j in range(KT):
                    last = v.tensor_tensor_scan(gi[0][:, j], rr[0][:, j], th[0][:, j], 0.0, ALU.mult, ALU.add)
        back = slice(None, None, -1)
        for i in range(KT + 2):
            before = count["dve_step"]
            if i < KT:
                signal(v.tensor_tensor_scan(gi[1][:, i, back], rr[1][:, i, back], th[1][:, i, back], 0.0, ALU.mult, ALU.add),
                       "dve_step")
            dve.wait_ge(S["dve_step"], before)
            if 1 <= i <= KT:
                signal(v.tensor_tensor(rr[0][:, i - 1], gi[0][:, i - 1], gi[1][:, i - 1], ALU.add), "dve_step")
            if i >= 2:
                signal(v.tensor_tensor(rr[0][:, i - 2], rr[0][:, i - 2], yg[:, i - 2], ALU.mult), "lru_h")
        add_output("out_b")
        moe(1)
        ple(1)
        roots()
        for k in range(KT):
            last = v.scalar_tensor_tensor(yT[:, k], hT[:, k], par("norm_final", k, 1), rstd, ALU.mult, ALU.mult)
        signal(last, "fin_ready")

    ctx_block.__exit__(None, None, None)


def tiles(w):
    k, n = w.shape
    return np.ascontiguousarray(w.reshape(k // P, P, n).transpose(1, 0, 2))


def columns(v):
    v = v.reshape(-1, P)
    return np.ascontiguousarray(v.T)


def constants():
    i = np.arange(P)
    sel = np.zeros((P, P), np.float32)
    for j in range(4):
        sel[32 * j, 0] = sel[32 * j + 1, 1] = 1.0
    parts = {
        "ident": np.eye(P), "upper": np.triu(np.ones((P, P))), "lower": np.tril(np.ones((P, P))),
        "strict": np.triu(np.ones((P, P)), 1), "ones": np.ones((P, P)), "sel": sel,
        "iota": np.broadcast_to(np.arange(SLOTS), (P, SLOTS)), "eps": np.full((P, 1), EPS),
    }
    consts = np.concatenate([parts[n].reshape(P, -1) for n in CONSTS], 1).astype(np.float32)
    neg = np.stack([np.where(i[None, :] >= i[:, None], 0.0, NEG), np.where(i[None, :] <= i[:, None], 0.0, NEG)], 1)
    level = []
    for l in range(LEVELS):
        size = 1 << l
        b = i // size
        level.append((b[:, None] // 2 == b[None, :] // 2) & (b[:, None] != b[None, :]))
    masks = np.concatenate([neg.reshape(P, -1), np.stack(level, 1).reshape(P, -1)], 1).astype(np.float32)
    c = 2 * np.pi * np.outer(i, i) / P
    l = 2 * np.pi * np.outer(np.arange(SEQ), np.arange(SEQ)) / SEQ
    norm = 1.0 / math.sqrt(P * SEQ)
    dft = {"cos_c": np.cos(c), "nsin_c": -np.sin(c), "cos_l": tiles(np.cos(l) * norm), "sin_l": tiles(np.sin(l) * norm)}
    return consts, masks, {k: v.reshape(P, -1).astype(np.float32) for k, v in dft.items()}


_ORDER = ["x", "ctx", "p", "params", "consts", "masks", "dense", "w_gate", "w_up", "w_down"]


def kernel(**inputs):
    import concourse.bacc as bacc
    from concourse.bass_utils import run_bass_kernel_spmd

    a = {k: np.asarray(v) for k, v in inputs.items()}
    consts, masks, dft = constants()
    each = lambda v: np.broadcast_to(v.reshape(1, -1), (P, v.size))
    w_in, conv = a["w_in"][0], a["w_qkv_conv"][0]
    both = np.stack([a["c"][0], a["c_ctx"]], 1)
    parts = {
        "c": tiles(both), "b_ada": columns(a["b_ada"]), "g_pre_mix": columns(a["g_pre_mix"]),
        "g_post_mix": columns(a["g_post_mix"]), "g_pre_ffn": columns(a["g_pre_ffn"]),
        "g_post_ffn": columns(a["g_post_ffn"]), "w_ab": tiles(w_in[:, 2560:]),
        "conv": conv.reshape(3, 12, P).transpose(2, 1, 0), "a_log": each(a["a_log"]), "dt_bias": each(a["dt_bias"]),
        "g_gdn": columns(a["g_gdn"]), "w_dwc": a["w_dwc"].reshape(9, FT, P).transpose(2, 1, 0),
        "norm_mix": columns(a["norm_mix_2"]), "conv_a": a["conv_a_2"].reshape(3, KT, P).transpose(2, 1, 0),
        "conv_b": a["conv_b_2"].reshape(4, KT, P).transpose(2, 1, 0), "conv_bias": columns(a["conv_bias_b_2"]),
        "b_rg": columns(a["b_rgate_b_2"]), "b_ig": columns(a["b_igate_b_2"]), "lam": columns(a["lam_b_2"]),
        "norm_ffn": columns(a["norm_ffn_2"]), "norm_ple": columns(a["norm_ple_2"]), "b_ple": columns(a["b_ple_gate_2"]),
        "norm_final": columns(a["norm_final_2"]),
        "w_router": np.stack([tiles(np.concatenate([a["w_router_group_2"][l], a["w_router_expert_2"][l]], 1))
                              for l in range(2)], 1),
        "b_router": each(np.concatenate([a["b_router_group_2"], a["b_router_expert_2"]], 1)),
    }
    params = np.concatenate([parts[n].reshape(P, -1) for n in PARAMS], 1)
    assert params.shape == (P, PARAMS_N) and consts.shape == (P, CONSTS_N) and masks.shape == (P, MASKS_N)
    dft["w_f"] = a["w_fourier"][0].transpose(1, 0, 2).reshape(P, -1)

    def chunks(w, width=512):
        return [tiles(w[:, n:n + width]).reshape(P, -1) for n in range(0, w.shape[1], width)]

    def tile_order(w, order):
        return np.concatenate([w[:, P * i:P * i + P] for i in order], 1)

    up_order = [i for f in range(FT) for i in (f, FT + f)]
    a_order = [i for j in range(0, KT, 2) for i in (KT + j, 2 * KT + j, KT + j + 1, 2 * KT + j + 1, j, j + 1)]
    gate_w = [a[n][0].reshape(8, 2, P, 256).transpose(2, 0, 1, 3).reshape(P, -1) for n in ("w_rgate_b_2", "w_igate_b_2")]
    ada = chunks(a["w_ada"][0])
    dense = ada[:4]
    dense += [c for n in (1024, 1536, 512, 2048, 0) for c in chunks(w_in[:, n:n + 512])]
    dense += [np.concatenate([dft[n] for n in FOURIER], 1)] + ada[4:]
    dense += chunks(a["w_out"][0]) + chunks(tile_order(a["w_up"][0], up_order)) + chunks(a["w_down"][0], P)
    dense += chunks(tile_order(a["w_in_a_2"][0], a_order)) + chunks(a["w_out_a_2"][0])
    dense += chunks(a["w_ple_gate_2"][0]) + chunks(a["w_ple_2"][0], D)
    dense += chunks(a["w_in_b_2"][0][:, D:]) + chunks(a["w_in_b_2"][0][:, :D]) + gate_w + chunks(a["w_out_b_2"][0])
    dense += chunks(a["w_ple_gate_2"][1]) + chunks(a["w_ple_2"][1], D)
    stream = np.zeros((len(dense), P, CHUNK), np.float32)
    for i, c in enumerate(dense):
        stream[i, :, :c.shape[1]] = c

    arrays = {
        "x": tiles(a["x"][0].T), "ctx": tiles(a["ctx"][0].T),
        "p": np.ascontiguousarray(np.stack([tiles(a["p_2"][l, 0].T) for l in range(2)], 1)),
        "params": np.ascontiguousarray(params), "consts": consts, "masks": masks, "dense": stream,
        "w_gate": a["w_exp_gate_2"], "w_up": a["w_exp_up_2"], "w_down": a["w_exp_down_2"],
    }
    nc = bacc.Bacc("TRN2", target_bir_lowering=False, num_devices=1)
    t = {n: nc.dram_tensor(f"in_{n}", list(arrays[n].shape), F32, kind="ExternalInput").ap() for n in _ORDER}
    t["out"] = nc.dram_tensor("out", [P, KT, SEQ], F32, kind="ExternalOutput").ap()
    build(nc, t)
    r = run_bass_kernel_spmd(nc, [{f"in_{n}": arrays[n] for n in _ORDER}], core_ids=[0])
    out = np.asarray(r.results[0]["out"])
    return np.ascontiguousarray(out.transpose(1, 0, 2).reshape(D, SEQ).T)[None]
```

```python
import math

import numpy as np
import concourse.bass as bass
from concourse import mybir

F32 = mybir.dt.float32
F32R = mybir.dt.float32r
I32 = mybir.dt.int32
U32 = mybir.dt.uint32
ALU = mybir.AluOpType
ACT = mybir.ActivationFunctionType
AX = mybir.AxisListType.X

P = 128
D = 1024
KT = D // P
SEQ = 256
NH = SEQ // P
HEADS = 4
DFF = 2816
FT = DFF // P
GRID_W = 64
ROWS = SEQ // GRID_W
EPS = 1e-6
RG_C = 8.0
N_GROUPS = 4
PER_GROUP = 8
E = N_GROUPS * PER_GROUP
DE = 512
SLOTS = 64
PAIRS = E // 2
RING = 6
LOAD_SLOTS = 4
CHUNK = 4096
LEVELS = 7
NEG = -1e30
LN_EXP, SILU, SIGMOID, GELU, EXP, SQRT = (
    f"{n}_and_others" for n in ("natural_log_exp", "silu", "sigmoid", "gelu_apprx_tanh", "exp", "sqrt"))
BANKS = 4
LOG1P = [1.0 / (2 * i + 1) for i in range(8)]


def layout(items):
    at, out = 0, {}
    for name, n in items:
        out[name] = (at, n)
        at += n
    return out, at


PARAMS, PARAMS_N = layout([
    ("c", 16), ("b_ada", 48), ("g_pre_mix", 8), ("g_post_mix", 8), ("g_pre_ffn", 8), ("g_post_ffn", 8),
    ("w_ab", KT * 16), ("conv", 12 * 3), ("a_log", 8), ("dt_bias", 8), ("g_gdn", 1), ("w_dwc", FT * 9),
    ("norm_mix", 16), ("conv_a", 8 * 3), ("conv_b", 8 * 4), ("conv_bias", 8), ("b_rg", 16), ("b_ig", 16),
    ("lam", 16), ("norm_ffn", 16), ("norm_ple", 16), ("b_ple", 16), ("norm_final", 8),
    ("w_router", 2 * KT * 36), ("b_router", 2 * 36),
])
CONSTS, CONSTS_N = layout([
    ("ident", P), ("upper", P), ("lower", P), ("strict", P), ("ones", P), ("sel", P), ("iota", SLOTS), ("eps", 1),
])
MASKS, MASKS_N = layout([("neg", 2 * P), ("level", LEVELS * P)])
FOURIER, FOURIER_N = layout([("cos_c", P), ("nsin_c", P), ("w_f", 4 * P), ("cos_l", 2 * SEQ), ("sin_l", 2 * SEQ)])

DENSE = [("ada0", 4, CHUNK), ("w_in", 5, CHUNK), ("fourier", 1, FOURIER_N), ("ada1", 4, CHUNK), ("ada2", 4, CHUNK), ("w_out", 2, CHUNK), ("w_up", 11, CHUNK),
         ("w_down", 8, FT * P), ("w_in_a", 6, CHUNK), ("w_out_a", 2, CHUNK), ("moe0", 0, 0), ("ple0", 2, CHUNK),
         ("ple_w0", 1, 2 * D), ("w_in_b", 4, CHUNK), ("gates", 2, CHUNK), ("w_out_b", 2, CHUNK), ("moe1", 0, 0),
         ("ple1", 2, CHUNK), ("ple_w1", 1, 2 * D)]
SPLIT = ("w_in", "w_out", "w_up", "w_down", "w_in_a", "w_out_a", "ple0", "w_in_b", "w_out_b", "ple1")
USES = [("ada0", 8), ("kv", 8), ("q", 2), ("z", 2), ("u", 2), ("dft_w", 2), ("vtok", 4), ("dft_b", 4),
        ("ada1", 8), ("dft_y", 2), ("ada2", 8), ("ktok", 4),
        ("w_out", 4), ("up", FT), ("down", 4), ("in_a", 12), ("out_a", 4), ("ple0", 8), ("in_b", 8), ("gates", 16),
        ("out_b", 4), ("ple1", 8)]


def plan():
    first, n, use, at = {}, 0, {}, 0
    for name, count, _ in DENSE:
        first[name] = n
        n += 6 * PAIRS if name.startswith("moe") else count
    for name, count in USES:
        use[name] = at
        at += count
    free = {}
    for stage in ("ada0", "ada1", "ada2"):
        for c in range(4):
            free[first[stage] + c] = ("dense_full", use[stage] + max(1, 2 * c))
    for c, last in enumerate((4, 8, 10, 12, 14)):
        free[first["w_in"] + c] = ("dense_full", use["kv"] + last)
    free[first["fourier"]] = ("dense_full", use["dft_y"] + 2)
    for stage, users, per, n_chunks in (("w_out", "w_out", 2, 2), ("w_up", "up", 2, 11), ("w_in_a", "in_a", 2, 6),
                                        ("w_out_a", "out_a", 2, 2), ("w_in_b", "in_b", 2, 4), ("w_out_b", "out_b", 2, 2)):
        for c in range(n_chunks):
            free[first[stage] + c] = ("dense_full", use[users] + per * (c + 1))
    for c in range(4):
        free[first["w_down"] + 2 * c] = ("down_half", c + 1)
        free[first["w_down"] + 2 * c + 1] = ("dense_full", use["down"] + c + 1)
    for c in range(2):
        free[first["gates"] + c] = ("dense_full", use["gates"] + 16)
    for layer in range(2):
        free[first[f"ple{layer}"]] = ("dense_full", use[f"ple{layer}"] + 3)
        free[first[f"ple{layer}"] + 1] = ("dense_full", use[f"ple{layer}"] + 7)
        free[first[f"ple_w{layer}"]] = ("dense_full", use[f"ple{layer}"] + 8)
        for c, (sem, per) in enumerate((("gate_mm", 1), ("gate_mm", 1), ("up_mm", 1), ("up_mm", 1), ("down_mm", 2), ("down_mm", 2))):
            for i in range(PAIRS):
                free[first[f"moe{layer}"] + 6 * i + c] = (sem, per * (layer * PAIRS + i + 1))
    slot, arrival, load_after, splits, high_slot, high_after = {}, {}, {}, [], {}, {}
    loads, until, turn = [0] * RING, {}, 0
    for name, count, _ in DENSE:
        moe = name.startswith("moe")
        for c in range(6 if moe else count):
            n = first[name] + c
            if moe:
                r = c
            elif name == "fourier":
                r = RING - 1
            else:
                r, turn = turn % LOAD_SLOTS, turn + 1
            slot[n], arrival[n], load_after[n] = r, 16 * (loads[r] + 1), until.get(r)
            own = moe and c < 2
            loads[r] += (PAIRS // 2 if own else PAIRS) if moe else 1
            until[r] = free[n + 6 * (PAIRS - (2 if own else 1))] if moe else free[n]
            if name in SPLIT:
                r = LOAD_SLOTS + len(splits) % 2
                high_slot[n], high_after[n] = r, until.get(r)
                until[r] = free[n]
                splits.append(n)
    by_dve = [first["w_down"] + c for c in range(2, 8)] + [first["w_in_a"]]
    low_done, made = {}, {"w_low": 0, "w_low_dve": 0}
    for n in splits:
        for half in range(2):
            name = "w_low_dve" if n in by_dve and half == 0 else "w_low"
            made[name] += 1
            low_done[n, half] = (name, made[name])
    return first, use, free, slot, arrival, load_after, splits, high_slot, high_after, by_dve, low_done


FIRST, USE, FREE, SLOT, ARRIVAL, LOAD_AFTER, SPLITS, HIGH_SLOT, HIGH_AFTER, BY_DVE, LOW_DONE = plan()
WORK, WORK_N = layout([
    ("kc", 2048), ("vc", 2048), ("qc", 1024), ("ktok", 2048), ("vtok", 2048), ("zs", 1024), ("cat", 2048),
    ("S", 1024), ("oT", 1024), ("masks", MASKS_N), ("dtmp", 4096), ("small", 328),
])
SEMAPHORES = [
    "param_load", "const_load", "ctx_load", "x_load", "mask_load", "p_load", "out_store",
    "zeroed", "c_cols", "dve_step", "act_step", 
    "sq_ready", "ss_ready", "rstd_ready", "xn_scaled", "xn_ready", "h_ready", "dense_full",
    "ab_mm", "ab_sb", "ab_cols", "ab_act", "ab_dve", "silu_ready",
    "qk_sq", "qk_ss", "qk_rstd", "qk_norm",
    "g_rows", "g_diff", "g_masked", "decay", "at_ready", "g_pool", "lvl_mask", "lvl_p", "lvl_p_sb", "lvl_tp", "lvl_t",
    "qk_mm", "ks_mm", "x_ready", "vn_mm", "vn_sb", "o_mm", "ds_mm", "s_ready", "o_ready",
    "o_sq", "o_ss", "o_rstd", "cat_ready", "ffn_conv", "ffn_silu", "c_sb",
    "tok_mm", "tok_sb", "mask_ready", "gates_ready", "lg_mm", "lg_sb", "lg_cols", "route_dve", "route_act", "rank_mm", "route_ready", 
    "onehot", "onehot_w", "gather_mm", "xg_act", "xg_dve", "gate_mm", "up_mm", "sg_sb", "hh_sb", "t_mm", "ht_sb",
    "down_mm", "y_act", "y_dve", "pwt_mm", "pwt_sb", "scat_mm", "scat_add", "moe_done",
    "lru_log", "lru_exp", "lru_var", "lru_sqrt", "lru_h", "fin_ready",
    "down_half", "w_high", "w_low", "w_low_dve", "x_high", "prod_ready", "y_ready", "cat_gated", "lru_mul", "lru_high",
] + [f"slot_full{r}" for r in range(RING)] + ["odd_full0", "odd_full1"] + [f"dense_free{b}" for b in range(BANKS)] \
  + [f"ov_{what}{layer}" for layer in range(2) for what in ("full", "gu", "sg", "hh", "t", "ht", "down", "add")]


def build(nc, t):
    S = {name: nc.alloc_semaphore(name) for name in SEMAPHORES}

    rounded = {}

    def both_ways(name, shape):
        tensor = nc.alloc_sbuf_tensor(name, shape, F32)
        at = nc.sbuf_base - 4 * int(np.prod(shape[1:]))
        rounded[tensor.name] = nc.alloc_sbuf_tensor_at(f"{name}_rounded", shape, F32R, offset=at)
        return tensor

    def rv(ap):
        return bass.AP(rounded[ap.tensor.name], ap.offset, ap.ap)

    ring = [both_ways(f"ring{r}", [P, CHUNK]) for r in range(RING)]
    bank = [nc.alloc_psum_tensor(f"bank{b}", [P, 512], F32) for b in range(8)]
    hT = nc.alloc_sbuf_tensor("hT", [P, KT, SEQ], F32)
    xn = both_ways("xn", [P, KT, 2, SEQ])
    params = both_ways("params", [P, PARAMS_N])
    consts = nc.alloc_sbuf_tensor("consts", [P, CONSTS_N], F32)
    work = both_ways("work", [P, WORK_N])
    mod = nc.alloc_sbuf_tensor("mod", [P, 48, 2], F32)
    gains = nc.alloc_sbuf_tensor("gains", [P, 5, KT], F32)
    w_abh = both_ways("w_abh", [P, KT * 16])
    flag = nc.alloc_sbuf_tensor("flag", [P, 1], I32)

    def par(name, a=0, size=None):
        at, n = PARAMS[name]
        return params[:, at + a:at + (n if size is None else a + size)]

    def con(name):
        at, n = CONSTS[name]
        return consts[:, at:at + n]

    def wk(name, size=None, off=0):
        at, n = WORK[name]
        return work[:, at + off:at + off + (size or n)]

    def flat(at, n):
        assert at + n <= WORK_N
        return work[:, at:at + n]

    ident, ones, strict = con("ident"), con("ones"), con("strict")
    cums = [con("upper"), con("lower")]

    kc = wk("kc").rearrange("p (h s t) -> p h s t", h=HEADS, s=2)
    vc = wk("vc").rearrange("p (h s t) -> p h s t", h=HEADS, s=2)
    qc = wk("qc").rearrange("p (h t) -> p h t", h=HEADS)
    ktok = wk("ktok").rearrange("p (u h d) -> p u h d", u=4, h=HEADS)
    vtok = wk("vtok").rearrange("p (u h d) -> p u h d", u=4, h=HEADS)
    ctxT = wk("ktok").rearrange("p (k t) -> p k t", k=KT)
    zs = wk("zs").rearrange("p (h t) -> p h t", h=HEADS)
    cat = wk("cat").rearrange("p (k t) -> p k t", k=KT)
    uT = wk("oT").rearrange("p (g t) -> p g t", g=4)
    state = wk("S").rearrange("p (d h e) -> p d h e", d=2, h=HEADS)
    oT = wk("oT").rearrange("p (h t) -> p h t", h=HEADS)
    neg = wk("masks", 2 * P).rearrange("p (d t) -> p d t", d=2)
    level = wk("masks", LEVELS * P, 2 * P).rearrange("p (l t) -> p l t", l=LEVELS)
    dtmp = wk("dtmp").rearrange("p (n d h t) -> p n d h t", n=4, d=2, h=HEADS)
    decayT, attnT, qd, kd = (dtmp[:, n] for n in range(4))
    tri = xn[:].rearrange("p k s t -> p (k s t)").rearrange("p (n d h t) -> p n d h t", n=4, d=2, h=HEADS)
    tinv, tinvT, pmat, amatT = (tri[:, n] for n in range(4))
    xv = wk("vc").rearrange("p (n d h t) -> p n d h t", n=2, d=2, h=HEADS)
    lmask, xmat = xv[:, 0], xv[:, 1]
    vnew = lmask
    sq2 = wk("dtmp").rearrange("p (k s t) -> p k s t", k=KT, s=2)
    sqk = wk("dtmp", 1024, 3072).rearrange("p (n t) -> p n t", n=2)
    ada_row = wk("cat", 1024, 1024).rearrange("p (m n) -> p m n", m=2)
    c_cols = wk("S", KT * 32).rearrange("p (k m) -> p k m", k=KT)
    ab_rows = wk("S", 512, 512)
    fo_w = wk("dtmp", 1024).rearrange("p (x n) -> p x n", x=2)
    fo_b = wk("dtmp", 2048, 1024).rearrange("p (x u g e) -> p x u g e", x=2, u=2, g=4)
    ab = wk("small", 64, 0).rearrange("p (u c) -> p u c", u=4)
    beta = wk("small", 32, 64).rearrange("p (u c) -> p u c", u=4)
    glog = wk("small", 32, 96).rearrange("p (u c) -> p u c", u=4)
    gtmp = [wk("small", 32, 128 + 32 * i).rearrange("p (u c) -> p u c", u=4) for i in range(5)]
    gcol = wk("small", 8, 288).rearrange("p (d h) -> p d h", d=2)
    egcol = wk("small", 8, 296).rearrange("p (d h) -> p d h", d=2)
    begc = wk("small", 8, 304).rearrange("p (d h) -> p d h", d=2)
    egl = wk("small", 8, 312).rearrange("p (d h) -> p d h", d=2)
    alog_e = wk("small", 8, 320)

    yT = flat(0, 2048).rearrange("p (k t) -> p k t", k=KT)
    xnT, sq1 = xn[:, :, 0], xn[:, :, 1]
    prod = flat(2048, FT * SEQ).rearrange("p (f t) -> p f t", f=FT)
    acc = flat(7680, 1024).rearrange("p (n t) -> p n t", n=4)
    sgate = flat(8704, 512).rearrange("p (n t) -> p n t", n=2)
    tmp = flat(9216, 1024).rearrange("p (n t) -> p n t", n=4)
    c_sb = flat(2048, 512).rearrange("p (n t) -> p n t", n=2)
    ch = flat(2560, 512).rearrange("p (n t) -> p n t", n=2)
    cu = flat(3072, 1024).rearrange("p (n t) -> p n t", n=4)
    xtok = flat(0, 2048).rearrange("p (u f) -> p u f", u=NH)
    xg = flat(2048, 1024).rearrange("p (k s) -> p k s", k=KT)
    sg, hh = flat(3072, 512), flat(3584, 512)
    hidT = flat(4096, 512).rearrange("p (j s) -> p j s", j=4)
    ysb = flat(4608, 1024)
    pwt = flat(5632, 256)
    oneh = flat(5888, 256).rearrange("p (u x s) -> p u x s", u=NH, x=2)
    onehw = flat(6144, 256).rearrange("p (u x s) -> p u x s", u=NH, x=2)
    lgT = flat(6400, 256)
    lg = flat(6656, 72).rearrange("p (u c) -> p u c", u=NH)
    EP = E + 2
    rankm = flat(7928, NH * EP).rearrange("p (u e) -> p u e", u=NH)
    wgt = flat(7996, NH * EP).rearrange("p (u e) -> p u e", u=NH)
    wov = flat(8064, NH * E).rearrange("p (u e) -> p u e", u=NH)

    def rt(at, n):
        return flat(6728 + at, NH * n).rearrange("p (u c) -> p u c", u=NH)

    gsb = flat(2048, 2048).rearrange("p (k t) -> p k t", k=KT)
    yg = flat(0, 2048).rearrange("p (k t) -> p k t", k=KT)
    uu = flat(2048, 2048).rearrange("p (k t) -> p k t", k=KT)
    rr, th, gi = ([flat(4096 + 2048 * (2 * i + d), 2048).rearrange("p (k t) -> p k t", k=KT) for d in range(2)]
                  for i in range(3))
    a_sq = [xn[:, :, d] for d in range(2)]
    nls = flat(17408, 16)
    nlt = [flat(17424 + 16 * i, 16) for i in range(5)]
    xh2 = wk("dtmp").rearrange("p (k s t) -> p k s t", k=KT, s=2)
    cath = wk("ktok").rearrange("p (k t) -> p k t", k=KT)
    prodh = flat(10240, FT * SEQ).rearrange("p (f t) -> p f t", f=FT)
    yh = flat(4096, 2048).rearrange("p (k t) -> p k t", k=KT)
    xh = sq1
    odd = [flat(8192 + CHUNK * x, CHUNK) for x in range(2)]
    pT = flat(16384, 1024).rearrange("p (l k t) -> p l k t", l=2, k=2)

    def arrived(eng, n):
        eng.wait_ge(S[f"slot_full{SLOT[n]}"], ARRIVAL[n])
        return ring[SLOT[n]]

    def parts_of(n):
        size = FT * P if FIRST["w_down"] <= n < FIRST["w_down"] + 8 else CHUNK
        return (0, size // 2), (size // 2, size)


    def released(eng, n):
        eng.wait_ge(S[f"dense_free{n % BANKS}"], n // BANKS + 1)

    ctx_block = nc.Block()
    block = ctx_block.__enter__()

    @block.sync
    def _(sp):
        def load(n, src, size):
            if LOAD_AFTER[n]:
                sem, value = LOAD_AFTER[n]
                sp.wait_ge(S[sem], value)
            sp.dma_start(ring[SLOT[n]][:, 0:size], src).then_inc(S[f"slot_full{SLOT[n]}"], 16)

        sp.dma_start(ctxT, t["ctx"]).then_inc(S["ctx_load"], 16)
        sp.dma_start(hT[:], t["x"]).then_inc(S["x_load"], 16)
        seen = 0
        for name, count, size in DENSE:
            base = FIRST[name]
            if not name.startswith("moe"):
                for c in range(count):
                    load(base + c, t["dense"][seen + c][:, 0:size], size)
                seen += count
                continue
            layer = int(name[3:])
            gate, up = (t[w][layer].rearrange("e (p j) f -> e p (j f)", j=KT) for w in ("w_gate", "w_up"))
            down = t["w_down"][layer].rearrange("e (p j) f -> e p (j f)", j=4)
            chunks = (gate, gate, up, up, down, down)
            def used(c, pair, back):
                sem, value = FREE[base + c]
                sp.wait_ge(S[sem], value + (pair - back) * (2 if c >= 4 else 1))

            def load_gates(pair, into, name):
                for c in range(2):
                    sp.dma_start(into[c], gate[pair * 2 + c]).then_inc(S[f"{name}{c}"], 16)

            def load_rest(pair):
                for c in range(2, 6):
                    used(c, pair, 1)
                    sp.dma_start(ring[c][:], chunks[c][pair * 2 + c % 2]).then_inc(S[f"slot_full{c}"], 16)

            order = sorted(range(6), key=lambda c: LOAD_AFTER[base + c][1])
            early = [c for c in order if layer and LOAD_AFTER[base + c][1] <= USE["out_b"]]
            for c in early:
                load(base + c, chunks[c][c % 2], CHUNK)
            sp.wait_ge(*((S["h_ready"], 2 * KT), (S["lru_h"], KT))[layer])
            load_gates(1, odd, "odd_full")
            for c in order[len(early):]:
                load(base + c, chunks[c][c % 2], CHUNK)
            load_rest(1)
            with sp.Fori(1, PAIRS // 2) as h:
                used(0, h * 2, 2)
                load_gates(h * 2, [ring[0][:], ring[1][:]], "slot_full")
                load_rest(h * 2)
                used(0, h * 2 + 1, 2)
                load_gates(h * 2 + 1, odd, "odd_full")
                load_rest(h * 2 + 1)
            sp.wait_ge(S["route_ready"], layer + 1)
            over = sp.value_load(flag[0:1, 0:1], min_val=0, max_val=1)
            with sp.If(over > 0):
                gate, up = (t[w][layer].rearrange("e (j p) f -> e p j f", p=P) for w in ("w_gate", "w_up"))
                down = t["w_down"][layer].rearrange("e (j p) f -> e p j f", p=P)
                with sp.Fori(0, E) as e:
                    sp.wait_ge(S[f"ov_down{layer}"], e * 2 + 1)
                    for c, (w, k) in enumerate(((gate, KT), (up, KT), (down, 4))):
                        sp.dma_start(ring[c][:].rearrange("p (j f) -> p j f", j=k), w[e]).then_inc(S[f"ov_full{layer}"], 16)
                sp.wait_ge(S[f"ov_down{layer}"], 2 * E + 1)
                sp.nop()
        sp.wait_ge(S["fin_ready"], 1)
        sp.dma_start(t["out"], yT).then_inc(S["out_store"], 16)
        sp.wait_ge(S["out_store"], 16)

    @block.tensor
    def _(pe):
        mm = nc.tensor.matmul
        count = {}

        def signal(ins, name):
            ins.then_inc(S[name], 1)
            count[name] = count.get(name, 0) + 1
            return count[name]

        def dense(n, tiles):
            if n >= BANKS:
                released(pe, n - BANKS)
            for a, b, products in tiles:
                for k, (w, x) in enumerate(products):
                    last = mm(bank[n % BANKS][:, a:b], w, x, start=k == 0, stop=k == len(products) - 1)
            assert signal(last, "dense_full") == n + 1

        def split_product(out, chunk, tile, x, k, n_k=KT, width=512):
            at = k * width + tile * P
            for j, (r, part) in enumerate(((HIGH_SLOT[chunk], 0), (HIGH_SLOT[chunk], 1), (SLOT[chunk], 0))):
                last = mm(out, rv(ring[r][:, at:at + P]), rv(x[part][k]), start=k == 0 and j == 0,
                          stop=k == n_k - 1 and j == 2)
            return last

        def split_arrived(chunk, k, n_k=KT):
            if k in (0, n_k // 2):
                name, value = LOW_DONE[chunk, 0 if k == 0 else 1]
                pe.wait_ge(S[name], value)

        def dense_split(use, tiles, x, ready=None, n_k=KT, width=512):
            if use >= BANKS:
                released(pe, use - BANKS)
            n = x[0][0].shape[-1]
            for i, (chunk, tile) in enumerate(tiles):
                for k in range(n_k):
                    split_arrived(chunk, k, n_k)
                    if ready and i == 0:
                        pe.wait_ge(S[ready[0]], ready[1] + k)
                    last = split_product(bank[use % BANKS][:, n * i:n * i + n], chunk, tile, x, k, n_k, width)
                if n_k == FT and i == 0:
                    signal(last, "down_half")
            assert signal(last, "dense_full") == use + 1

        def first_uses(uses, x, ready, step=None):
            n = x[0][0].shape[-1]
            for use, _ in uses:
                if use >= BANKS:
                    released(pe, use - BANKS)
            for k in range(KT):
                pe.wait_ge(S[ready[0]], ready[1] + k)
                if step:
                    step(k)
                for use, tiles in uses:
                    chunk, tile = tiles[0]
                    split_arrived(chunk, k)
                    last = split_product(bank[use % BANKS][:, 0:n], chunk, tile, x, k)
                    if k == KT - 1 and len(tiles) == 1:
                        assert signal(last, "dense_full") == use + 1
            for use, tiles in uses:
                if len(tiles) == 2:
                    chunk, tile = tiles[1]
                    for k in range(KT):
                        last = split_product(bank[use % BANKS][:, n:2 * n], chunk, tile, x, k)
                    assert signal(last, "dense_full") == use + 1

        def projection(stage, chunk, uses, x, ready):
            def tiles(b):
                return USE[stage] + b, [(FIRST[chunk] + b // 2, (2 * b + i) % 4) for i in range(2)]

            first_uses([tiles(0), tiles(1)], x, ready)
            for b in range(2, uses):
                dense_split(*tiles(b), x)

        def sum_squares():
            for k in range(KT):
                if k % 2 == 0:
                    pe.wait_ge(S["sq_ready"], 4 * (count.get("norms", 0) + 1) + k // 2 + 1)
                last = mm(bank[4][:, 0:SEQ], ones, sq1[:, k], start=k == 0, stop=k == KT - 1)
            signal(last, "ss_ready")
            count["norms"] = count.get("norms", 0) + 1

        n_normed = [1]

        pe.wait_ge(S["const_load"], 16)
        for k in range(KT):
            pe.wait_ge(S["sq_ready"], k // 2 + 1)
            last = mm(bank[4][:], ones, sq2[:, k].rearrange("p s t -> p (s t)"), start=k == 0, stop=k == KT - 1)
        signal(last, "ss_ready")

        pe.wait_ge(S["c_cols"], 1)

        def ada_rows(part, m):
            n = USE[f"ada{part}"] + max(0, 2 * m - 1)
            w = arrived(pe, FIRST[f"ada{part}"] + m)
            if n >= BANKS:
                released(pe, n - BANKS)
            for kk in range(2):
                for j in range(4):
                    k = 2 * j + kk
                    last = mm(bank[n % BANKS][32 * j:32 * j + 32, :], c_cols[:, k, :], w[:, 512 * k:512 * k + 512],
                              start=kk == 0, stop=kk == 1)
            assert signal(last, "dense_full") == n + 1

        def ada_columns(part, m):
            first = USE[f"ada{part}"]
            released(pe, first + max(0, 2 * m - 1))
            dense(first + min(2 * m + 2, 7), [
                (P * i, P * i + P, [(ada_row[:, m % 2, P * i:P * i + P], con("sel"))]) for i in range(4)])

        def ada_step(part, m):
            if m < 4:
                ada_rows(part, m)
            if m:
                ada_columns(part, m - 1)

        for m in range(5):
            ada_step(0, m)

        both = [[x[:, k].rearrange("p s t -> p (s t)") for k in range(KT)] for x in (xh2, xn)]
        w_ab = [w.rearrange("p (k c) -> p k c", k=KT) for w in (w_abh[:], par("w_ab"))]

        def ab_product(k):
            for j, (w, x) in enumerate(((0, 0), (0, 1), (1, 0))):
                last = mm(bank[7][0:16, :], rv(w_ab[w][:, k]), rv(both[x][k]), start=k == 0 and j == 0,
                          stop=k == KT - 1 and j == 2)
            if k == KT - 1:
                signal(last, "ab_mm")

        first_uses([(USE["kv"] + i, [(FIRST["w_in"], i)]) for i in range(2)], both, ("xn_ready", 1), ab_product)
        for i in range(2, 8):
            dense_split(USE["kv"] + i, [(FIRST["w_in"] + i // 4, i % 4)], both)
        pe.wait_ge(S["ab_sb"], 1)
        for u in range(4):
            last = nc.tensor.transpose(bank[6][:, 16 * u:16 * u + 16], ab_rows[0:16, P * u:P * u + P], ident[0:16, 0:16])
        signal(last, "ab_cols")
        x_lat = [[x[:, k, 1] for k in range(KT)] for x in (xh2, xn)]

        def four(stage, c):
            for b in range(2):
                dense_split(USE[stage] + b, [(FIRST["w_in"] + c, 2 * b + i) for i in range(2)], x_lat)

        four("q", 2)
        four("z", 3)
        four("u", 4)
        w_fourier = arrived(pe, FIRST["fourier"])

        def fo(name, a=0, n=None):
            at, size = FOURIER[name]
            return w_fourier[:, at + a:at + a + (n or size)]

        def token_major(stage, x):
            for u in range(4):
                s, half = u // 2, u % 2
                n = USE[stage] + u
                released(pe, n - BANKS)
                for h in range(HEADS):
                    last = nc.tensor.transpose(bank[n % BANKS][:, P * h:P * h + P], x[:, h, s, P * half:P * half + P], ident)
                assert signal(last, "dense_full") == n + 1

        def sums_qk(a):
            pe.wait_ge(S["qk_sq"], a + 1)
            if a >= 2:
                pe.wait_ge(S["qk_rstd"], a - 1)
            signal(mm(bank[4 + a % 2][:], ones, sqk[:, a % 2], start=True, stop=True), "qk_ss")

        for x, name in enumerate(("cos_c", "nsin_c")):
            dense(USE["dft_w"] + x, [(0, 512, [(fo(name), fo("w_f"))])])
        pe.wait_ge(S["silu_ready"], 8)
        token_major("vtok", vc)
        released(pe, USE["dft_w"])
        released(pe, USE["dft_w"] + 1)
        for x in range(2):
            for u in range(NH):
                dense(USE["dft_b"] + 2 * x + u, [
                    (P * g, P * g + P, [(uT[:, g, P * u:P * u + P], fo_w[:, x, P * g:P * g + P])]) for g in range(4)])
        for m in range(5):
            if m < 4:
                sums_qk(m)
            ada_step(1, m)
        for b in range(4):
            released(pe, USE["dft_b"] + b)
        for b in range(2):
            dense(USE["dft_y"] + b, [
                (SEQ * i, SEQ * i + SEQ, [(fo_b[:, x, u, 2 * b + i], fo(("cos_l", "sin_l")[x], SEQ * u, SEQ))
                                          for x in range(2) for u in range(NH)]) for i in range(2)])
        for m in range(5):
            if m < 2:
                sums_qk(4 + m)
            ada_step(2, m)
        pe.wait_ge(S["qk_norm"], 6)
        token_major("ktok", kc)

        banks = [[bank[0], bank[1], bank[4], bank[5]], [bank[2], bank[3], bank[6], bank[7]]]
        for u in range(4):
            released(pe, USE["ktok"] + u)
        pe.wait_ge(S["gates_ready"], 1)

        def heads(out, left, right, start=True, stop=True):
            for h in range(HEADS):
                last = mm(out[:, P * h:P * h + P], left(h), right(h), start=start, stop=stop)
            return last

        for n in range(4):
            s, c = n // 2, n % 2
            for d in range(2):
                half, e = (c if d == 0 else 1 - c), 2 * n + d
                a0, a1, a2, a3 = banks[d]
                token = slice(P * half, P * half + P)
                u = 2 * s + half
                if n >= 2:
                    pe.wait_ge(S["x_ready"], 2 * (n - 2) + d + 1)
                heads(a0, lambda h: glog[:, u, 4 * d + h:4 * d + h + 1].to_broadcast([P, P]), lambda h: cums[d])
                heads(a1, lambda h: beta[:, u, 4 * d + h:4 * d + h + 1].to_broadcast([P, P]), lambda h: ident)
                if n == 3:
                    pe.wait_ge(S["o_ready"], d + 1)
                heads(a2, lambda h: kc[:, h, s, token], lambda h: kc[:, h, s, token])
                if n:
                    pe.wait_ge(S["s_ready"], e - 1)
                signal(mm(a3[:, 0:HEADS], cums[d], glog[:, u, 4 * d:4 * d + 4], start=True, stop=True), "g_rows")
            for d in range(2):
                half, e = (c if d == 0 else 1 - c), 2 * n + d
                a0, a1, a2, a3 = banks[d]
                token = slice(P * half, P * half + P)
                if s:
                    pe.wait_ge(S["g_diff"], e + 1)
                    signal(heads(a3, lambda h: kc[:, h, s, token], lambda h: qc[:, h, token]), "qk_mm")
            for l in range(LEVELS):
                for d in range(2):
                    half, e = (c if d == 0 else 1 - c), 2 * n + d
                    a0, a1, a2, a3 = banks[d]
                    i = 2 * (LEVELS * n + l) + d
                    pe.wait_ge(S["lvl_mask"], i + 1)
                    if l:
                        pe.wait_ge(S["lvl_t"], i - 1)
                        signal(heads(a0, lambda h: lmask[:, d, h], lambda h: tinv[:, d, h]), "lvl_p")
                    else:
                        pe.wait_ge(S["decay"], e + 1)
                        signal(heads(a0, lambda h: lmask[:, d, h], lambda h: ident), "lvl_p")
                for d in range(2):
                    a0, a1, a2, a3 = banks[d]
                    i = 2 * (LEVELS * n + l) + d
                    if l:
                        pe.wait_ge(S["lvl_p_sb"], 2 * ((LEVELS - 1) * n + l - 1) + d + 1)
                        if l < LEVELS - 1:
                            heads(a1, lambda h: tinvT[:, d, h], lambda h: pmat[:, d, h])
                        signal(heads(a2, lambda h: pmat[:, d, h], lambda h: tinvT[:, d, h]), "lvl_tp")
            for d in range(2):
                half, e = (c if d == 0 else 1 - c), 2 * n + d
                a0 = banks[d][0]
                token = slice(P * half, P * half + P)
                if n:
                    signal(heads(a0, lambda h: kc[:, h, s, token], lambda h: state[:, d, h]), "ks_mm")
            for d in range(2):
                a1 = banks[d][1]
                pe.wait_ge(S["lvl_t"], 2 * (LEVELS * n + LEVELS - 1) + d + 1)
                if n:
                    pe.wait_ge(S["x_ready"], 2 * (n - 1) + d + 1)
                else:
                    pe.wait_ge(S["g_pool"], d + 1)
                signal(heads(a1, lambda h: tinvT[:, d, h], lambda h: xmat[:, d, h]), "vn_mm")
            for d in range(2):
                half, e = (c if d == 0 else 1 - c), 2 * n + d
                a2, a3 = banks[d][2:]
                pe.wait_ge(S["vn_sb"], e + 1)
                pe.wait_ge(S["g_pool"], e + 1)
                if s:
                    for h in range(HEADS):
                        mm(a2[:, P * h:P * h + P], state[:, d, h], qd[:, d, h], start=True, stop=False)
                        last = mm(a2[:, P * h:P * h + P], vnew[:, d, h], attnT[:, d, h], start=False, stop=True)
                    signal(last, "o_mm")
                if n < 3:
                    signal(heads(a3, lambda h: kd[:, d, h], lambda h: vnew[:, d, h]), "ds_mm")

        for b in range(2):
            pe.wait_ge(S["o_sq"], b + 1)
            signal(mm(bank[4 + b][:], ones, sqk[:, b], start=True, stop=True), "o_ss")
        projection("w_out", "w_out", 4, [[x[:, k] for k in range(KT)] for x in (cath, cat)], ("cat_ready", 1))

        xs = [xnT[:, k] for k in range(KT)]
        xparts = [[x[:, k] for k in range(KT)] for x in (xh, xnT)]

        def norm_input():
            sum_squares()
            n_normed[0] += 1
            return "xn_ready", KT * (n_normed[0] - 1) + 1

        sum_squares()
        ready = norm_input()
        projection("up", "w_up", FT, xparts, ready)
        for b in range(4):
            dense_split(USE["down"] + b, [(FIRST["w_down"] + 2 * b + i, 0) for i in range(2)],
                        [[x[:, k] for k in range(FT)] for x in (prodh, prod)], None if b else ("prod_ready", 1), FT, P)
        sum_squares()
        ready = norm_input()
        projection("in_a", "w_in_a", 12, xparts, ready)
        projection("out_a", "w_out_a", 4, [[x[:, k] for k in range(KT)] for x in (yh, yT)], ("y_ready", 1))

        def moe(layer):
            ready = norm_input()
            w_r = par("w_router").rearrange("p (l k c) -> p l k c", l=2, k=KT)
            for k in range(KT):
                pe.wait_ge(S[ready[0]], ready[1] + k)
                last = mm(bank[7][0:36, 0:SEQ], w_r[:, layer, k], xs[k], start=k == 0, stop=k == KT - 1)
            signal(last, "lg_mm")
            for b in range(BANKS):
                released(pe, moe.last_use[layer] - b)

            def tokens(m):
                for i in range(4):
                    last = nc.tensor.transpose(bank[m][:, P * i:P * i + P],
                                               xnT[:, 4 * (m % 2) + i, P * (m // 2):P * (m // 2) + P], ident)
                signal(last, "tok_mm")

            tokens(0)
            pe.wait_ge(S["lg_sb"], layer + 1)
            for u in range(NH):
                last = nc.tensor.transpose(bank[6][:, 36 * u:36 * u + 36], lgT[0:36, P * u:P * u + P], ident[0:36, 0:36])
            signal(last, "lg_cols")
            for m in range(1, 4):
                tokens(m)
            pe.wait_ge(S["mask_ready"], layer + 1)
            m0, m1 = rt(240, E)[:, 0], rt(240, E)[:, 1]
            mm(bank[5][:, 0:E], strict, m0, start=True, stop=True)
            mm(bank[5][:, E:2 * E], ones, m0, start=True, stop=False)
            mm(bank[5][:, E:2 * E], strict, m1, start=False, stop=True)
            mm(bank[5][:, 2 * E:3 * E], ones, m0, start=True, stop=False)
            signal(mm(bank[5][:, 2 * E:3 * E], ones, m1, start=False, stop=True), "rank_mm")

            done, extra = layer * PAIRS, layer * (PAIRS + 1)

            def gather(i):
                pe.wait_ge(S["onehot"], i + extra + 1)
                for k in range(KT):
                    out = bank[2 + k // 4][:, P * (k % 4):P * (k % 4) + P]
                    for u in range(NH):
                        last = mm(out, xtok[:, u, k:D:KT], oneh[:, u].rearrange("p x s -> p (x s)"),
                                  start=u == 0, stop=u == NH - 1)
                last.then_inc(S["gather_mm"], 1)

            def scatter(i):
                pe.wait_ge(S["y_act"], i + done + layer)
                pe.wait_ge(S["y_dve"], i + done + layer)
                pe.wait_ge(S["pwt_sb"], i + done + layer)
                for q in range(4):
                    if q in (0, 3):
                        pe.wait_ge(S["scat_add"], (i - 1) * 4 + (1 if q == 3 else 0) + layer * (4 * PAIRS + 5) + 1)
                    b = bank[(5, 2, 3, 5)[q]]
                    for x in range(2):
                        last = mm(b[:, SEQ * x:SEQ * x + SEQ], ysb[:, P * (2 * q + x):P * (2 * q + x) + P], pwt,
                                  start=True, stop=True)
                    last.then_inc(S["scat_mm"], 1)

            def arrived_gate(h, x, c):
                if x:
                    pe.wait_ge(S[f"odd_full{c}"], h * 16 + 16 * (layer * PAIRS // 2 + 1))
                    return odd[c]
                pe.wait_ge(S[f"slot_full{c}"], h * 16 + ARRIVAL[FIRST[f"moe{layer}"] + c])
                return ring[c]

            def arrived_pair(i, c):
                pe.wait_ge(S[f"slot_full{c}"], i * 16 + ARRIVAL[FIRST[f"moe{layer}"] + c])
                return ring[c]

            pe.wait_ge(S["tok_sb"], 4 * (layer + 1))
            gather(0)
            def experts(h, x):
                i = h * 2 + x
                pe.wait_ge(S["xg_act"], i + extra + 1)
                pe.wait_ge(S["xg_dve"], i + extra + 1)
                for b, sem in ((bank[0], "gate_mm"), (bank[1], "up_mm")):
                    ws = [arrived_gate(h, x, y) if sem == "gate_mm" else arrived_pair(i, 2 + y) for y in range(2)]
                    for k in range(KT):
                        for y in range(2):
                            last = mm(b[64 * y:64 * y + 64, :], xg[:, k, 64 * y:64 * y + 64],
                                      ws[y][:, 512 * k:512 * k + 512], start=k == 0, stop=k == KT - 1)
                    last.then_inc(S[sem], 1)
                pe.wait_ge(S["scat_add"], i * 4 + layer * (4 * PAIRS + 5) + 1)
                gather(i + 1)
                pe.wait_ge(S["pwt_sb"], i + 1 + done + layer)
                pe.wait_ge(S["hh_sb"], i + 1 + done)
                for j in range(4):
                    last = nc.tensor.transpose(bank[4][:, P * j:P * j + P], hh[:, j:DE:4], ident)
                last.then_inc(S["t_mm"], 1)
                pe.wait_ge(S["xg_act"], i + extra + 2)
                pe.wait_ge(S["xg_dve"], i + extra + 2)
                scatter(i + 1)
                pe.wait_ge(S["ht_sb"], i + 1 + done)
                ws = [arrived_pair(i, 4 + y) for y in range(2)]
                for half in range(2):
                    for j in range(4):
                        for y in range(2):
                            at = D * j + 512 * half
                            last = mm(bank[6 + half][64 * y:64 * y + 64, :], hidT[:, j, 64 * y:64 * y + 64],
                                      ws[y][:, at:at + 512], start=j == 0, stop=j == 3)
                    last.then_inc(S["down_mm"], 1)
                pe.wait_ge(S["onehot_w"], i + 1 + done)
                for u in range(NH):
                    last = nc.tensor.transpose(bank[4][:, P * u:P * u + P], onehw[:, u].rearrange("p x s -> p (x s)"), ident)
                last.then_inc(S["pwt_mm"], 1)

            with pe.Fori(0, PAIRS // 2) as h:
                experts(h, 0)
                experts(h, 1)
            scatter(PAIRS + 1)

            over = pe.value_load(flag[0:1, 0:1], min_val=0, max_val=1)
            with pe.If(over > 0):
                with pe.Fori(0, E) as e:
                    pe.wait_ge(S[f"ov_full{layer}"], e * 48 + 48)
                    for u in range(NH):
                        pe.wait_ge(S[f"ov_add{layer}"], e * 2 + u + 1)
                        for b in range(2):
                            for k in range(KT):
                                last = mm(bank[b][:], xnT[:, k, P * u:P * u + P], ring[b][:, 512 * k:512 * k + 512],
                                          start=k == 0, stop=k == KT - 1)
                        last.then_inc(S[f"ov_gu{layer}"], 1)
                        pe.wait_ge(S[f"ov_hh{layer}"], e * 2 + u + 1)
                        for j in range(4):
                            last = nc.tensor.transpose(bank[4][:, P * j:P * j + P], hh[:, P * j:P * j + P], ident)
                        last.then_inc(S[f"ov_t{layer}"], 1)
                        pe.wait_ge(S[f"ov_ht{layer}"], e * 2 + u + 1)
                        for f in range(KT):
                            out = bank[6 + f // 4][:, P * (f % 4):P * (f % 4) + P]
                            for j in range(4):
                                last = mm(out, ring[2][:, D * j + P * f:D * j + P * f + P], hidT[:, j],
                                          start=j == 0, stop=j == 3)
                        last.then_inc(S[f"ov_down{layer}"], 1)
                pe.wait_ge(S[f"ov_add{layer}"], 2 * E + 1)
                nc.tensor.nop()
            pe.wait_ge(S["moe_done"], layer + 1)

        def ple(layer):
            ready = norm_input()
            for b in range(4):
                chunk = FIRST[f"ple{layer}"] + b // 2
                dense_split(USE[f"ple{layer}"] + 2 * b, [(chunk, (2 * b + i) % 4) for i in range(2)], xparts,
                            None if b else ready)
                w = arrived(pe, FIRST[f"ple_w{layer}"])
                pe.wait_ge(S["p_load"], 16)
                dense(USE[f"ple{layer}"] + 2 * b + 1, [
                    (SEQ * i, SEQ * i + SEQ, [(w[:, D * k + P * (2 * b + i):D * k + P * (2 * b + i) + P], pT[:, layer, k])
                                              for k in range(2)]) for i in range(2)])

        moe.last_use = [USE["out_a"] + 3, USE["out_b"] + 3]
        moe(0)
        ple(0)
        ready = norm_input()
        projection("in_b", "w_in_b", 8, xparts, ready)
        for b in range(4):
            released(pe, USE["in_b"] + b)
        wr, wi = (arrived(pe, FIRST["gates"] + x) for x in range(2))
        for d in range(2):
            for j in range(KT):
                at = [((d * 4 + j // 2) * 2 + k) * 256 + P * (j % 2) for k in range(2)]
                dense(USE["gates"] + KT * d + j, [
                    (SEQ * x, SEQ * x + SEQ, [(w[:, at[k]:at[k] + P], uu[:, 2 * (j // 2) + k]) for k in range(2)])
                    for x, w in enumerate((wr, wi))])
        projection("out_b", "w_out_b", 4, [[rr[d][:, k] for k in range(KT)] for d in (1, 0)], ("lru_h", 1))
        moe(1)
        ple(1)
        sum_squares()

    def bc(ap, shape):
        for _ in range(len(shape) - len(ap.shape)):
            ap = ap.unsqueeze(len(ap.shape))
        return ap.to_broadcast(shape)

    @block.scalar
    def _(act):
        count = {}

        def signal(ins, name):
            ins.then_inc(S[name], 1)
            count[name] = count.get(name, 0) + 1
            return count[name]

        def after(ins):
            act.wait_ge(S["act_step"], signal(ins, "act_step"))

        def free(ins, use):
            ins.then_inc(S[f"dense_free{use % BANKS}"], 1)

        def full(use):
            act.wait_ge(S["dense_full"], use + 1)

        def root(source, out, scale, sem, name):
            act.wait_ge(S[sem], count.get(sem + "s", 0) + 1)
            count[sem + "s"] = count.get(sem + "s", 0) + 1
            after(act.activation(out, source, ACT.Ln, bias=con("eps"), scale=scale))
            signal(act.activation(out, out, ACT.Exp, scale=-0.5), name)

        def squares(src, waits):
            functions(LN_EXP)
            for i, (sem, value) in enumerate(waits):
                act.wait_ge(S[sem], value)
                signal(act.activation(sq1[:, 2 * i:2 * i + 2], src[:, 2 * i:2 * i + 2], ACT.Square), "sq_ready")
            root(bank[4][:, 0:SEQ], bank[5][:, 0:SEQ], 1.0 / D, "ss_ready", "rstd_ready")

        def split_next():
            n = SPLITS[count.get("splits", 0)]
            count["splits"] = count.get("splits", 0) + 1
            w = arrived(act, n)
            if HIGH_AFTER[n]:
                sem, value = HIGH_AFTER[n]
                act.wait_ge(S[sem], value)
            for a, b in parts_of(n):
                signal(act.activation(rv(ring[HIGH_SLOT[n]][:, a:b]), w[:, a:b], ACT.Copy), "w_high")

        def high(out, x):
            signal(act.activation(rv(out), x, ACT.Copy), "x_high")

        def scaled_input(at=None):
            first = count.get("scaled", KT)
            count["scaled"] = first + KT
            for k in range(KT + 1):
                if k < KT:
                    act.wait_ge(S["xn_scaled"], first + k + 1)
                    if at is None:
                        high(xh[:, k], xnT[:, k])
                        continue
                    signal(act.activation(xnT[:, k], xnT[:, k], ACT.Identity, bias=mod[:, at + k, 0:1]), "act_step")
                if k and at is not None:
                    act.wait_ge(S["act_step"], count["act_step"] - (1 if k < KT else 0))
                    high(xh[:, k - 1], xnT[:, k - 1])

        def uses_free(first):
            return [(f"dense_free{n % BANKS}", n // BANKS + 1) for n in range(first, first + 4)]

        held = {}

        def functions(name):
            if held.get("set") != name:
                act.preload_act_table_set(name)
            held["set"] = name

        act.dma_start(params[:], t["params"]).then_inc(S["param_load"], 16)
        act.dma_start(consts[:], t["consts"]).then_inc(S["const_load"], 16)
        act.wait_ge(S["param_load"], 16)
        act.wait_ge(S["zeroed"], 1)
        signal(act.activation(c_cols[:, :, 0:2], par("c").rearrange("p (k m) -> p k m", k=KT), ACT.Silu), "c_cols")
        functions(LN_EXP)
        signal(act.activation(alog_e, par("a_log"), ACT.Exp), "ab_act")
        high(w_abh[:], par("w_ab"))
        act.wait_ge(S["const_load"], 16)
        act.wait_ge(S["ctx_load"], 16)
        act.wait_ge(S["x_load"], 16)
        for i in range(4):
            pair = slice(2 * i, 2 * i + 2)
            act.activation(sq2[:, pair, 0], ctxT[:, pair], ACT.Square)
            signal(act.activation(sq2[:, pair, 1], hT[:, pair], ACT.Square), "sq_ready")
        root(bank[4][:], bank[5][:], 1.0 / D, "ss_ready", "rstd_ready")

        split_next()
        for k in range(KT + 1):
            if k < KT:
                act.wait_ge(S["xn_scaled"], k + 1)
                for s in range(2):
                    last = act.activation(xn[:, k, s], xn[:, k, s], ACT.Identity, bias=mod[:, k, 1 - s:2 - s])
                signal(last, "act_step")
            if k:
                act.wait_ge(S["act_step"], count["act_step"] - (1 if k < KT else 0))
                high(xh2[:, k - 1], xn[:, k - 1])
        split_next()
        act.dma_start(wk("masks"), t["masks"]).then_inc(S["mask_load"], 16)
        act.wait_ge(S["ab_mm"], 1)
        signal(act.activation(ab_rows[0:16, :], bank[7][0:16, :], ACT.Copy), "ab_sb")

        functions(SILU)
        for i in range(8):
            released(act, USE["kv"] + i)
            x = (kc if i < 4 else vc)[:, i % 4]
            signal(act.activation(x, x, ACT.Silu), "silu_ready")
            if i in (3, 7):
                split_next()
        for b in range(2):
            released(act, USE["q"] + b)
            signal(act.activation(qc[:, 2 * b:2 * b + 2], qc[:, 2 * b:2 * b + 2], ACT.Silu), "silu_ready")
        split_next()
        for b in range(2):
            full(USE["z"] + b)
            free(act.activation(wk("zs", 512, 512 * b), bank[(USE["z"] + b) % BANKS][:], ACT.Silu), USE["z"] + b)
        for b in range(2):
            full(USE["u"] + b)
            free(act.activation(wk("oT", 512, 512 * b), bank[(USE["u"] + b) % BANKS][:], ACT.Copy), USE["u"] + b)
        for x in range(2):
            n = USE["dft_w"] + x
            full(n)
            free(act.activation(fo_w[:, x], bank[n % BANKS][:], ACT.Copy), n)
        act.wait_ge(S["ab_dve"], 1)
        functions(SIGMOID)
        signal(act.activation(beta, ab[:, :, 0:8], ACT.Sigmoid), "ab_act")
        functions(LN_EXP)
        act.wait_ge(S["ab_dve"], 2)
        signal(act.activation(gtmp[1], gtmp[1], ACT.Exp, scale=-1.0), "ab_act")
        for u in range(4):
            n = USE["vtok"] + u
            full(n)
            free(act.activation(wk("vtok", 512, 512 * u), bank[n % BANKS][:], ACT.Copy), n)

        heads_of = [wk("kc", 512, 512 * h) for h in range(4)] + [wk("qc", 512, 512 * h) for h in range(2)]

        def square_qk(a):
            if a >= 2:
                act.wait_ge(S["qk_ss"], a - 1)
            signal(act.activation(sqk[:, a % 2], heads_of[a], ACT.Square), "qk_sq")

        act.wait_ge(S["silu_ready"], 10)
        square_qk(0)
        square_qk(1)
        for x in range(4):
            n = USE["dft_b"] + x
            full(n)
            free(act.activation(fo_b[:, x // 2, x % 2].rearrange("p g e -> p (g e)"), bank[n % BANKS][:], ACT.Copy), n)
        for a in range(6):
            if a >= 2:
                act.wait_ge(S["qk_norm"], a - 1)
            root(bank[4 + a % 2][:], bank[6 + a % 2][:], 1.0, "qk_ss", "qk_rstd")
            if a + 2 < 6:
                square_qk(a + 2)
        for b in range(2):
            n = USE["dft_y"] + b
            full(n)
            free(act.activation(wk("cat", 512, 512 * b), bank[n % BANKS][:], ACT.Copy), n)
        for u in range(4):
            n = USE["ktok"] + u
            full(n)
            free(act.activation(wk("ktok", 512, 512 * u), bank[n % BANKS][:], ACT.Copy), n)
        split_next()
        split_next()

        banks = [[bank[0], bank[1], bank[4], bank[5]], [bank[2], bank[3], bank[6], bank[7]]]

        def by_head(b):
            return b[:].rearrange("p (h t) -> p h t", h=HEADS)

        for n in range(4):
            s = n // 2
            for d in range(2):
                e, last = 2 * n + d, (P - 1 if d == 0 else 0)
                a0 = by_head(banks[d][0])
                act.wait_ge(S["g_diff"], e + 1)
                if s:
                    act.activation(qd[:, d], a0, ACT.Exp)
                act.activation(egl[:, d], a0[:, :, last], ACT.Exp)
                act.activation(egcol[:, d], gcol[:, d], ACT.Exp)
                act.wait_ge(S["g_masked"], e + 1)
                signal(act.activation(decayT[:, d], decayT[:, d], ACT.Exp), "decay")
            for l in range(1, LEVELS):
                for d in range(2):
                    i = 2 * (LEVELS * n + l) + d
                    act.wait_ge(S["lvl_p"], i + 1)
                    signal(act.activation(pmat[:, d], by_head(banks[d][0]), ACT.Copy), "lvl_p_sb")
            for d in range(2):
                act.wait_ge(S["vn_mm"], 2 * n + d + 1)
                signal(act.activation(vnew[:, d], by_head(banks[d][1]), ACT.Copy), "vn_sb")
        for k in range(4):
            high(cath[:, k], cat[:, k])
        act.wait_ge(S["o_ready"], 4)
        for b in range(2):
            signal(act.activation(sqk[:, b], wk("oT", 512, 512 * b), ACT.Square), "o_sq")
        for b in range(2):
            root(bank[4 + b][:], bank[6 + b][:], 1.0 / P, "o_ss", "o_rstd")
        for h in range(HEADS):
            act.wait_ge(S["cat_gated"], h + 1)
            high(cath[:, 4 + h], cat[:, 4 + h])
        act.dma_start(pT, t["p"]).then_inc(S["p_load"], 16)

        def rows(stage):
            functions(LN_EXP)
            for b in range(4):
                n = USE[stage] + b
                if stage == "down":
                    split_next()
                full(n)
                signal(act.activation(sq1[:, 2 * b:2 * b + 2], bank[n % BANKS][:], ACT.Square), "sq_ready")
                free(act.activation(yT[:, 2 * b:2 * b + 2], bank[n % BANKS][:], ACT.Copy), n)
                if b % 2 or stage == "down":
                    if b < 3:
                        split_next()
            root(bank[4][:, 0:SEQ], bank[5][:, 0:SEQ], 1.0 / D, "ss_ready", "rstd_ready")
            split_next()

        rows("w_out")
        squares(hT, [("h_ready", 2 * i + 2) for i in range(4)])
        scaled_input(24)
        functions(SILU)
        for f in range(FT):
            if f % 2:
                full(USE["up"] + f)
                split_next()
            act.wait_ge(S["ffn_conv"], f + 1)
            signal(act.activation(sgate[:, f % 2], acc[:, f % 4], ACT.Silu), "ffn_silu")
            if f:
                released(act, USE["up"] + f - 1)
                high(prodh[:, f - 1], prod[:, f - 1])
        released(act, USE["up"] + FT - 1)
        high(prodh[:, FT - 1], prod[:, FT - 1])
        rows("down")
        squares(hT, [("h_ready", 8 + 2 * i + 2) for i in range(4)])
        scaled_input()
        for j in range(KT):
            n = USE["in_a"] + 3 * (j // 2) + j % 2
            full(n)
            if j >= 2:
                m = USE["in_a"] + 3 * ((j - 2) // 2) + j % 2
                released(act, m)
            signal(act.activation(c_sb[:, j % 2], bank[n % BANKS][:, 0:SEQ], ACT.Copy), "c_sb")
            if j in (1, 2, 3, 5, 6, 7):
                split_next()
            if j in (3, 5, 7):
                released(act, USE["in_a"] + 3 * (j // 2) - 1)
                high(yh[:, j - 3:j - 1], yT[:, j - 3:j - 1])
        released(act, USE["in_a"] + 11)
        high(yh[:, 6:8], yT[:, 6:8])

        def moe(layer):
            squares(hT, uses_free(USE[("out_a", "out_b")[layer]]))
            act.wait_ge(S["lg_mm"], layer + 1)
            signal(act.activation(lgT[0:36, :], bank[7][0:36, 0:SEQ], ACT.Copy), "lg_sb")

            def tokens(m):
                act.wait_ge(S["tok_mm"], 4 * layer + m + 1)
                signal(act.activation(xtok[:, m // 2, 512 * (m % 2):512 * (m % 2) + 512], bank[m][:], ACT.Copy), "tok_sb")

            tokens(0)
            tokens(1)
            act.wait_ge(S["route_dve"], 2 * layer + 1)
            for u in range(NH):
                last = act.activation(rt(52, 4)[:, u], lg[:, u, 0:4], ACT.Exp, bias=rt(50, 1)[:, u], accum_out=rt(60, 1)[:, u])
            signal(last, "route_act")
            tokens(2)
            act.wait_ge(S["route_dve"], 2 * layer + 2)
            signal(act.activation(rt(190, 1), rt(188, 1), ACT.Exp), "route_act")
            tokens(3)

            done, extra = layer * PAIRS, layer * (PAIRS + 1)
            functions(SILU)
            act.wait_ge(S["gather_mm"], extra + 1)
            act.activation(xg[:, 0:4], bank[2][:], ACT.Copy).then_inc(S["xg_act"], 1)
            with act.Fori(0, PAIRS) as i:
                act.wait_ge(S["gate_mm"], i + done + 1)
                act.activation(sg, bank[0][:], ACT.Silu).then_inc(S["sg_sb"], 1)
                act.wait_ge(S["gather_mm"], i + extra + 2)
                act.activation(xg[:, 0:4], bank[2][:], ACT.Copy).then_inc(S["xg_act"], 1)
                act.wait_ge(S["t_mm"], i + done + 1)
                act.activation(hidT, bank[4][:], ACT.Copy).then_inc(S["ht_sb"], 1)
                act.wait_ge(S["down_mm"], i * 2 + 2 * done + 1)
                act.activation(ysb[:, 0:512], bank[6][:], ACT.Copy).then_inc(S["y_act"], 1)
                act.wait_ge(S["pwt_mm"], i + extra + 2)
                act.activation(pwt, bank[4][:, 0:SEQ], ACT.Copy).then_inc(S["pwt_sb"], 1)

            over = act.value_load(flag[0:1, 0:1], min_val=0, max_val=1)
            with act.If(over > 0):
                with act.Fori(0, E) as e:
                    for u in range(NH):
                        act.wait_ge(S[f"ov_gu{layer}"], e * 2 + u + 1)
                        act.activation(sg, bank[0][:], ACT.Silu).then_inc(S[f"ov_sg{layer}"], 1)
                        act.wait_ge(S[f"ov_t{layer}"], e * 2 + u + 1)
                        act.activation(hidT, bank[4][:], ACT.Copy).then_inc(S[f"ov_ht{layer}"], 1)

        def ple(layer):
            held.clear()
            functions(LN_EXP)
            split_next()
            squares(hT, [("moe_done", layer + 1)] * 4)
            scaled_input()
            split_next()
            functions(SIGMOID)
            for b in range(4):
                n = USE[f"ple{layer}"] + 2 * b
                full(n)
                for x in range(2):
                    j = 2 * b + x
                    last = act.activation(gsb[:, j], bank[n % BANKS][:, SEQ * x:SEQ * x + SEQ], ACT.Sigmoid,
                                          bias=par("b_ple", 8 * layer + j, 1))
                free(last, n)
                if layer == 0 and b % 2:
                    split_next()

        moe(0)
        ple(0)
        squares(hT, [("h_ready", 16 + i + 1) for i in range(4)])
        scaled_input()
        act.wait_ge(S["lru_log"], 1)
        signal(act.activation(nlt[1], nlt[1], ACT.Exp, scale=-1.0), "lru_exp")
        functions(GELU)
        split_next()
        split_next()
        for b in range(4):
            n = USE["in_b"] + 4 + b
            full(n)
            free(act.activation(yg[:, 2 * b:2 * b + 2], bank[n % BANKS][:], ACT.Gelu_apprx_tanh), n)
            if b == 1:
                split_next()
        functions(SIGMOID)
        for i in range(2 * KT + 1):
            if i < 2 * KT:
                d, j = i // KT, i % KT
                n = USE["gates"] + i
                full(n)
                act.activation(rr[d][:, j], bank[n % BANKS][:, 0:SEQ], ACT.Sigmoid, bias=par("b_rg", 8 * d + j, 1))
                free(act.activation(gi[d][:, j], bank[n % BANKS][:, SEQ:512], ACT.Sigmoid, bias=par("b_ig", 8 * d + j, 1)), n)
            if i == KT // 2:
                split_next()
            if i:
                d, j = (i - 1) // KT, (i - 1) % KT
                act.wait_ge(S["lru_log"], i + 1)
                last = act.activation(th[d][:, j], rr[d][:, j], ACT.Tanh)
        after(last)
        functions(EXP)
        for d in range(2):
            signal(act.activation(a_sq[d], rr[d], ACT.Exp, scale=2.0), "lru_exp")
        functions(SQRT)
        for d in range(2):
            act.wait_ge(S["lru_var"], d + 1)
            signal(act.activation(th[d], th[d], ACT.Sqrt, scale=-1.0), "lru_sqrt")
        functions(EXP)
        act.wait_ge(S["lru_exp"], 3)
        for d in range(2):
            signal(act.activation(rr[d], rr[d], ACT.Exp), "lru_exp")
        for k in range(KT):
            act.wait_ge(S["lru_mul"], k + 1)
            signal(act.activation(rv(rr[1][:, k]), rr[0][:, k], ACT.Copy), "lru_high")
        moe(1)
        ple(1)
        squares(hT, [("h_ready", 20 + i + 1) for i in range(4)])

    @block.gpsimd
    def _(pool):
        pool.memset(wk("S", KT * 32), 0.0).then_inc(S["zeroed"], 1)
        n_split = [0]

        def split_low(chunks):
            for _ in range(chunks):
                n = SPLITS[n_split[0]]
                for i, (a, b) in enumerate(parts_of(n)):
                    if LOW_DONE[n, i][0] != "w_low":
                        continue
                    pool.wait_ge(S["w_high"], 2 * n_split[0] + i + 1)
                    w = ring[SLOT[n]][:, a:b]
                    pool.tensor_tensor(rv(w), w, rv(ring[HIGH_SLOT[n]][:, a:b]), ALU.subtract).then_inc(S["w_low"], 1)
                n_split[0] += 1

        split_low(5)
        pool.wait_ge(S["mask_load"], 16)
        shape = [P, HEADS, P]

        def heads(m):
            return m.unsqueeze(1).to_broadcast(shape)

        for n in range(4):
            s, c = n // 2, n % 2
            for d in range(2):
                e = 2 * n + d
                pool.wait_ge(S["g_diff"], e + 1)
                pool.tensor_tensor(decayT[:, d], decayT[:, d], heads(neg[:, d]), ALU.add).then_inc(S["g_masked"], 1)
            for l in range(LEVELS):
                for d in range(2):
                    e, half, last = 2 * n + d, (c if d == 0 else 1 - c), (P - 1 if d == 0 else 0)
                    u = 2 * s + half
                    if l == 0:
                        pool.wait_ge(S["at_ready"], e + 1)
                    else:
                        pool.wait_ge(S["lvl_p"], 2 * (LEVELS * n + l - 1) + d + 1)
                        if l == 1:
                            pool.wait_ge(S["lvl_t"], 2 * LEVELS * n + d + 1)
                    pool.tensor_tensor(lmask[:, d], amatT[:, d], heads(level[:, l]), ALU.mult).then_inc(S["lvl_mask"], 1)
                    if l == 1:
                        if n < 3:
                            pool.tensor_tensor(kd[:, d], ktok[:, u], bc(decayT[:, d, :, last], shape), ALU.mult)
                        if s:
                            pool.tensor_tensor(qd[:, d], qd[:, d], qc[:, :, P * half:P * half + P], ALU.mult)
                        pool.tensor_tensor(xmat[:, d], vtok[:, u], bc(beta[:, u, 4 * d:4 * d + 4], shape), ALU.mult)\
                            .then_inc(S["g_pool"], 1)
        split_low(2 + 11 + 8 + 6 + 2)
        for layer in range(2):
            done, extra = layer * PAIRS, layer * (PAIRS + 1)
            with pool.Fori(0, PAIRS) as i:
                pool.wait_ge(S["onehot"], i + extra + 1)
                pool.wait_ge(S["pwt_mm"], i + extra + 1)
                for u in range(NH):
                    last = pool.tensor_tensor(onehw[:, u], oneh[:, u], bc(wgt[:, u, bass.ds(i * 2, 2)], [P, 2, SLOTS]), ALU.mult)
                last.then_inc(S["onehot_w"], 1)
            split_low((2 + 4 + 2, 2)[layer])
            if layer == 0:
                for k in range(KT):
                    pool.wait_ge(S["lru_high"], k + 1)
                    pool.tensor_tensor(rv(rr[0][:, k]), rr[0][:, k], rv(rr[1][:, k]), ALU.subtract).then_inc(S["lru_h"], 1)

    @block.vector
    def _(dve):
        v = nc.vector
        count = {}

        def signal(ins, name):
            ins.then_inc(S[name], 1)
            count[name] = count.get(name, 0) + 1
            return count[name]

        def after(ins):
            dve.wait_ge(S["dve_step"], signal(ins, "dve_step"))

        def free(ins, use):
            ins.then_inc(S[f"dense_free{use % BANKS}"], 1)

        def full(use):
            dve.wait_ge(S["dense_full"], use + 1)
            return bank[use % BANKS]

        rstd = bank[5][:, 0:SEQ]

        def low(x, high, name):
            count["highs"] = count.get("highs", 0) + 1
            dve.wait_ge(S["x_high"], count["highs"])
            signal(v.tensor_tensor(rv(x), x, rv(high), ALU.subtract), name)

        def roots():
            count["roots"] = count.get("roots", 0) + 1
            dve.wait_ge(S["rstd_ready"], count["roots"])

        def scaled(src, gain, split=True):
            roots()
            for k in range(KT + 2):
                if k < KT:
                    signal(v.scalar_tensor_tensor(xnT[:, k], src[:, k], gain(k), rstd, ALU.mult, ALU.mult),
                           "xn_scaled" if split else "xn_ready")
                if k >= 2 and split:
                    low(xnT[:, k - 2], xh[:, k - 2], "xn_ready")

        def residual(gain):
            roots()
            for k in range(KT + 1):
                if k < KT:
                    signal(v.scalar_tensor_tensor(tmp[:, k % 4], yT[:, k], gain(k), rstd, ALU.mult, ALU.mult), "dve_step")
                if k:
                    dve.wait_ge(S["dve_step"], count["dve_step"] - (1 if k < KT else 0))
                    signal(v.tensor_tensor(hT[:, k - 1], hT[:, k - 1], tmp[:, (k - 1) % 4], ALU.add), "h_ready")

        def log1p(z, e, scratch):
            a, b = scratch
            after(v.tensor_scalar(a, e, 2.0, None, ALU.add))
            after(v.reciprocal(b, a))
            after(v.tensor_tensor(z, e, b, ALU.mult))
            after(v.tensor_tensor(a, z, z, ALU.mult))
            after(v.tensor_scalar(b, a, LOG1P[7], None, ALU.mult))
            for coefficient in LOG1P[6:0:-1]:
                after(v.scalar_tensor_tensor(b, b, coefficient, a, ALU.add, ALU.mult))
            after(v.scalar_tensor_tensor(z, b, 1.0, z, ALU.add, ALU.mult))
            after(v.tensor_scalar(z, z, 2.0, None, ALU.mult))

        def ada_step(part, m):
            first = USE[f"ada{part}"]
            if m < 4:
                n = first + max(0, 2 * m - 1)
                x = full(n)
                if m >= 2:
                    dve.wait_ge(S["dense_full"], first + 2 * m - 1)
                free(v.tensor_copy(ada_row[:, m % 2], x[:]), n)
            if m:
                n = first + min(2 * m, 7)
                x = full(n)[:].rearrange("p (i c) -> p i c", i=4)[:, :, 0:2]
                at = 4 * (4 * part + m - 1)
                free(v.tensor_tensor(mod[:, at:at + 4], x, bc(par("b_ada", at, 4), [P, 4, 2]), ALU.add), n)

        dve.wait_ge(S["param_load"], 16)
        for m in range(5):
            ada_step(0, m)
        for n in (2, 4, 6, 7):
            released(dve, USE["ada0"] + n)
        for i, (tile, m, g) in enumerate(((8, 1, "g_pre_mix"), (8, 0, "g_pre_mix"))):
            last = v.scalar_tensor_tensor(gains[:, i], mod[:, tile:tile + 8, m], 1.0, par(g), ALU.add, ALU.mult)
        after(last)

        roots()
        dve.wait_ge(S["ctx_load"], 16)
        dve.wait_ge(S["x_load"], 16)
        low(par("w_ab"), w_abh[:], "dve_step")
        for k in range(KT + 2):
            if k >= 2:
                low(xn[:, k - 2], xh2[:, k - 2], "xn_ready")
            if k >= KT:
                continue
            for s, src in enumerate((ctxT, hT)):
                ins = v.scalar_tensor_tensor(xn[:, k, s], src[:, k], gains[:, s, k:k + 1], bank[5][:, SEQ * s:SEQ * s + SEQ],
                                             ALU.mult, ALU.mult)
            signal(ins, "xn_scaled")

        def conv3(n, out, x, w):
            after(v.tensor_scalar(out, x, w(1), None, ALU.mult))
            a, b = slice(0, SEQ - 1), slice(1, SEQ)
            after(v.scalar_tensor_tensor(out[..., b], x[..., a], w(0), out[..., b], ALU.mult, ALU.add))
            ins = v.scalar_tensor_tensor(out[..., a], x[..., b], w(2), out[..., a], ALU.mult, ALU.add)
            return ins

        def conv_w(tile):
            return lambda j: par("conv", 3 * tile + j, 1)

        for i in range(8):
            n = USE["kv"] + i
            b = full(n)
            free(conv3(n, (kc if i < 4 else vc)[:, i % 4], b[:].rearrange("p (s t) -> p s t", s=2), conv_w(4 + i)), n)
            if i == 7:
                dve.wait_ge(S["ab_cols"], 1)
                signal(v.tensor_copy(ab, bank[6][:, 0:64].rearrange("p (u c) -> p u c", u=4)), "ab_dve")
                dve.wait_ge(S["ab_dve"], 1)
                after(v.tensor_tensor(gtmp[0], ab[:, :, 8:16], par("dt_bias").unsqueeze(1).to_broadcast([P, 4, 8]), ALU.add))
                signal(v.scalar_tensor_tensor(gtmp[1], gtmp[0], -1.0, gtmp[0], ALU.mult, ALU.max), "ab_dve")
        for b in range(2):
            n = USE["q"] + b
            x = full(n)
            for i in range(2):
                ins = conv3(n, qc[:, 2 * b + i], x[:, SEQ * i:SEQ * i + SEQ], conv_w(2 * b + i))
            free(ins, n)
        dve.wait_ge(S["ab_act"], 3)
        log1p(gtmp[2], gtmp[1], gtmp[3:5])
        after(v.scalar_tensor_tensor(gtmp[0], gtmp[0], 0.0, gtmp[2], ALU.max, ALU.add))
        signal(v.scalar_tensor_tensor(glog, gtmp[0], -1.0, alog_e.unsqueeze(1).to_broadcast([P, 4, 8]), ALU.mult, ALU.mult),
               "gates_ready")
        def norm_qk(a):
            dve.wait_ge(S["qk_rstd"], a + 1)
            r = bank[6 + a % 2][:]
            x = wk("kc", 512, 512 * a) if a < 4 else wk("qc", 512, 512 * (a - 4))
            signal(v.scalar_tensor_tensor(x, x, 1.0 if a < 4 else float(P) ** -0.5, r, ALU.mult, ALU.mult), "qk_norm")

        for m in range(5):
            if m < 4:
                norm_qk(m)
            ada_step(1, m)
        for m in range(5):
            if m < 2:
                norm_qk(4 + m)
            ada_step(2, m)
        for n in (2, 4, 6, 7):
            released(dve, USE["ada2"] + n)
        v.scalar_tensor_tensor(gains[:, 2], mod[:, 32:40, 0], 1.0, par("g_pre_ffn"), ALU.add, ALU.mult)
        v.tensor_tensor(gains[:, 3], mod[:, 16:24, 0], par("g_post_mix"), ALU.mult)
        after(v.tensor_tensor(gains[:, 4], mod[:, 40:48, 0], par("g_post_ffn"), ALU.mult))

        banks = [[bank[0], bank[1], bank[4], bank[5]], [bank[2], bank[3], bank[6], bank[7]]]
        shape = [P, HEADS, P]

        def by_head(b):
            return b[:].rearrange("p (h t) -> p h t", h=HEADS)

        eye = ident.unsqueeze(1).to_broadcast(shape)
        for n in range(4):
            s, c = n // 2, n % 2
            for d in range(2):
                e = 2 * n + d
                a0, a1, a2, a3 = banks[d]
                dve.wait_ge(S["g_rows"], e + 1)
                after(v.tensor_copy(gcol[:, d], a3[:, 0:HEADS]))
                signal(v.tensor_tensor(decayT[:, d], by_head(a0), bc(gcol[:, d], shape), ALU.subtract), "g_diff")
            for d in range(2):
                e, half = 2 * n + d, (c if d == 0 else 1 - c)
                u = 2 * s + half
                a0, a1, a2, a3 = banks[d]
                dve.wait_ge(S["decay"], e + 1)
                after(v.tensor_tensor(amatT[:, d], by_head(a2), decayT[:, d], ALU.mult))
                signal(v.tensor_tensor(amatT[:, d], amatT[:, d], by_head(a1), ALU.mult), "at_ready")
                signal(v.tensor_tensor(begc[:, d], beta[:, u, 4 * d:4 * d + 4], egcol[:, d], ALU.mult), "dve_step")
                if s:
                    dve.wait_ge(S["qk_mm"], e - 3)
                    v.tensor_tensor(attnT[:, d], by_head(a3), decayT[:, d], ALU.mult)
            for l in range(LEVELS):
                for d in range(2):
                    a0, a1, a2, a3 = banks[d]
                    i = 2 * (LEVELS * n + l) + d
                    if l == 0:
                        dve.wait_ge(S["lvl_p"], i + 1)
                        v.tensor_tensor(tinv[:, d], eye, by_head(a0), ALU.subtract)
                        signal(v.tensor_tensor(tinvT[:, d], eye, lmask[:, d], ALU.subtract), "lvl_t")
                    else:
                        dve.wait_ge(S["lvl_tp"], 2 * ((LEVELS - 1) * n + l - 1) + d + 1)
                        dve.wait_ge(S["lvl_t"], i - 1)
                        if l < LEVELS - 1:
                            v.tensor_tensor(tinv[:, d], tinv[:, d], by_head(a1), ALU.subtract)
                        signal(v.tensor_tensor(tinvT[:, d], tinvT[:, d], by_head(a2), ALU.subtract), "lvl_t")
            for d in range(2):
                a0 = banks[d][0]
                if n:
                    dve.wait_ge(S["ks_mm"], 2 * (n - 1) + d + 1)
                    dve.wait_ge(S["g_pool"], 2 * n + d + 1)
                    dve.wait_ge(S["dve_step"], count["dve_step"])
                    after(v.tensor_tensor(pmat[:, d], by_head(a0), bc(begc[:, d], shape), ALU.mult))
                    signal(v.tensor_tensor(xmat[:, d], xmat[:, d], pmat[:, d], ALU.subtract), "x_ready")
            for d in range(2):
                e, half = 2 * n + d, (c if d == 0 else 1 - c)
                a2, a3 = banks[d][2:]
                if s:
                    dve.wait_ge(S["o_mm"], 2 * (n - 2) + d + 1)
                    out = oT[:, :, P * half:P * half + P]
                    if c == 0:
                        signal(v.tensor_copy(out, by_head(a2)), "o_ready")
                    else:
                        dve.wait_ge(S["o_ready"], 2)
                        signal(v.tensor_tensor(out, out, by_head(a2), ALU.add), "o_ready")
                if n < 3:
                    dve.wait_ge(S["ds_mm"], e + 1)
                    if n == 0:
                        signal(v.tensor_copy(state[:, d], by_head(a3)), "s_ready")
                    else:
                        after(v.tensor_tensor(pmat[:, d], state[:, d], bc(egl[:, d], shape), ALU.mult))
                        signal(v.tensor_tensor(state[:, d], pmat[:, d], by_head(a3), ALU.add), "s_ready")

        for k in range(4):
            low(cat[:, k], cath[:, k], "cat_ready")
        for b in range(2):
            dve.wait_ge(S["o_rstd"], b + 1)
            o = wk("oT", 512, 512 * b)
            after(v.scalar_tensor_tensor(o, o, par("g_gdn"), bank[6 + b][:], ALU.mult, ALU.mult))
            for i in range(2):
                h = 2 * b + i
                signal(v.tensor_tensor(cat[:, 4 + h], oT[:, h], zs[:, h], ALU.mult), "cat_gated")
        for h in range(HEADS):
            low(cat[:, 4 + h], cath[:, 4 + h], "cat_ready")

        residual(lambda k: gains[:, 3, k:k + 1])
        scaled(hT, lambda k: gains[:, 2, k:k + 1])

        def gated(f):
            n = USE["up"] + f
            dve.wait_ge(S["ffn_silu"], f + 1)
            free(v.tensor_tensor(prod[:, f], bank[n % BANKS][:, 0:SEQ], sgate[:, f % 2], ALU.mult), n)

        for f in range(FT):
            x = full(USE["up"] + f)[:, SEQ:2 * SEQ].rearrange("p (r c) -> p r c", r=ROWS)
            o = acc[:, f % 4].rearrange("p (r c) -> p r c", r=ROWS)
            after(v.tensor_scalar(o, x, par("w_dwc", 9 * f + 4, 1), None, ALU.mult))
            taps = [(dy, dx) for dy in (-1, 0, 1) for dx in (-1, 0, 1) if (dy, dx) != (0, 0)]
            for dy, dx in taps:
                r0, r1, c0, c1 = max(0, -dy), ROWS - max(0, dy), max(0, -dx), GRID_W - max(0, dx)
                dst = o[:, r0:r1, c0:c1]
                ins = v.scalar_tensor_tensor(dst, x[:, r0 + dy:r1 + dy, c0 + dx:c1 + dx],
                                             par("w_dwc", 9 * f + 3 * (dy + 1) + dx + 1, 1), dst, ALU.mult, ALU.add)
                if (dy, dx) == taps[-1]:
                    signal(ins, "ffn_conv")
                else:
                    after(ins)
            if f:
                gated(f - 1)
            if f >= 2:
                low(prod[:, f - 2], prodh[:, f - 2], "prod_ready")
        gated(FT - 1)
        for f in (FT - 2, FT - 1):
            low(prod[:, f], prodh[:, f], "prod_ready")
        for n in BY_DVE:
            a, b = parts_of(n)[0]
            dve.wait_ge(S["w_high"], 2 * SPLITS.index(n) + 1)
            w = ring[SLOT[n]][:, a:b]
            v.tensor_tensor(rv(w), w, rv(ring[HIGH_SLOT[n]][:, a:b]), ALU.subtract).then_inc(S["w_low_dve"], 1)
        residual(lambda k: gains[:, 4, k:k + 1])

        def low_pair(k):
            count["highs"] += 1
            dve.wait_ge(S["x_high"], count["highs"])
            for i in (k, k + 1):
                signal(v.tensor_tensor(rv(yT[:, i]), yT[:, i], rv(yh[:, i]), ALU.subtract), "y_ready")

        scaled(hT, lambda k: par("norm_mix", k, 1))
        for j in range(KT):
            n = USE["in_a"] + 3 * (j // 2) + j % 2
            x = full(n)
            dve.wait_ge(S["c_sb"], j + 1)
            ins = v.tensor_tensor(ch[:, j % 2], c_sb[:, j % 2], x[:, SEQ:2 * SEQ], ALU.mult)
            free(ins, n)
            released(dve, n)
            after(conv3(None, cu[:, j % 4], ch[:, j % 2], lambda i: par("conv_a", 3 * j + i, 1)))
            if j % 2:
                n = USE["in_a"] + 3 * (j // 2) + 2
                x = full(n)
                for i in range(2):
                    m = j - 1 + i
                    ins = v.tensor_tensor(yT[:, m], x[:, SEQ * i:SEQ * i + SEQ], cu[:, m % 4], ALU.mult)
                free(ins, n)
                if j > 1:
                    low_pair(j - 3)
        low_pair(6)

        def add_output(stage):
            for b in range(4):
                n = USE[stage] + b
                x = full(n)
                pair = slice(2 * b, 2 * b + 2)
                free(v.tensor_tensor(hT[:, pair], hT[:, pair], x[:].rearrange("p (k t) -> p k t", k=2), ALU.add), n)

        add_output("out_a")

        def moe(layer):
            done, extra = layer * PAIRS, layer * (PAIRS + 1)
            scaled(hT, lambda k: par("norm_ffn", 8 * layer + k, 1), False)
            signal(v.memset(ysb[:, 0:512], 0.0), "y_act")
            signal(v.memset(ysb[:, 512:1024], 0.0), "y_dve")
            signal(v.memset(pwt, 0.0), "pwt_sb")
            v.memset(rt(0, 8), -3e38)
            v.memset(wgt, 0.0)
            after(v.memset(rankm, -1.0))
            iota = con("iota")
            dve.wait_ge(S["lg_cols"], layer + 1)
            bias = par("b_router", 36 * layer, 36).unsqueeze(1).to_broadcast([P, NH, 36])
            after(v.tensor_tensor(lg, bank[6][:, 0:72].rearrange("p (u c) -> p u c", u=NH), bias, ALU.add))
            g8, gm, gi, oneg, let, les, em, ei = (rt(a, n) for a, n in (
                (0, 8), (16, 8), (32, 8), (64, 4), (72, 32), (136, 8), (152, 8), (168, 8)))
            after(v.tensor_copy(g8[:, :, 0:N_GROUPS], lg[:, :, 0:N_GROUPS]))
            for u in range(NH):
                last = v.max(gm[:, u], g8[:, u])
            after(last)
            signal(v.tensor_scalar(rt(50, 1), gm[:, :, 0:1], -1.0, None, ALU.mult), "route_dve")
            for u in range(NH):
                last = v.max_index(gi[:, u].bitcast(U32), gm[:, u], g8[:, u])
            after(last)
            gif = rt(48, 1)
            after(v.tensor_copy(gif, gi.bitcast(U32)[:, :, 0:1]))
            after(v.tensor_tensor(oneg, iota[:, 0:N_GROUPS].unsqueeze(1).to_broadcast([P, NH, N_GROUPS]),
                                  gif.to_broadcast([P, NH, N_GROUPS]), ALU.is_equal))
            for u in range(NH):
                last = v.tensor_tensor(let[:, u].rearrange("p (e g) -> p e g", g=N_GROUPS),
                                       lg[:, u, N_GROUPS:].rearrange("p (g e) -> p e g", g=N_GROUPS),
                                       oneg[:, u].unsqueeze(1).to_broadcast([P, PER_GROUP, N_GROUPS]), ALU.mult)
            after(last)
            after(v.reduce_sum(les, let.rearrange("p u (e g) -> p u e g", g=N_GROUPS), axis=AX))
            for u in range(NH):
                last = v.max(em[:, u], les[:, u])
            after(last)
            signal(v.tensor_tensor(rt(188, 1), em[:, :, 1:2], em[:, :, 0:1], ALU.subtract), "route_dve")
            for u in range(NH):
                last = v.max_index(ei[:, u].bitcast(U32), em[:, u], les[:, u])
            after(last)
            eif = rt(184, 2)
            after(v.tensor_copy(eif, ei.bitcast(U32)[:, :, 0:2]))
            picked = rt(200, 2)
            after(v.scalar_tensor_tensor(picked, gif.to_broadcast([P, NH, 2]), float(PER_GROUP), eif, ALU.mult, ALU.add))
            m1, m2, m12 = rt(304, E), rt(368, E), rt(240, E)
            for i, m in enumerate((m1, m2)):
                last = v.tensor_tensor(m, iota[:, 0:E].unsqueeze(1).to_broadcast([P, NH, E]),
                                       picked[:, :, i:i + 1].to_broadcast([P, NH, E]), ALU.is_equal)
            after(last)
            signal(v.tensor_tensor(m12, m1, m2, ALU.add), "mask_ready")
            dve.wait_ge(S["route_act"], 2 * layer + 2)
            v.reciprocal(rt(62, 1), rt(60, 1))
            after(v.tensor_scalar(rt(192, 1), rt(190, 1), 1.0, None, ALU.add))
            after(v.reciprocal(rt(194, 1), rt(192, 1)))
            after(v.tensor_tensor(rt(196, 1), rt(194, 1), rt(62, 1), ALU.mult))
            after(v.tensor_tensor(rt(198, 1), rt(196, 1), rt(190, 1), ALU.mult))
            v.tensor_tensor(m1, m1, rt(196, 1).to_broadcast([P, NH, E]), ALU.mult)
            after(v.tensor_tensor(m2, m2, rt(198, 1).to_broadcast([P, NH, E]), ALU.mult))
            after(v.tensor_tensor(wgt[:, :, 0:E], m1, m2, ALU.add))
            dve.wait_ge(S["rank_mm"], layer + 1)
            ranks = bank[5][:, 0:2 * E].rearrange("p (u e) -> p u e", u=NH)
            after(v.scalar_tensor_tensor(rankm[:, :, 0:E], ranks, 1.0, m12, ALU.add, ALU.mult))
            after(v.tensor_scalar(rankm[:, :, 0:E], rankm[:, :, 0:E], -1.0, None, ALU.add))
            after(v.reduce_max(rt(496, 1)[:, 0], bank[5][:, 2 * E:3 * E], axis=AX))
            after(v.scalar_tensor_tensor(wov, rankm[:, :, 0:E], float(SLOTS), wgt[:, :, 0:E], ALU.is_ge, ALU.mult))
            signal(v.tensor_scalar(flag[:], rt(496, 1)[:, 0], float(SLOTS), None, ALU.is_gt), "route_ready")
            signal(v.memset(rt(600, 1), 0.0), "scat_add")
            signal(v.memset(rt(602, 1), 0.0), "pwt_mm")

            def select(pair):
                for u in range(NH):
                    last = v.tensor_tensor(oneh[:, u], iota.unsqueeze(1).to_broadcast([P, 2, SLOTS]),
                                           bc(rankm[:, u, bass.ds(pair * 2, 2)], [P, 2, SLOTS]), ALU.is_equal)
                last.then_inc(S["onehot"], 1)

            def take():
                v.tensor_copy(xg[:, 4:8], bank[3][:].rearrange("p (k s) -> p k s", k=4)).then_inc(S["xg_dve"], 1)

            def add(i):
                base = layer * (4 * PAIRS + 5) + 1
                dve.wait_ge(S["scat_add"], i * 4 + base)
                for q in range(4):
                    dve.wait_ge(S["scat_mm"], i * 4 + layer * (4 * PAIRS + 4) + q + 1)
                    pair = slice(2 * q, 2 * q + 2)
                    v.tensor_tensor(hT[:, pair], hT[:, pair], bank[(5, 2, 3, 5)[q]][:].rearrange("p (k t) -> p k t", k=2), ALU.add)\
                        .then_inc(S["scat_add"], 1)

            select(0)
            dve.wait_ge(S["gather_mm"], extra + 1)
            take()
            with dve.Fori(0, PAIRS) as i:
                dve.wait_ge(S["gather_mm"], i + extra + 1)
                dve.wait_ge(S["onehot_w"], i + done + 1)
                select(i + 1)
                dve.wait_ge(S["sg_sb"], i + done + 1)
                dve.wait_ge(S["up_mm"], i + done + 1)
                v.tensor_tensor(hh, sg, bank[1][:], ALU.mult).then_inc(S["hh_sb"], 1)
                dve.wait_ge(S["gather_mm"], i + extra + 2)
                take()
                add(i)
                dve.wait_ge(S["down_mm"], i * 2 + 2 * done + 2)
                v.tensor_copy(ysb[:, 512:1024], bank[7][:]).then_inc(S["y_dve"], 1)
            add(PAIRS)
            dve.wait_ge(S["scat_add"], (layer + 1) * (4 * PAIRS + 5))

            over = dve.value_load(flag[0:1, 0:1], min_val=0, max_val=1)
            with dve.If(over > 0):
                v.memset(rt(604, 1), 0.0).then_inc(S[f"ov_down{layer}"], 1)
                v.memset(rt(606, 1), 0.0).then_inc(S[f"ov_add{layer}"], 1)
                with dve.Fori(0, E) as e:
                    for u in range(NH):
                        dve.wait_ge(S[f"ov_sg{layer}"], e * 2 + u + 1)
                        v.scalar_tensor_tensor(hh, sg, wov[:, u, bass.ds(e, 1)], bank[1][:], ALU.mult, ALU.mult)\
                            .then_inc(S[f"ov_hh{layer}"], 1)
                        dve.wait_ge(S[f"ov_down{layer}"], e * 2 + u + 2)
                        dve.wait_ge(S[f"ov_add{layer}"], e * 2 + u + 1)
                        for b in range(2):
                            x = hT[:, 4 * b:4 * b + 4, P * u:P * u + P]
                            last = v.tensor_tensor(x, x, bank[6 + b][:].rearrange("p (k t) -> p k t", k=4), ALU.add)
                        last.then_inc(S[f"ov_add{layer}"], 1)
                dve.wait_ge(S[f"ov_add{layer}"], 2 * E + 1)
                v.memset(rt(608, 1), 0.0)
            v.memset(rt(610, 1), 0.0).then_inc(S["moe_done"], 1)

        def ple(layer):
            scaled(hT, lambda k: par("norm_ple", 8 * layer + k, 1))
            for b in range(4):
                n = USE[f"ple{layer}"] + 2 * b
                x = full(n + 1)
                released(dve, n)
                pair = slice(2 * b, 2 * b + 2)
                g = gsb[:, pair]
                free(v.tensor_tensor(g, g, x[:].rearrange("p (k t) -> p k t", k=2), ALU.mult), n + 1)
                released(dve, n + 1)
                signal(v.tensor_tensor(hT[:, pair], hT[:, pair], g, ALU.add), "h_ready")

        moe(0)
        ple(0)

        x = par("lam")
        signal(v.scalar_tensor_tensor(nlt[1], x, -1.0, x, ALU.mult, ALU.max), "lru_log")
        scaled(hT, lambda k: par("norm_mix", 8 + k, 1))
        dve.wait_ge(S["lru_exp"], 1)
        log1p(nlt[2], nlt[1], nlt[3:5])
        after(v.tensor_scalar(nlt[0], par("lam"), -1.0, 0.0, ALU.mult, ALU.max))
        after(v.tensor_tensor(nlt[0], nlt[0], nlt[2], ALU.add))
        after(v.tensor_scalar(nls, nlt[0], -RG_C, None, ALU.mult))
        for b in range(4):
            n = USE["in_b"] + b
            p = full(n)
            for i in range(2):
                j = 2 * b + i
                x, o = p[:, SEQ * i:SEQ * i + SEQ], uu[:, j]
                after(v.tensor_scalar(o, x, par("conv_b", 4 * j + 2, 1), par("conv_bias", j, 1), ALU.mult, ALU.add))
                after(v.scalar_tensor_tensor(o[:, 1:], x[:, :SEQ - 1], par("conv_b", 4 * j + 1, 1), o[:, 1:], ALU.mult, ALU.add))
                after(v.scalar_tensor_tensor(o[:, 2:], x[:, :SEQ - 2], par("conv_b", 4 * j, 1), o[:, 2:], ALU.mult, ALU.add))
                last = v.scalar_tensor_tensor(o[:, :SEQ - 1], x[:, 1:], par("conv_b", 4 * j + 3, 1), o[:, :SEQ - 1], ALU.mult, ALU.add)
            free(last, n)
        for d in range(2):
            for j in range(KT):
                released(dve, USE["gates"] + KT * d + j)
                signal(v.tensor_scalar(rr[d][:, j], rr[d][:, j], nls[:, 8 * d + j:8 * d + j + 1], None, ALU.mult), "lru_log")
                last = v.tensor_tensor(gi[d][:, j], gi[d][:, j], uu[:, j], ALU.mult)
        after(last)
        for d in range(2):
            dve.wait_ge(S["lru_exp"], d + 2)
            signal(v.scalar_tensor_tensor(th[d], a_sq[d], 1.0, th[d], ALU.add, ALU.mult), "lru_var")
        for d in range(2):
            dve.wait_ge(S["lru_sqrt"], d + 1)
            last = v.tensor_tensor(th[d], th[d], gi[d], ALU.mult)
        after(last)
        dve.wait_ge(S["lru_exp"], 4)
        for j in range(KT):
            last = v.tensor_tensor_scan(gi[0][:, j], rr[0][:, j], th[0][:, j], 0.0, ALU.mult, ALU.add)
        after(last)
        dve.wait_ge(S["lru_exp"], 5)
        back = slice(None, None, -1)
        for i in range(KT + 2):
            before = count["dve_step"]
            if i < KT:
                signal(v.tensor_tensor_scan(gi[1][:, i, back], rr[1][:, i, back], th[1][:, i, back], 0.0, ALU.mult, ALU.add),
                       "dve_step")
            dve.wait_ge(S["dve_step"], before)
            if 1 <= i <= KT:
                signal(v.tensor_tensor(rr[0][:, i - 1], gi[0][:, i - 1], gi[1][:, i - 1], ALU.add), "dve_step")
            if i >= 2:
                signal(v.tensor_tensor(rr[0][:, i - 2], rr[0][:, i - 2], yg[:, i - 2], ALU.mult), "lru_mul")
        add_output("out_b")
        moe(1)
        ple(1)
        roots()
        for k in range(KT):
            last = v.scalar_tensor_tensor(yT[:, k], hT[:, k], par("norm_final", k, 1), rstd, ALU.mult, ALU.mult)
        signal(last, "fin_ready")

    ctx_block.__exit__(None, None, None)


def tiles(w):
    k, n = w.shape
    return np.ascontiguousarray(w.reshape(k // P, P, n).transpose(1, 0, 2))


def columns(v):
    v = v.reshape(-1, P)
    return np.ascontiguousarray(v.T)


def constants():
    i = np.arange(P)
    sel = np.zeros((P, P), np.float32)
    for j in range(4):
        sel[32 * j, 0] = sel[32 * j + 1, 1] = 1.0
    parts = {
        "ident": np.eye(P), "upper": np.triu(np.ones((P, P))), "lower": np.tril(np.ones((P, P))),
        "strict": np.triu(np.ones((P, P)), 1), "ones": np.ones((P, P)), "sel": sel,
        "iota": np.broadcast_to(np.arange(SLOTS), (P, SLOTS)), "eps": np.full((P, 1), EPS),
    }
    consts = np.concatenate([parts[n].reshape(P, -1) for n in CONSTS], 1).astype(np.float32)
    neg = np.stack([np.where(i[None, :] >= i[:, None], 0.0, NEG), np.where(i[None, :] <= i[:, None], 0.0, NEG)], 1)
    level = []
    for l in range(LEVELS):
        size = 1 << l
        b = i // size
        level.append((b[:, None] // 2 == b[None, :] // 2) & (b[:, None] != b[None, :]))
    masks = np.concatenate([neg.reshape(P, -1), np.stack(level, 1).reshape(P, -1)], 1).astype(np.float32)
    c = 2 * np.pi * np.outer(i, i) / P
    l = 2 * np.pi * np.outer(np.arange(SEQ), np.arange(SEQ)) / SEQ
    norm = 1.0 / math.sqrt(P * SEQ)
    dft = {"cos_c": np.cos(c), "nsin_c": -np.sin(c), "cos_l": tiles(np.cos(l) * norm), "sin_l": tiles(np.sin(l) * norm)}
    return consts, masks, {k: v.reshape(P, -1).astype(np.float32) for k, v in dft.items()}


_ORDER = ["x", "ctx", "p", "params", "consts", "masks", "dense", "w_gate", "w_up", "w_down"]


def kernel(**inputs):
    import concourse.bacc as bacc
    from concourse.bass_utils import run_bass_kernel_spmd

    a = {k: np.asarray(v) for k, v in inputs.items()}
    consts, masks, dft = constants()
    each = lambda v: np.broadcast_to(v.reshape(1, -1), (P, v.size))
    w_in, conv = a["w_in"][0], a["w_qkv_conv"][0]
    both = np.stack([a["c"][0], a["c_ctx"]], 1)
    parts = {
        "c": tiles(both), "b_ada": columns(a["b_ada"]), "g_pre_mix": columns(a["g_pre_mix"]),
        "g_post_mix": columns(a["g_post_mix"]), "g_pre_ffn": columns(a["g_pre_ffn"]),
        "g_post_ffn": columns(a["g_post_ffn"]), "w_ab": tiles(w_in[:, 2560:]),
        "conv": conv.reshape(3, 12, P).transpose(2, 1, 0), "a_log": each(a["a_log"]), "dt_bias": each(a["dt_bias"]),
        "g_gdn": columns(a["g_gdn"]), "w_dwc": a["w_dwc"].reshape(9, FT, P).transpose(2, 1, 0),
        "norm_mix": columns(a["norm_mix_2"]), "conv_a": a["conv_a_2"].reshape(3, KT, P).transpose(2, 1, 0),
        "conv_b": a["conv_b_2"].reshape(4, KT, P).transpose(2, 1, 0), "conv_bias": columns(a["conv_bias_b_2"]),
        "b_rg": columns(a["b_rgate_b_2"]), "b_ig": columns(a["b_igate_b_2"]), "lam": columns(a["lam_b_2"]),
        "norm_ffn": columns(a["norm_ffn_2"]), "norm_ple": columns(a["norm_ple_2"]), "b_ple": columns(a["b_ple_gate_2"]),
        "norm_final": columns(a["norm_final_2"]),
        "w_router": np.stack([tiles(np.concatenate([a["w_router_group_2"][l], a["w_router_expert_2"][l]], 1))
                              for l in range(2)], 1),
        "b_router": each(np.concatenate([a["b_router_group_2"], a["b_router_expert_2"]], 1)),
    }
    params = np.concatenate([parts[n].reshape(P, -1) for n in PARAMS], 1)
    assert params.shape == (P, PARAMS_N) and consts.shape == (P, CONSTS_N) and masks.shape == (P, MASKS_N)
    dft["w_f"] = a["w_fourier"][0].transpose(1, 0, 2).reshape(P, -1)

    def chunks(w, width=512):
        return [tiles(w[:, n:n + width]).reshape(P, -1) for n in range(0, w.shape[1], width)]

    def tile_order(w, order):
        return np.concatenate([w[:, P * i:P * i + P] for i in order], 1)

    up_order = [i for f in range(FT) for i in (f, FT + f)]
    a_order = [i for j in range(0, KT, 2) for i in (KT + j, 2 * KT + j, KT + j + 1, 2 * KT + j + 1, j, j + 1)]
    gate_w = [a[n][0].reshape(8, 2, P, 256).transpose(2, 0, 1, 3).reshape(P, -1) for n in ("w_rgate_b_2", "w_igate_b_2")]
    ada = chunks(a["w_ada"][0])
    dense = ada[:4]
    dense += [c for n in (1024, 1536, 512, 2048, 0) for c in chunks(w_in[:, n:n + 512])]
    dense += [np.concatenate([dft[n] for n in FOURIER], 1)] + ada[4:]
    dense += chunks(a["w_out"][0]) + chunks(tile_order(a["w_up"][0], up_order)) + chunks(a["w_down"][0], P)
    dense += chunks(tile_order(a["w_in_a_2"][0], a_order)) + chunks(a["w_out_a_2"][0])
    dense += chunks(a["w_ple_gate_2"][0]) + chunks(a["w_ple_2"][0], D)
    dense += chunks(a["w_in_b_2"][0][:, D:]) + chunks(a["w_in_b_2"][0][:, :D]) + gate_w + chunks(a["w_out_b_2"][0])
    dense += chunks(a["w_ple_gate_2"][1]) + chunks(a["w_ple_2"][1], D)
    stream = np.zeros((len(dense), P, CHUNK), np.float32)
    for i, c in enumerate(dense):
        stream[i, :, :c.shape[1]] = c

    arrays = {
        "x": tiles(a["x"][0].T), "ctx": tiles(a["ctx"][0].T),
        "p": np.ascontiguousarray(np.stack([tiles(a["p_2"][l, 0].T) for l in range(2)], 1)),
        "params": np.ascontiguousarray(params), "consts": consts, "masks": masks, "dense": stream,
        "w_gate": a["w_exp_gate_2"], "w_up": a["w_exp_up_2"], "w_down": a["w_exp_down_2"],
    }
    nc = bacc.Bacc("TRN2", target_bir_lowering=False, num_devices=1)
    t = {n: nc.dram_tensor(f"in_{n}", list(arrays[n].shape), F32, kind="ExternalInput").ap() for n in _ORDER}
    t["out"] = nc.dram_tensor("out", [P, KT, SEQ], F32, kind="ExternalOutput").ap()
    build(nc, t)
    r = run_bass_kernel_spmd(nc, [{f"in_{n}": arrays[n] for n in _ORDER}], core_ids=[0])
    out = np.asarray(r.results[0]["out"])
    return np.ascontiguousarray(out.transpose(1, 0, 2).reshape(D, SEQ).T)[None]
```
